# Optimizing a Trainium2 kernel written in Bass

```python
import math
import jax, jax.numpy as jnp
from jax import lax
import numpy as np

D_MODEL = 1024
BATCH = 1
SEQ = 512
DEPTH = 2

GRID_W = 64
CTX_LEN = 256
EPS = 1e-6
ROPE_BASE = 10000.0
QBLK = 128

GQA_HEADS = 4
GQA_KV_HEADS = 2
GQA_GROUP = GQA_HEADS // GQA_KV_HEADS
GQA_DIM = 64
NA_HEADS = 4
NA_DIM = 64
NA_WIN_ROWS = 8
NA_WIN_COLS = 16
DIFF_HEADS = 4
DIFF_QK_DIM = 32
DIFF_V_DIM = 64
MLA_HEADS = 4
MLA_NOPE = 64
MLA_ROPE = 32
MLA_V = 64
MLA_Q_LORA = 192
MLA_KV_LORA = 128

MIX_WIDTH = GQA_HEADS * GQA_DIM + NA_HEADS * NA_DIM + DIFF_HEADS * DIFF_V_DIM + MLA_HEADS * MLA_V
IN_SPLITS = (
    GQA_HEADS * GQA_DIM, GQA_KV_HEADS * GQA_DIM, GQA_KV_HEADS * GQA_DIM,
    NA_HEADS * NA_DIM, NA_HEADS * NA_DIM, NA_HEADS * NA_DIM,
    DIFF_HEADS * 2 * DIFF_QK_DIM, DIFF_HEADS * 2 * DIFF_QK_DIM, DIFF_HEADS * DIFF_V_DIM,
    MLA_Q_LORA, MLA_KV_LORA, MLA_ROPE,
)
IN_COLS = sum(IN_SPLITS)

N_EXPERTS = 16
MOE_GROUPS = 4
EXPERTS_PER_GROUP = N_EXPERTS // MOE_GROUPS
MOE_TOPK_GROUPS = 1
MOE_TOPK = 2
D_EXPERT = 256
D_SHARED = 256

kernel_name = 'hymba_style_hybrid_dit_block'

def rms_norm(x, g):
    xf = x.astype(jnp.float32)
    y = xf * lax.rsqrt(jnp.mean(xf * xf, axis=-1, keepdims=True) + EPS)
    return (y * g.astype(jnp.float32)).astype(x.dtype)

def modulate(h, shift, scale):
    return h * (1 + scale) + shift

def axial_angles(n_tok, rot_dim):
    half = rot_dim // 2
    freqs = ROPE_BASE ** (-jnp.arange(0, half, 2, dtype=jnp.float32) / half)
    t = jnp.arange(n_tok, dtype=jnp.int32)
    row = (t // GRID_W).astype(jnp.float32)
    col = (t % GRID_W).astype(jnp.float32)
    return row[:, None] * freqs, col[:, None] * freqs

def rope_1d(x, ang):
    shape = (1, ang.shape[0]) + (1,) * (x.ndim - 3) + (ang.shape[1],)
    cos = jnp.cos(ang).reshape(shape).astype(x.dtype)
    sin = jnp.sin(ang).reshape(shape).astype(x.dtype)
    x1, x2 = jnp.split(x, 2, axis=-1)
    return jnp.concatenate([x1 * cos - x2 * sin, x1 * sin + x2 * cos], axis=-1)

def rope_2d(x, ang):
    ang_r, ang_c = ang
    m = x.shape[-1] // 2
    return jnp.concatenate([rope_1d(x[..., :m], ang_r), rope_1d(x[..., m:], ang_c)], axis=-1)

def split_cols(u):
    offsets = [int(o) for o in np.cumsum(IN_SPLITS)[:-1]]
    return jnp.split(u, offsets, axis=-1)

def attend(q, kvs, scale):
    s = jnp.concatenate([jnp.einsum('bqhgd,bkhd->bhgqk', q, k) for k, _ in kvs], axis=-1)
    p = jax.nn.softmax(s.astype(jnp.float32) * scale, axis=-1)
    out = 0
    start = 0
    for k, v in kvs:
        n = k.shape[1]
        out = out + jnp.einsum('bhgqk,bkhd->bqhgd', p[..., start:start + n].astype(v.dtype), v)
        start += n
    return out

def blocked_attend(q, kvs, scale):
    b, s = q.shape[:2]
    nb = s // QBLK
    qb = jnp.moveaxis(q.reshape((b, nb, QBLK) + q.shape[2:]), 1, 0)
    ob = lax.map(lambda qi: attend(qi, kvs, scale), qb)
    return jnp.moveaxis(ob, 0, 1).reshape((b, s) + ob.shape[3:])

def gqa_mixer(q, k, v, qc, kc, vc, q_gain, k_gain, ang, want_ctx):
    scale = GQA_DIM ** -0.5
    def heads(qx, kx, vx, rotate):
        b, n = qx.shape[:2]
        qx = rms_norm(qx.reshape(b, n, GQA_KV_HEADS, GQA_GROUP, GQA_DIM), q_gain)
        kx = rms_norm(kx.reshape(b, n, GQA_KV_HEADS, GQA_DIM), k_gain)
        vx = vx.reshape(b, n, GQA_KV_HEADS, GQA_DIM)
        if rotate:
            qx = rope_2d(qx, ang)
            kx = rope_2d(kx, ang)
        return qx, kx, vx
    ql, kl, vl = heads(q, k, v, True)
    qcx, kcx, vcx = heads(qc, kc, vc, False)
    b, s = q.shape[:2]
    out_lat = blocked_attend(ql, ((kl, vl), (kcx, vcx)), scale).reshape(b, s, GQA_HEADS * GQA_DIM)
    out_ctx = None
    if want_ctx:
        out_ctx = attend(qcx, ((kcx, vcx),), scale).reshape(b, qc.shape[1], GQA_HEADS * GQA_DIM)
    return out_lat, out_ctx

def na_mixer(q, k, v, qc, kc, vc, rel_bias, want_ctx):
    scale = NA_DIM ** -0.5
    b, s = q.shape[:2]
    L = qc.shape[1]
    rows = s // GRID_W
    kh = min(NA_WIN_ROWS, rows)
    kw = NA_WIN_COLS
    n_nb = kh * kw
    qg = q.reshape(b, rows, GRID_W, NA_HEADS, NA_DIM)
    kg = k.reshape(b, rows, GRID_W, NA_HEADS, NA_DIM)
    vg = v.reshape(b, rows, GRID_W, NA_HEADS, NA_DIM)
    qcx = qc.reshape(b, L, NA_HEADS, NA_DIM)
    kcx = kc.reshape(b, L, NA_HEADS, NA_DIM)
    vcx = vc.reshape(b, L, NA_HEADS, NA_DIM)
    cols = jnp.arange(GRID_W)
    col_idx = jnp.clip(cols - kw // 2, 0, GRID_W - kw)[:, None] + jnp.arange(kw)[None, :]
    dc = col_idx - cols[:, None]

    def row_block(r):
        r0 = jnp.clip(r - kh // 2, 0, rows - kh)
        k_rows = lax.dynamic_slice_in_dim(kg, r0, kh, axis=1)
        v_rows = lax.dynamic_slice_in_dim(vg, r0, kh, axis=1)
        k_nb = jnp.moveaxis(k_rows[:, :, col_idx], 1, 2).reshape(b, GRID_W, n_nb, NA_HEADS, NA_DIM)
        v_nb = jnp.moveaxis(v_rows[:, :, col_idx], 1, 2).reshape(b, GRID_W, n_nb, NA_HEADS, NA_DIM)
        q_row = lax.dynamic_index_in_dim(qg, r, axis=1, keepdims=False)
        dr = r0 + jnp.arange(kh) - r
        bias = rel_bias[:, dr[:, None, None] + (NA_WIN_ROWS - 1), dc[None] + (NA_WIN_COLS - 1)]
        bias = jnp.moveaxis(bias, 1, 2).reshape(NA_HEADS, GRID_W, n_nb)
        s_nb = jnp.einsum('bqhd,bqkhd->bhqk', q_row, k_nb).astype(jnp.float32) * scale + bias.astype(jnp.float32)
        s_c = jnp.einsum('bqhd,bkhd->bhqk', q_row, kcx).astype(jnp.float32) * scale
        p = jax.nn.softmax(jnp.concatenate([s_nb, s_c], axis=-1), axis=-1)
        return (jnp.einsum('bhqk,bqkhd->bqhd', p[..., :n_nb].astype(v.dtype), v_nb)
                + jnp.einsum('bhqk,bkhd->bqhd', p[..., n_nb:].astype(v.dtype), vcx))

    o = lax.map(row_block, jnp.arange(rows))
    out_lat = jnp.moveaxis(o, 0, 1).reshape(b, s, NA_HEADS * NA_DIM)
    out_ctx = None
    if want_ctx:
        out_ctx = attend(qcx[:, :, :, None], ((kcx, vcx),), scale).reshape(b, L, NA_HEADS * NA_DIM)
    return out_lat, out_ctx

def diff_mixer(q, k, v, qc, kc, vc, lq1, lk1, lq2, lk2, subln, lam_init, ang, want_ctx):
    scale = DIFF_QK_DIM ** -0.5
    lam = (jnp.exp(jnp.sum(lq1.astype(jnp.float32) * lk1.astype(jnp.float32)))
           - jnp.exp(jnp.sum(lq2.astype(jnp.float32) * lk2.astype(jnp.float32))) + lam_init).astype(q.dtype)
    def heads(qx, kx, vx, rotate):
        b, n = qx.shape[:2]
        qx = qx.reshape(b, n, DIFF_HEADS * 2, DIFF_QK_DIM)
        kx = kx.reshape(b, n, DIFF_HEADS * 2, DIFF_QK_DIM)
        if rotate:
            qx = rope_2d(qx, ang)
            kx = rope_2d(kx, ang)
        return (qx.reshape(b, n, DIFF_HEADS, 2, DIFF_QK_DIM), kx.reshape(b, n, DIFF_HEADS, 2, DIFF_QK_DIM),
                vx.reshape(b, n, DIFF_HEADS, DIFF_V_DIM))
    def combine(o1, o2):
        o = rms_norm(o1 - lam * o2, subln) * (1.0 - lam_init)
        return o.reshape(o.shape[0], o.shape[1], DIFF_HEADS * DIFF_V_DIM)
    ql, kl, vl = heads(q, k, v, True)
    qcx, kcx, vcx = heads(qc, kc, vc, False)
    o1 = blocked_attend(ql[:, :, :, 0:1], ((kl[:, :, :, 0], vl), (kcx[:, :, :, 0], vcx)), scale)
    o2 = blocked_attend(ql[:, :, :, 1:2], ((kl[:, :, :, 1], vl), (kcx[:, :, :, 1], vcx)), scale)
    out_lat = combine(o1, o2)
    out_ctx = None
    if want_ctx:
        c1 = attend(qcx[:, :, :, 0:1], ((kcx[:, :, :, 0], vcx),), scale)
        c2 = attend(qcx[:, :, :, 1:2], ((kcx[:, :, :, 1], vcx),), scale)
        out_ctx = combine(c1, c2)
    return out_lat, out_ctx

def mla_mixer(cq, ckv, kpe, cqc, ckvc, kpec, q_norm, w_q_up, kv_norm, w_kv_up, ang, want_ctx):
    scale = (MLA_NOPE + MLA_ROPE) ** -0.5
    def heads(cqx, ckvx, kpex, rotate):
        b, n = cqx.shape[:2]
        qx = (rms_norm(cqx, q_norm) @ w_q_up).reshape(b, n, MLA_HEADS, MLA_NOPE + MLA_ROPE)
        kvx = (rms_norm(ckvx, kv_norm) @ w_kv_up).reshape(b, n, MLA_HEADS, MLA_NOPE + MLA_V)
        q_nope, q_pe = qx[..., :MLA_NOPE], qx[..., MLA_NOPE:]
        k_nope, vx = kvx[..., :MLA_NOPE], kvx[..., MLA_NOPE:]
        k_pe = kpex[:, :, None, :]
        if rotate:
            q_pe = rope_2d(q_pe, ang)
            k_pe = rope_2d(k_pe, ang)
        qx = jnp.concatenate([q_nope, q_pe], axis=-1)
        kx = jnp.concatenate([k_nope, jnp.broadcast_to(k_pe, k_nope.shape[:-1] + (MLA_ROPE,))], axis=-1)
        return qx[:, :, :, None], kx, vx
    ql, kl, vl = heads(cq, ckv, kpe, True)
    qcx, kcx, vcx = heads(cqc, ckvc, kpec, False)
    b, s = cq.shape[:2]
    out_lat = blocked_attend(ql, ((kl, vl), (kcx, vcx)), scale).reshape(b, s, MLA_HEADS * MLA_V)
    out_ctx = None
    if want_ctx:
        out_ctx = attend(qcx, ((kcx, vcx),), scale).reshape(b, cqc.shape[1], MLA_HEADS * MLA_V)
    return out_lat, out_ctx

def swiglu(x, wg, wu, wd):
    return (jax.nn.silu(x @ wg) * (x @ wu)) @ wd

def moe_ffn(h, router_w, router_b, w_gate, w_up, w_down, ws_gate, ws_up, ws_down):
    shp = h.shape
    xs = h.reshape(-1, shp[-1])
    scores = jax.nn.sigmoid((xs @ router_w).astype(jnp.float32))
    sel = scores + router_b.astype(jnp.float32)
    grp = sel.reshape(-1, MOE_GROUPS, EXPERTS_PER_GROUP)
    grp_score = lax.top_k(grp, 2)[0].sum(-1)
    _, g_idx = lax.top_k(grp_score, MOE_TOPK_GROUPS)
    g_mask = (g_idx[..., None] == jnp.arange(MOE_GROUPS)).any(axis=1)
    e_mask = jnp.repeat(g_mask, EXPERTS_PER_GROUP, axis=1)
    _, e_idx = lax.top_k(jnp.where(e_mask, sel, -jnp.inf), MOE_TOPK)
    w = jnp.take_along_axis(scores, e_idx, axis=-1)
    w = w / jnp.sum(w, axis=-1, keepdims=True)
    gates = jnp.sum(jax.nn.one_hot(e_idx, N_EXPERTS, dtype=jnp.float32) * w[..., None], axis=1).astype(xs.dtype)
    out = swiglu(xs, ws_gate, ws_up, ws_down)
    for e in range(N_EXPERTS):
        out = out + gates[:, e:e + 1] * swiglu(xs, w_gate[e], w_up[e], w_down[e])
    return out.reshape(shp)

def setup_inputs(seed: int = 0) -> dict:
    key = jax.random.key(seed)
    ks = list(jax.random.split(key, 31))
    def nrm(shape, scale):
        return jax.random.normal(ks.pop(), shape, jnp.float32) * scale
    def gain(shape):
        return 1.0 + nrm(shape, 0.1)
    D = D_MODEL
    return {
        'x': nrm((BATCH, SEQ, D), 1.0),
        'c': nrm((BATCH, D), 1.0),
        'ctx': nrm((BATCH, CTX_LEN, D), 1.0),
        'c_ctx': nrm((D,), 1.0),
        'w_mod': nrm((DEPTH, D, 6 * D), 0.5 * D ** -0.5),
        'b_mod': nrm((DEPTH, 6 * D), 0.01),
        'norm_mix': gain((DEPTH, D)),
        'norm_ffn': gain((DEPTH, D)),
        'w_in': nrm((DEPTH, D, IN_COLS), D ** -0.5),
        'w_out': nrm((DEPTH, MIX_WIDTH, D), MIX_WIDTH ** -0.5),
        'gqa_q_norm': gain((DEPTH, GQA_DIM)),
        'gqa_k_norm': gain((DEPTH, GQA_DIM)),
        'na_rel_bias': nrm((DEPTH, NA_HEADS, 2 * NA_WIN_ROWS - 1, 2 * NA_WIN_COLS - 1), 0.1),
        'diff_lq1': nrm((DEPTH, DIFF_QK_DIM), 0.1),
        'diff_lk1': nrm((DEPTH, DIFF_QK_DIM), 0.1),
        'diff_lq2': nrm((DEPTH, DIFF_QK_DIM), 0.1),
        'diff_lk2': nrm((DEPTH, DIFF_QK_DIM), 0.1),
        'diff_subln': gain((DEPTH, DIFF_V_DIM)),
        'mla_q_norm': gain((DEPTH, MLA_Q_LORA)),
        'mla_w_q_up': nrm((DEPTH, MLA_Q_LORA, MLA_HEADS * (MLA_NOPE + MLA_ROPE)), MLA_Q_LORA ** -0.5),
        'mla_kv_norm': gain((DEPTH, MLA_KV_LORA)),
        'mla_w_kv_up': nrm((DEPTH, MLA_KV_LORA, MLA_HEADS * (MLA_NOPE + MLA_V)), MLA_KV_LORA ** -0.5),
        'router_w': nrm((D, N_EXPERTS), D ** -0.5),
        'router_b': nrm((N_EXPERTS,), 0.01),
        'moe_w_gate': nrm((DEPTH, N_EXPERTS, D, D_EXPERT), D ** -0.5),
        'moe_w_up': nrm((DEPTH, N_EXPERTS, D, D_EXPERT), D ** -0.5),
        'moe_w_down': nrm((DEPTH, N_EXPERTS, D_EXPERT, D), D_EXPERT ** -0.5),
        'shared_w_gate': nrm((DEPTH, D, D_SHARED), D ** -0.5),
        'shared_w_up': nrm((DEPTH, D, D_SHARED), D ** -0.5),
        'shared_w_down': nrm((DEPTH, D_SHARED, D), D_SHARED ** -0.5),
        'final_norm': gain((D,)),
    }

def reference(x, c, ctx, c_ctx, w_mod, b_mod, norm_mix, norm_ffn, w_in, w_out,
              gqa_q_norm, gqa_k_norm, na_rel_bias, diff_lq1, diff_lk1, diff_lq2, diff_lk2, diff_subln,
              mla_q_norm, mla_w_q_up, mla_kv_norm, mla_w_kv_up, router_w, router_b,
              moe_w_gate, moe_w_up, moe_w_down, shared_w_gate, shared_w_up, shared_w_down, final_norm):
    s = x.shape[1]
    ang_gqa = axial_angles(s, GQA_DIM)
    ang_diff = axial_angles(s, DIFF_QK_DIM)
    ang_mla = axial_angles(s, MLA_ROPE)
    xc = ctx
    for l in range(DEPTH):
        want_ctx = l < DEPTH - 1
        lam_init = 0.8 - 0.6 * math.exp(-0.3 * l)
        mod = jax.nn.silu(c) @ w_mod[l] + b_mod[l]
        mod_c = jax.nn.silu(c_ctx) @ w_mod[l] + b_mod[l]
        sh1, sc1, g1, sh2, sc2, g2 = jnp.split(mod[:, None, :], 6, axis=-1)
        sh1c, sc1c, g1c, sh2c, sc2c, g2c = jnp.split(mod_c, 6, axis=-1)

        h = modulate(rms_norm(x, norm_mix[l]), sh1, sc1)
        hc = modulate(rms_norm(xc, norm_mix[l]), sh1c, sc1c)
        u = split_cols(h @ w_in[l])
        uc = split_cols(hc @ w_in[l])
        a_lat, a_ctx = gqa_mixer(u[0], u[1], u[2], uc[0], uc[1], uc[2], gqa_q_norm[l], gqa_k_norm[l], ang_gqa, want_ctx)
        b_lat, b_ctx = na_mixer(u[3], u[4], u[5], uc[3], uc[4], uc[5], na_rel_bias[l], want_ctx)
        c_lat, c_ctx_out = diff_mixer(u[6], u[7], u[8], uc[6], uc[7], uc[8], diff_lq1[l], diff_lk1[l],
                                      diff_lq2[l], diff_lk2[l], diff_subln[l], lam_init, ang_diff, want_ctx)
        d_lat, d_ctx = mla_mixer(u[9], u[10], u[11], uc[9], uc[10], uc[11], mla_q_norm[l], mla_w_q_up[l],
                                 mla_kv_norm[l], mla_w_kv_up[l], ang_mla, want_ctx)
        x = x + g1 * (jnp.concatenate([a_lat, b_lat, c_lat, d_lat], axis=-1) @ w_out[l])

        h2 = modulate(rms_norm(x, norm_ffn[l]), sh2, sc2)
        x = x + g2 * moe_ffn(h2, router_w, router_b, moe_w_gate[l], moe_w_up[l], moe_w_down[l],
                             shared_w_gate[l], shared_w_up[l], shared_w_down[l])

        if want_ctx:
            xc = xc + g1c * (jnp.concatenate([a_ctx, b_ctx, c_ctx_out, d_ctx], axis=-1) @ w_out[l])
            h2c = modulate(rms_norm(xc, norm_ffn[l]), sh2c, sc2c)
            xc = xc + g2c * moe_ffn(h2c, router_w, router_b, moe_w_gate[l], moe_w_up[l], moe_w_down[l],
                                    shared_w_gate[l], shared_w_up[l], shared_w_down[l])
    return rms_norm(x, final_norm)


_drawn_inputs = setup_inputs


def setup_inputs(seed=0):
    import zlib

    import numpy as np

    out = dict(_drawn_inputs(seed))
    spreads = {}
    factors = {'gqa_q_norm': 8.0,
     'gqa_k_norm': 8.0,
     'na_rel_bias': 8.0,
     'diff_lk1': 2.763,
     'diff_lq2': 7.818,
     'diff_lk2': 5.325,
     'mla_q_norm': 8.0,
     'mla_kv_norm': 4.995}
    for name, (base, spread) in spreads.items():
        noise = np.random.default_rng([zlib.crc32(name.encode()), seed]).standard_normal(out[name].shape)
        drawn = base * np.exp(spread * noise) if base else spread * noise
        out[name] = __import__('jax').numpy.asarray(drawn.astype(out[name].dtype))
    for name, factor in factors.items():
        out[name] = (out[name] * factor).astype(out[name].dtype)
    return out
```

```python
import math
from contextlib import ExitStack

import numpy as np
import concourse.bass as bass
from concourse import mybir

ALU = mybir.AluOpType
ACT = mybir.ActivationFunctionType
AX = mybir.AxisListType
F32 = mybir.dt.float32
BF16 = mybir.dt.bfloat16
I32 = mybir.dt.int32
U32 = mybir.dt.uint32

P = 128
D = 1024
DEPTH = 2
SEQ = 512
CTX = 256
NTOK = SEQ + CTX
T = NTOK // P
TL = SEQ // P
TC = CTX // P
KT = D // P
GRID_W = 64
GRID_H = SEQ // GRID_W
EPS = 1e-6
IN_COLS = 2400
UCH = 480
NCH = IN_COLS // UCH
MCH = 512
NMCH = 6 * D // MCH
NE = 16
NG = 4
DE = 256
BIG = 1e30
TOPK = 2
NBK = [-(-((TOPK * n + NE * (P - 1)) // P) // 2) * 2 for n in (NTOK, SEQ)]
HEADS = 20

AQ, AK, AV, NQ, NK_, NV, DQ, DK, DV, CQ, CKV, KPE = (
    0, 256, 384, 512, 768, 1024, 1280, 1536, 1792, 2048, 2240, 2368)
ST_AK, ST_DK, ST_AQ, ST_DQ, ST_MK, ST_MQ, ST_W = 0, 128, 384, 640, 896, 1280, 1664
SL_NK, SL_NQ, SL_AK, SL_DK, SL_AQ, SL_DQ, SL_MK, SL_MQ, NSL = 0, 2, 4, 5, 7, 9, 11, 15, 19
V_A, V_N, V_D, V_M, V_W = 0, 128, 384, 640, 896
ROUNDS = 8


def constants():
    parts, at = [], {}
    width = 0

    def add(name, a):
        nonlocal width
        a = np.asarray(a, np.float32).reshape(P, -1)
        at[name] = (width, width + a.shape[1])
        parts.append(a)
        width += a.shape[1]

    p = np.arange(P)
    add("ident", np.eye(P))
    add("ones", np.ones((P, P)))
    add("before", p[:, None] < p[None, :])
    for rot, heads in ((64, "64"), (32, "32")):
        half = rot // 2
        freqs = (np.float32(10000.0) ** (-np.arange(0, half, 2, dtype=np.float32) / np.float32(half))).astype(np.float32)
        cos = np.ones((NTOK, rot), np.float32)
        sin = np.zeros((NTOK, rot), np.float32)
        tok = np.arange(SEQ)
        for a, place in enumerate((tok // GRID_W, tok % GRID_W)):
            ang = place.astype(np.float32)[:, None] * freqs
            n = freqs.size
            o = a * half
            cos[:SEQ, o:o + n] = cos[:SEQ, o + n:o + 2 * n] = np.cos(ang)
            sin[:SEQ, o:o + n] = -np.sin(ang)
            sin[:SEQ, o + n:o + 2 * n] = np.sin(ang)
        add("cos" + heads, cos.reshape(T, P, rot).transpose(1, 0, 2))
        add("sin" + heads, sin.reshape(T, P, rot).transpose(1, 0, 2))
    col = p % GRID_W
    lo = np.clip(col - 8, 0, GRID_W - 16)[:, None]
    keys = np.arange(GRID_W)[None, :]
    add("window", np.where((keys >= lo) & (keys < lo + 16), 0.0, -BIG))
    add("pick", (p[:, None] % 32) == np.arange(2)[None, :])
    add("expert", np.broadcast_to(np.arange(NE), (P, NE)))
    add("group_of", np.broadcast_to(np.arange(NE) // (NE // NG), (P, NE)))
    add("block", np.broadcast_to(np.arange(NBK[0] + 1), (P, NBK[0] + 1)))
    add("tile_start", np.broadcast_to(P * np.arange(T), (P, T)))
    add("token", np.arange(T)[None, :] * P + p[:, None])
    return np.concatenate(parts, 1), at


def span(start, size):
    return slice(start, start + size) if isinstance(start, int) else bass.ds(start, size)


class Count:

    def __init__(self, eng, sem, start):
        self.eng, self.sem, self.start, self.n = eng, sem, start, 0

    def done(self, ins):
        ins.then_inc(self.sem, 1)
        self.n += 1
        return self

    def sync(self):
        self.eng.wait_ge(self.sem, self.start + self.n)


def program(nc, A, out, stop=None):
    table, at = constants()
    cst_d = nc.inline_tensor(table, name="shape_constants").ap()
    dram = lambda n, s, d=F32: nc.dram_tensor(n, s, d, kind="Internal").ap()
    x_in = [dram(f"x_in{l}", (NTOK, D)) for l in range(DEPTH)]
    x_mix = [dram(f"x_mix{l}", ((NTOK, SEQ)[l], D)) for l in range(DEPTH)]
    h2_d = [dram(f"h2_{l}", ((NTOK, SEQ)[l], D)) for l in range(DEPTH)]
    x_ffn = [dram(f"x_ffn{l}", ((NTOK, SEQ)[l], D)) for l in range(DEPTH)]
    y_d = [dram(f"y{l}", (NBK[l] * P, D)) for l in range(DEPTH)]
    slot_tok = [dram(f"slot_tok{l}", ((NBK[l] + 1) * P, 1), U32) for l in range(DEPTH)]
    REL_ROW = DEPTH * P
    REL_COPY = (4 * 15 + 2) * REL_ROW
    rel_d = dram("rel_padded", (1, REL_COPY))
    rel_copies = dram("rel_copies", (GRID_W, REL_COPY))
    mod_d = [dram(f"mod{l}", (2, 6 * D)) for l in range(DEPTH)]

    with ExitStack() as ctx:
        sb = lambda n, s, d=F32: ctx.enter_context(nc.sbuf_tensor(n, s, d))
        pb = lambda n, s: ctx.enter_context(nc.psum_tensor(n, s, F32))
        sem = lambda n: ctx.enter_context(nc.semaphore(n))

        cst = sb("cst", [P, table.shape[1]])
        C = lambda n: cst[:, at[n][0]:at[n][1]]
        ident, ones = C("ident"), C("ones")
        cos = {64: C("cos64").rearrange("p (t c) -> p t c", t=T), 32: C("cos32").rearrange("p (t c) -> p t c", t=T)}
        sin = {64: C("sin64").rearrange("p (t c) -> p t c", t=T), 32: C("sin32").rearrange("p (t c) -> p t c", t=T)}
        csrc = sb("csrc", [P, 2, KT])
        ctmp = sb("ctmp", [P, 2, KT])
        cs = sb("cs", [P, KT, 32])
        modcol = sb("modcol", [P, T, 2, KT])
        gains = sb("gains", [P, 6, 64])
        lgain = sb("lgain", [P, 320])
        sumsq = sb("sumsq", [P, 2])
        meansq = sb("meansq", [P, 2])
        rstd = sb("rstd", [P, 2])
        s8 = sb("s8", [P, 8])
        m8 = sb("m8", [P, 8])
        r8 = sb("r8", [P, 8])
        halfs = sb("halfs", [P, 24])
        inv8, eps8 = halfs[:, 8:16], halfs[:, 16:24]
        nmax = sb("nmax", [P, HEADS])
        rsum = sb("rsum", [P, HEADS])
        rinv = sb("rinv", [P, HEADS])
        nlam = sb("nlam", [P, 4])
        dtmp = sb("dtmp", [P, 128])
        dstat = sb("dstat", [P, 8])
        subg = sb("subg", [P, 64])
        h2s = sb("h2s", [P, 4])

        ARENA = 49928
        arena = sb("arena", [P, ARENA])

        def region(start):
            at_ = [start]

            def take(*shape, parts=P, dt=None):
                n = int(np.prod(shape))
                a = arena[0:parts, at_[0]:at_[0] + n]
                at_[0] += n
                assert at_[0] <= ARENA, (shape, at_[0])
                if len(shape) == 2:
                    a = a.rearrange("p (a b) -> p a b", a=shape[0])
                return a
            take.at = at_
            return take

        take = region(0)
        win = take(KT, IN_COLS)
        WIN_END = take.at[0]
        qk = take(NSL, NTOK)
        vals = take(T, V_W)
        QKV_END = take.at[0]
        U = take(IN_COLS)
        st = take(ST_W)
        xt = take(D)
        junk = take(D // 2).bitcast(BF16)
        hT = [take(KT, P) for _ in range(2)]
        tmpA, tmpB = take(512), take(512)
        lor = take(320)
        lorT = take(3, P)
        wqu = take(2, 384)
        wkvu = take(512)
        kper = take(32)
        take = region(WIN_END)
        wm = [take(KT, MCH) for _ in range(2)]
        part = [take(MCH) for _ in range(2)]
        modrow = take(6 * D, parts=2)
        brow = take(6 * D, parts=2)
        nrow = take(2, D, parts=2)

        relpad = arena[0:62, 45000:45000 + DEPTH * P]
        zeros_u = arena[:, 45400:45400 + NBK[0] + 1].bitcast(U32)
        take = region(0)
        wout = take(KT, D)
        vec = take(6, D)
        bias_t = take(4, 16 * GRID_W)
        assert take.at[0] <= WIN_END
        take = region(QKV_END)
        Qs = take(HEADS, P)
        Pb = [take(NTOK) for _ in range(2)]
        PTs = [take(T, P) for _ in range(2)]
        O = take(D)
        OT = take(KT, P)
        xa, xb, h2b = take(D), take(D), take(D)
        lamb = O[:, 0:128].rearrange("p (a b) -> p a b", a=4)
        take = region(WIN_END)
        swgu = take(KT, 512)
        swd = take(2, D)
        hs = [take(D) for _ in range(2)]
        hT2 = [take(KT, P) for _ in range(2)]
        gex = [take(DE) for _ in range(2)]
        hid = [take(DE) for _ in range(2)]
        hidT = [take(2, P) for _ in range(2)]
        x1b = [take(D) for _ in range(2)]
        ob = [take(D) for _ in range(2)]
        g2 = take(2, D)
        rw = take(KT, NE)
        rb = take(NE)
        take = region(take.at[0])
        wgu = [take(2, KT * DE) for _ in range(2)]
        wdn = [take(2, D) for _ in range(2)]
        take = region(0)
        xg = [take(D) for _ in range(2)]
        XT = [take(KT, P) for _ in range(2)]
        yb = [take(D) for _ in range(2)]
        y12 = [take(2, D) for _ in range(2)]
        x2b = [take(D) for _ in range(2)]
        x3b = [take(D) for _ in range(2)]
        fgain = take(D)
        lg = take(T, NE)
        score, selb, oh0, oh1, both, tmp16, tots, offs, posn = [take(T, NE) for _ in range(9)]
        gs8, mx8 = take(T, 8), take(T, 8)
        ix8 = take(T, 8).bitcast(U32)
        pair = take(5, T * NG)
        gidx = take(T)
        eidx = take(T, 2)
        wts = take(T, 2)
        wsum = take(T)
        slotf = take(T, 2)
        slots = take(T, 2).bitcast(U32)
        nblk, bend, bbase, count_e = take(NE), take(NE), take(NE), take(NE)
        cmp6 = take(NE, T)
        cmpb = take(NBK[0] + 1, NE)
        bexp = take(NBK[0] + 1)
        bexp_i = take(NBK[0] + 1).bitcast(I32)
        tok_u = take(T).bitcast(U32)
        table_u = take(NBK[0] + 1).bitcast(U32)
        idx1 = [take(1).bitcast(U32) for _ in range(2)]
        idx2 = [take(2).bitcast(U32) for _ in range(2)]
        assert take.at[0] <= WIN_END, take.at[0]

        S0, S1, PT = pb("S0", [P, 1024]), pb("S1", [P, 1024]), pb("PT", [P, 1024])
        B6, B7 = pb("B6", [P, 512]), pb("B7", [P, 512])
        ubank = [S0[:, 0:512], S0[:, 512:1024], S1[:, 0:512], S1[:, 512:1024], B6[:, :]]

        consts_in, inputs_copied, cond_in = sem("consts_in"), sem("inputs_copied"), sem("cond_in")
        exp_c, cs_ready = sem("exp_c"), sem("cs_ready")
        halfs_set = sem("halfs_set")
        relpad_set, relpad_in, rel_stored, zeros_stored, fgain_in = (
            sem("relpad_set"), sem("relpad_in"), sem("rel_stored"), sem("zeros_stored"), sem("fgain_in"))
        c_sum = sem("c_sum")
        UNITS = ["exp_done", "p_tr", "pt_v", "pt_s", "pv_done", "o_evac"]
        v_init = sem("v_init")
        NAMES = ["mod_w_in0", "mod_w_in1", "mod_rows_in", "mod_mm", "mod_part", "mod_sel", "mod_row", "mod_gain", "mod_stored",
                 "modcol_in", "wsmall_in", "x_in", "ssq", "rstd_ready", "xn_done", "hT_tr", "hT_evac", "u_mm", "u_evac",
                 "v_copied", "u_used", "stats", "r8_ready", "lor_ready", "st_ready", "st_m_ready", "round_tr", "round_evac",
                 "v_prep", "g_prep", "mean_x",
                 "bias_in", "lam_in", "bias_ready", "wout_in", "vec_in", "lam_sum", "lam_exp", "lam_ready", "v_lam",
                 "xa_in", "qs_ready", "scored", "neg_max", "exp_done", "p_tr", "pt_v", "pt_s", "pv_done", "o_evac", "v_bias",
                 "v_o", "d_stat", "d_rs", "g_att", "o_all", "ot_tr", "ot_v", "ot_s", "op_mm", "res_mul", "x1_ready", "x1_sq",
                 "h2_ready", "x1_stored", "h2_stored",
                 "s_w_in", "hs_in0", "hs_in1", "x1_in0", "x1_in1", "s_tr", "s_t_v", "s_t_s", "s_rt", "s_lg", "s_g", "s_u", "s_ex",
                 "v_s", "s_hid", "s_ht", "s_htv", "s_d", "s_ob", "s_x2", "s_stored0", "s_stored1",
                 "r_exp", "v_r", "r_mat", "r_cum", "r_slots", "r_scat", "r_zero", "r_tab", "r_ready",
                 "e_w_in0", "e_w_in1", "e_idx", "e_x_in0", "e_x_in1", "e_tr", "e_t_v", "e_t_s", "e_g", "e_u", "e_ex", "v_e",
                 "e_hid", "e_ht", "e_htv", "e_d", "e_y_v", "e_y_s", "e_stored0", "e_stored1",
                 "c_idx", "idx_seen", "c_y_in0", "c_y_in1", "c_x_in0", "c_x_in1", "v_c", "c_x3", "c_stored0", "c_stored1", "c_sq", "c_mean",
                 "c_rs"]
        s = {n: sem(n) for n in NAMES}
        s["win_in"] = [sem(f"win_in{c}") for c in range(NCH)]

        block = ctx.enter_context(nc.Block())

        @block.sync
        def _(sp):
            sp.dma_start(cst[:, :], cst_d).then_inc(consts_in, 16)
            sp.dma_start(csrc[:, 0, :], A["c"].rearrange("a (p k) -> (a p) k", k=KT)).then_inc(cond_in, 16)
            sp.dma_start(csrc[:, 1, :], A["c_ctx"].rearrange("(p k) -> p k", k=KT)).then_inc(cond_in, 16)
            sp.dma_start(x_in[0][0:SEQ, :], A["x"][0]).then_inc(inputs_copied, 16)
            sp.dma_start(x_in[0][SEQ:NTOK, :], A["ctx"][0]).then_inc(inputs_copied, 16)
            sp.wait_ge(relpad_set, 2)
            for l in range(DEPTH):
                sp.dma_start(relpad[1:61, l * P + 48:l * P + 79], A["na_rel_bias"][l].rearrange("h a b -> (h a) b")).then_inc(relpad_in, 16)
                sp.dma_start(slot_tok[l].rearrange("(p b) o -> p (b o)", p=P), zeros_u[:, 0:NBK[l] + 1]).then_inc(zeros_stored, 16)
            sp.wait_ge(relpad_in, 16 * DEPTH)
            sp.dma_start(rel_d.rearrange("o (a c) -> (o a) c", c=REL_ROW), relpad).then_inc(rel_stored, 16)
            for u in range(2):
                for n in UNITS:
                    sp.sem_inc(s[n], 1)
            for l in range(1 if stop in ("P", "A") else DEPTH):
                g = lambda t: t + T * l
                wmod = A["w_mod"][l].rearrange("(p k) n -> p k n", k=KT)

                def mod_load(i, first):
                    for b in range(2):
                        if not first:
                            sp.wait_ge(s["mod_mm"], 2 * i + b - 1 + NMCH * l)
                        sp.dma_start(wm[b], wmod[:, :, span((2 * i + b) * MCH, MCH)]).then_inc(s[f"mod_w_in{b}"], 16)
                for r in range(2):
                    sp.dma_start(brow[r:r + 1, :], A["b_mod"][l:l + 1, :]).then_inc(s["mod_rows_in"], 16)
                    sp.dma_start(nrow[r:r + 1, 0, :], A["norm_mix"][l:l + 1, :]).then_inc(s["mod_rows_in"], 16)
                    sp.dma_start(nrow[r:r + 1, 1, :], A["norm_ffn"][l:l + 1, :]).then_inc(s["mod_rows_in"], 16)
                mod_load(0, True)
                with sp.Fori(1, NMCH // 2) as i:
                    mod_load(i, False)
                win_d = A["w_in"][l].rearrange("(p k) n -> p k n", k=KT)
                for c in range(NCH):
                    sp.dma_start(win[:, :, c * UCH:(c + 1) * UCH], win_d[:, :, c * UCH:(c + 1) * UCH]).then_inc(s["win_in"][c], 16)
                sp.wait_ge(s["mod_gain"], 2 * (l + 1))
                sp.dma_start(mod_d[l], modrow).then_inc(s["mod_stored"], 16)
                sp.wait_ge(s["mod_stored"], 16 * (l + 1))
                for t in range(T):
                    src = mod_d[l][int(t >= TL), 0:2 * D].rearrange("(w p k) -> p w k", w=2, k=KT)
                    sp.dma_start(modcol[:, t], src).then_inc(s["modcol_in"], 16)
                small = 0
                for h in range(6):
                    gain = A["gqa_q_norm"] if h < 4 else A["gqa_k_norm"]
                    sp.dma_start(gains[:, h, :], gain[l].partition_broadcast(P)).then_inc(s["wsmall_in"], 16)
                sp.dma_start(lgain[:, 0:192], A["mla_q_norm"][l].partition_broadcast(P)).then_inc(s["wsmall_in"], 16)
                sp.dma_start(lgain[:, 192:320], A["mla_kv_norm"][l].partition_broadcast(P)).then_inc(s["wsmall_in"], 16)
                sp.dma_start(wqu[0:96], A["mla_w_q_up"][l].rearrange("(k p) n -> p k n", p=96)).then_inc(s["wsmall_in"], 16)
                sp.dma_start(wkvu, A["mla_w_kv_up"][l]).then_inc(s["wsmall_in"], 16)
                if l == 0:
                    sp.wait_ge(inputs_copied, 32)

                def x_load(t, first):
                    if not first:
                        sp.wait_ge(s["hT_tr"], g(t))
                    sp.dma_start(xt, x_in[l][span(t * P, P), :]).then_inc(s["x_in"], 16)
                x_load(0, True)
                if l == 0:
                    sp.wait_ge(rel_stored, 16)
                    sp.dma_start(rel_copies, rel_d[0].partition_broadcast(GRID_W)).then_inc(rel_stored, 16)
                with sp.Fori(1, T) as t:
                    x_load(t, False)

                if stop == "P":
                    continue
                sp.wait_ge(s["u_mm"], NCH * T * (l + 1))
                if l == 0:
                    sp.wait_ge(rel_stored, 32)
                for h in range(4):
                    for r2 in range(2):
                        src = bass.AP(rel_copies.tensor, (1 + h * 15 - r2) * REL_ROW + l * P + GRID_W - 1,
                                      [[REL_COPY - 1, GRID_W], [REL_ROW, 16], [1, GRID_W]])
                        dst = bias_t[r2 * GRID_W:(r2 + 1) * GRID_W, h, :]
                        sp.dma_start(dst.rearrange("p (j c) -> p j c", c=GRID_W), src).then_inc(s["bias_in"], 16)
                sp.dma_start(wout, A["w_out"][l].rearrange("(p k) n -> p k n", k=KT)).then_inc(s["wout_in"], 16)
                for stream in range(2):
                    for n, w in enumerate((2, 4, 3)):
                        sp.dma_start(vec[:, 3 * stream + n, :], mod_d[l][stream, w * D:(w + 1) * D].partition_broadcast(P)).then_inc(s["vec_in"], 16)
                sp.wait_ge(s["round_evac"], ROUNDS * T * (l + 1))
                for n, w in enumerate(("diff_lq1", "diff_lk1", "diff_lq2", "diff_lk2")):
                    sp.dma_start(lamb[:, n, :], A[w][l].partition_broadcast(P)).then_inc(s["lam_in"], 16)
                sp.dma_start(subg[:, :], A["diff_subln"][l].partition_broadcast(P)).then_inc(s["lam_in"], 16)

                def att_rows(t, first):
                    rows = span(t * P, P)
                    if not first:
                        sp.wait_ge(s["x1_ready"], g(t))
                    sp.dma_start(xa, x_in[l][rows, :]).then_inc(s["xa_in"], 16)
                    sp.wait_ge(s["x1_ready"], g(t) + 1)
                    sp.dma_start(x_mix[l][rows, :], xb).then_inc(s["x1_stored"], 16)
                    sp.wait_ge(s["h2_ready"], g(t) + 1)
                    sp.dma_start(h2_d[l][rows, :], h2b).then_inc(s["h2_stored"], 16)

                att_rows(0, l == 0)
                with sp.Fori(1, T if l == 0 else TL) as t:
                    att_rows(t, False)
                if stop == "A":
                    continue
                nt = T if l == 0 else TL
                gend = T * l + nt
                sp.wait_ge(s["pv_done"], HEADS * gend + 2)
                for w, (name, e0) in enumerate((("shared_w_gate", 0), ("shared_w_up", DE))):
                    sp.dma_start(swgu[:, :, e0:e0 + DE], A[name][l].rearrange("(p k) n -> p k n", k=KT)).then_inc(s["s_w_in"], 16)
                sp.dma_start(swd, A["shared_w_down"][l].rearrange("(p k) n -> p k n", k=2)).then_inc(s["s_w_in"], 16)
                sp.dma_start(rw, A["router_w"].rearrange("(p k) n -> p k n", k=KT)).then_inc(s["s_w_in"], 16)
                sp.dma_start(rb, A["router_b"].partition_broadcast(P)).then_inc(s["s_w_in"], 16)
                for stream in range(2):
                    sp.dma_start(g2[:, stream, :], mod_d[l][stream, 5 * D:6 * D].partition_broadcast(P)).then_inc(s["s_w_in"], 16)
                sp.wait_ge(s["h2_stored"], 16 * gend)
                sp.wait_ge(s["x1_stored"], 16 * gend)

                def s_load(t, u, b, first):
                    if not first:
                        sp.wait_ge(s["s_tr"], g(t) - 1)
                    sp.dma_start(hs[b], h2_d[l][span(t * P, P), :]).then_inc(s[f"hs_in{b}"], 16)
                    if not first:
                        sp.wait_ge(s["s_x2"], g(t) - 1)
                    sp.dma_start(x1b[b], x_mix[l][span(t * P, P), :]).then_inc(s[f"x1_in{b}"], 16)

                def s_store(t, b):
                    sp.wait_ge(s["s_x2"], g(t) + 1)
                    sp.dma_start(x_ffn[l][span(t * P, P), :], ob[b]).then_inc(s[f"s_stored{b}"], 16)

                s_load(0, 0, 0, l == 0)
                s_load(1, 0, 1, l == 0)
                with sp.Fori(0, nt // 2 - 1) as i:
                    for b in range(2):
                        s_store(2 * i + b, b)
                        s_load(2 * i + 2 + b, i + 1, b, False)
                for b in range(2):
                    s_store(nt - 2 + b, b)
                sp.wait_ge(s["r_ready"], l + 1)
                nb = NBK[l]
                ge = lambda b: b + NBK[0] * l

                def w_load(blk, b, first):
                    if not first:
                        sp.wait_ge(s["e_d"], ge(blk) - 1)
                    e = sp.value_load(bexp_i[0:1, span(blk, 1)], min_val=0, max_val=NE - 1)
                    for n, name in enumerate(("moe_w_gate", "moe_w_up")):
                        src = A[name][l].rearrange("e (p k) n -> e p (k n)", k=KT)[bass.ds(e, 1)].rearrange("o p n -> (o p) n")
                        sp.dma_start(wgu[b][:, n, :], src).then_inc(s[f"e_w_in{b}"], 16)
                    src = A["moe_w_down"][l].rearrange("e (p k) n -> e p (k n)", k=2)[bass.ds(e, 1)].rearrange("o p n -> (o p) n")
                    sp.dma_start(wdn[b].rearrange("p a b -> p (a b)"), src).then_inc(s[f"e_w_in{b}"], 16)

                def y_store(blk, b):
                    sp.wait_ge(s["e_y_v"], ge(blk) + 1)
                    sp.wait_ge(s["e_y_s"], ge(blk) + 1)
                    sp.dma_start(y_d[l][span(blk * P, P), :], yb[b]).then_inc(s[f"e_stored{b}"], 16)

                w_load(0, 0, l == 0)
                w_load(1, 1, l == 0)
                with sp.Fori(0, nb // 2 - 1) as i:
                    for b in range(2):
                        w_load(2 * i + 2 + b, b, False)
                        y_store(2 * i + b, b)
                for b in range(2):
                    y_store(nb - 2 + b, b)
                for b in range(2):
                    sp.wait_ge(s[f"s_stored{b}"], 8 * gend if l == 0 else 16 * (T // 2 + TL // 2))
                gc = lambda t: t + T * l
                for b in range(2):
                    sp.dma_start(x2b[b], x_ffn[l][b * P:(b + 1) * P, :]).then_inc(s[f"c_x_in{b}"], 16)
                if l == DEPTH - 1:
                    sp.dma_start(fgain, A["final_norm"].partition_broadcast(P)).then_inc(fgain_in, 16)
                dst = (lambda rows: x_in[l + 1][rows, :]) if l < DEPTH - 1 else (lambda rows: out[0, rows, :])

                def c_store(t, b):
                    sp.wait_ge(s["c_x3"], gc(t) + 1)
                    sp.dma_start(dst(span(t * P, P)), x3b[b]).then_inc(s[f"c_stored{b}"], 16)

                with sp.Fori(0, nt // 2 - 1) as i:
                    for b in range(2):
                        c_store(2 * i + b, b)
                        sp.dma_start(x2b[b], x_ffn[l][span((2 * i + 2 + b) * P, P), :]).then_inc(s[f"c_x_in{b}"], 16)
                for b in range(2):
                    c_store(nt - 2 + b, b)
                for b in range(2):
                    sp.wait_ge(s[f"c_stored{b}"], 16 * (gend // 2))

        @block.scalar
        def _(act):
            act.wait_ge(cond_in, 32)
            act.activation(ctmp[:, :, :], csrc[:, :, :], ACT.Exp, scale=-1.0).then_inc(exp_c, 1)
            for l in range(1 if stop in ("P", "A") else DEPTH):
                g = lambda t: t + T * l

                def square(t, first):
                    b = 0
                    act.wait_ge(s["x_in"], 16 * g(t) + 16)
                    if not first:
                        act.wait_ge(s["rstd_ready"], g(t))
                    act.activation(junk, xt, ACT.Square, scale=D ** -0.5, accum_out=sumsq[:, 0:1]).then_inc(s["ssq"], 1)

                def evac_hT(t, b):
                    act.wait_ge(s["hT_tr"], g(t) + 1)
                    for j in range(KT):
                        ins = act.activation(hT[b][:, j, :], PT[:, j * P:(j + 1) * P], ACT.Identity,
                                             bias=modcol[:, span(t, 1), 0, j], scale=modcol[:, span(t, 1), 1, j])
                    ins.then_inc(s["hT_evac"], 1)

                def evac_u(t, c, first):
                    act.wait_ge(s["u_mm"], NCH * g(t) + c + 1)
                    if c == 0 and not first:
                        act.wait_ge(s["u_used"], g(t))
                        act.wait_ge(s["v_copied"], g(t))
                        act.wait_ge(s["round_tr"], ROUNDS * (g(t) - 1) + 1)
                    act.activation(U[:, c * UCH:(c + 1) * UCH], ubank[c][:, 0:UCH], ACT.Copy).then_inc(s["u_evac"], 1)

                def tile(t, b, first, last):
                    if not last:
                        square(t + 1, False)
                    for c in range(NCH - 1):
                        evac_u(t, c, first)
                    if not last:
                        evac_hT(t + 1, 1 - b)
                    evac_u(t, NCH - 1, first)

                act.wait_ge(s["modcol_in"], 16 * T * (l + 1))
                square(0, l == 0)
                evac_hT(0, 0)
                tile(0, 0, True, False)
                with act.Fori(0, (T - 2) // 2) as i:
                    tile(2 * i + 1, 1, False, False)
                    tile(2 * i + 2, 0, False, False)
                tile(T - 1, 1, False, True)

                if stop == "P":
                    continue
                act.wait_ge(s["lam_sum"], l + 1)
                act.activation(nlam[:, 0:2], nlam[:, 2:4], ACT.Exp).then_inc(s["lam_exp"], 1)

                def att(t, nk, first):
                    n0 = HEADS * g(t)
                    for k in range(HEADS + 1):
                        if k < HEADS:
                            act.wait_ge(s["neg_max"], n0 + k + 1)
                            act.wait_ge(s["p_tr"], n0 + k + 1)
                            act.activation(Pb[k % 2][:, 0:nk], (S0, S1)[k % 2][:, 0:nk], ACT.Exp, bias=nmax[:, k:k + 1],
                                           accum_out=rsum[:, k:k + 1]).then_inc(s["exp_done"], 1)
                        if k:
                            u = k - 1
                            h = 4 if nk == NTOK else 1
                            act.wait_ge(s["p_tr"], n0 + u + 3)
                            act.wait_ge(s["pv_done"], n0 + u + 1)
                            act.activation(PTs[u % 2][:, h:nk // P, :].rearrange("p a b -> p (a b)"), PT[:, 512:512 + nk - h * P], ACT.Copy).then_inc(s["pt_s"], 1)
                    act.wait_ge(s["ot_tr"], g(t) + 1)
                    act.activation(OT[:, 4:8, :].rearrange("p a b -> p (a b)"), PT[:, 512:1024], ACT.Copy).then_inc(s["ot_s"], 1)
                    act.wait_ge(s["x1_ready"], g(t) + 1)
                    if not first:
                        act.wait_ge(s["h2_stored"], 16 * g(t))
                    act.activation(h2b, xb, ACT.Square, scale=D ** -0.5, accum_out=h2s[:, 0:1]).then_inc(s["x1_sq"], 1)

                att(0, NTOK, l == 0)
                with act.Fori(1, TL) as t:
                    att(t, NTOK, False)
                if l == 0:
                    with act.Fori(TL, T) as t:
                        att(t, CTX, False)
                if stop == "A":
                    continue
                nt = T if l == 0 else TL
                gend = T * l + nt

                def ffn(m, gi, b, more):
                    act.wait_ge(s[m + "g"], gi + 1)
                    act.activation(gex[b], (S0, S1)[b][:, 0:DE], ACT.Exp, scale=-1.0).then_inc(s[m + "ex"], 1)
                    if more:
                        act.wait_ge(s[m + ("tr")], gi + 2)
                        act.activation((hT2, XT)[m == "e_"][1 - b][:, 4:8, :].rearrange("p a b -> p (a b)"), PT[:, 512:1024], ACT.Copy).then_inc(s[m + "t_s"], 1)

                def first_T(m, gi, b):
                    act.wait_ge(s[m + "tr"], gi + 1)
                    act.activation((hT2, XT)[m == "e_"][b][:, 4:8, :].rearrange("p a b -> p (a b)"), PT[:, 512:1024], ACT.Copy).then_inc(s[m + "t_s"], 1)

                first_T("s_", g(0), 0)
                with act.Fori(0, nt // 2 - 1) as i:
                    for b in range(2):
                        ffn("s_", g(2 * i + b), b, True)
                ffn("s_", g(nt - 2), 0, True)
                ffn("s_", g(nt - 1), 1, False)
                act.wait_ge(s["s_lg"], gend)
                act.activation(score[:, 0:nt, :], lg[:, 0:nt, :], ACT.Exp, scale=-1.0).then_inc(s["r_exp"], 1)
                nb = NBK[l]
                ge = lambda b: b + NBK[0] * l
                first_T("e_", ge(0), 0)

                def e_out(blk, b):
                    act.wait_ge(s["e_d"], ge(blk) + 1)
                    act.activation(yb[b][:, 512:1024], (S0, S1)[b][:, 512:1024], ACT.Copy).then_inc(s["e_y_s"], 1)

                def e_block(blk, u, b, more, first):
                    ffn("e_", ge(blk), b, more)
                    if not first:
                        act.wait_ge(s[f"e_stored{b}"], 16 * (u + NBK[0] // 2 * l))
                    e_out(blk, b)

                for b in range(2):
                    e_block(b, 0, b, True, l == 0)
                with act.Fori(1, nb // 2 - 1) as i:
                    for b in range(2):
                        e_block(2 * i + b, i, b, True, False)
                for b in range(2):
                    e_block(nb - 2 + b, nb // 2 - 1, b, b == 0, False)
                if l == DEPTH - 1:
                    for t in range(TL):
                        act.wait_ge(c_sum, t + 1)
                        act.activation(x2b[t % 2], x3b[t % 2], ACT.Square, scale=D ** -0.5, accum_out=h2s[:, 2:3]).then_inc(s["c_sq"], 1)

        @block.tensor
        def _(pe):
            pe.wait_ge(consts_in, 16)
            pe.wait_ge(cs_ready, 3)
            for l in range(1 if stop in ("P", "A") else DEPTH):
                g = lambda t: t + T * l
                mod_ps, row_ps = (B6, B7), (S0[:, 0:512], S0[:, 512:1024])

                def mod_chunk(i, first):
                    for b in range(2):
                        n = 2 * i + b
                        pe.wait_ge(s[f"mod_w_in{b}"], 16 * (i + 1 + NMCH // 2 * l))
                        if not first:
                            pe.wait_ge(s["mod_part"], n - 1 + NMCH * l)
                        for k in range(KT):
                            q = k % 4
                            mm = pe.matmul(mod_ps[b][32 * q:32 * q + 32, :], cs[:, k, :], wm[b][:, k, :],
                                           start=k < 4, stop=k >= 4)
                        mm.then_inc(s["mod_mm"], 1)
                        pe.wait_ge(s["mod_part"], n + 1 + NMCH * l)
                        if not first:
                            pe.wait_ge(s["mod_row"], n - 1 + NMCH * l)
                        pe.matmul(row_ps[b][0:2, :], C("pick"), part[b], start=True, stop=True).then_inc(s["mod_sel"], 1)

                mod_chunk(0, True)
                with pe.Fori(1, NMCH // 2) as i:
                    mod_chunk(i, False)

                def transpose_x(t, first):
                    pe.wait_ge(s["xn_done"], g(t) + 1)
                    if not first:
                        pe.wait_ge(s["hT_evac"], g(t))
                    xs = xt.rearrange("p (n k) -> p k n", k=KT)
                    for j in range(KT):
                        tr = pe.transpose(PT[:, j * P:(j + 1) * P], xs[:, j, :], ident)
                    tr.then_inc(s["hT_tr"], 1)

                def prep_round(t, r):
                    def copies(srcs, width):
                        for n, a in enumerate(srcs):
                            tr = pe.transpose(B7[0:width, n * P:(n + 1) * P], a, ident)
                        tr.then_inc(s["round_tr"], 1)
                    if r == 0:
                        pe.wait_ge(s["u_evac"], NCH * g(t) + NCH)
                    if not (l == 0 and r == 0 and isinstance(t, int) and t == 0):
                        pe.wait_ge(s["round_evac"], ROUNDS * g(t) + r)
                    if r == 0:
                        copies([U[:, a:a + P] for a in (NK_, NK_ + P, NQ, NQ + P)], P)
                    if r == 1:
                        pe.wait_ge(s["lor_ready"], g(t) + 1)
                        pe.transpose(B7[0:96, 0:P], lor[:, 0:96], ident)
                        pe.transpose(B7[0:96, P:2 * P], lor[:, 96:192], ident)
                        pe.transpose(B7[:, 2 * P:3 * P], lor[:, 192:320], ident).then_inc(s["round_tr"], 1)
                    if r == 2:
                        for k in range(2):
                            mm = pe.matmul(B7[:, 0:384], lorT[0:96, k, :], wqu[0:96, k, :], start=k == 0, stop=k == 1)
                        mm.then_inc(s["round_tr"], 1)
                    if r == 3:
                        pe.matmul(B7[:, :], lorT[:, 2, :], wkvu, start=True, stop=True).then_inc(s["round_tr"], 1)
                    if r == 4:
                        pe.wait_ge(s["st_ready"], g(t) + 1)
                        copies([st[:, P * n:P * n + P] for n in range(4)], P)
                    if r == 5:
                        copies([st[:, P * n:P * n + P] for n in range(4, 7)], P)
                    if r == 6:
                        pe.wait_ge(s["st_m_ready"], g(t) + 1)
                        copies([st[:, ST_MK + 96 * n:ST_MK + 96 * n + 96] for n in range(4)], 96)
                    if r == 7:
                        copies([st[:, ST_MQ + 96 * n:ST_MQ + 96 * n + 96] for n in range(4)], 96)

                def tile(t, b, first, last):
                    pe.wait_ge(s["hT_evac"], g(t) + 1)
                    for half in range(2 * NCH):
                        c, k0 = half // 2, (half % 2) * (KT // 2)
                        if k0 == 0:
                            pe.wait_ge(s["win_in"][c], 16 * (l + 1))
                            if not first:
                                pe.wait_ge(s["u_evac"], NCH * (g(t) - 1) + c + 1)
                        for k in range(k0, k0 + KT // 2):
                            mm = pe.matmul(ubank[c][:, 0:UCH], hT[b][:, k, :], win[:, k, c * UCH:(c + 1) * UCH],
                                           start=k == 0, stop=k == KT - 1)
                        if k0:
                            mm.then_inc(s["u_mm"], 1)
                        if not first and half < ROUNDS:
                            prep_round(t - 1, half)
                        if half == 7 and not last:
                            transpose_x(t + 1, False)

                transpose_x(0, True)
                pe.wait_ge(s["wsmall_in"], 16 * 10 * (l + 1))
                pe.wait_ge(s["mod_row"], NMCH * (l + 1))
                tile(0, 0, True, False)
                with pe.Fori(0, (T - 2) // 2) as i:
                    tile(2 * i + 1, 1, False, False)
                    tile(2 * i + 2, 0, False, False)
                tile(T - 1, 1, False, True)
                for r in range(ROUNDS):
                    prep_round(T - 1, r)

                if stop == "P":
                    continue
                units = [(P, SL_DK + m // 4, V_D + 64 * (m // 2)) for m in range(8)]
                units += [(P, SL_AK, V_A + 64 * (h // 2)) for h in range(4)]
                units += [(96, SL_MK + h, V_M + 64 * h) for h in range(4)]
                units += [(P, SL_NK + h // 2, V_N + 64 * h) for h in range(4)]

                def att(t, nk, first):
                    n0 = HEADS * g(t)
                    k0 = NTOK - nk
                    pe.wait_ge(s["qs_ready"], g(t) + 1)
                    if not first:
                        pe.wait_ge(s["res_mul"], 2 * g(t))
                    for k in range(HEADS + 2):
                        if k < HEADS:
                            nr, ks, _ = units[k]
                            pe.wait_ge(s["exp_done"], n0 + k + 1)
                            for c0 in range(0, nk, 512):
                                c1 = min(c0 + 512, nk)
                                mm = pe.matmul((S0, S1)[k % 2][:, c0:c1], Qs[0:nr, k, :], qk[0:nr, ks, k0 + c0:k0 + c1],
                                               start=True, stop=True)
                            mm.then_inc(s["scored"], 1)
                        if 1 <= k <= HEADS:
                            u = k - 1
                            pe.wait_ge(s["exp_done"], n0 + u + 3)
                            pe.wait_ge(s["pt_v"], n0 + u + 2)
                            pe.wait_ge(s["pt_s"], n0 + u + 2)
                            for j in range(nk // P):
                                c0 = j * P if nk == NTOK else j * 512
                                tr = pe.transpose(PT[:, c0:c0 + P], Pb[u % 2][:, j * P:(j + 1) * P], ident)
                            tr.then_inc(s["p_tr"], 1)
                        if k >= 2:
                            u = k - 2
                            pe.wait_ge(s["pt_v"], n0 + u + 3)
                            pe.wait_ge(s["pt_s"], n0 + u + 3)
                            pe.wait_ge(s["o_evac"], n0 + u + 1)
                            for j in range(nk // P):
                                mm = pe.matmul((B6, B7)[u % 2][:, 0:64], PTs[u % 2][:, j, :],
                                               vals[:, k0 // P + j, units[u][2]:units[u][2] + 64], start=j == 0, stop=j == nk // P - 1)
                            mm.then_inc(s["pv_done"], 1)
                    pe.wait_ge(s["o_all"], g(t) + 1)
                    o8 = O.rearrange("p (n k) -> p k n", k=KT)
                    for j in range(KT):
                        tr = pe.transpose(PT[:, j * P:(j + 1) * P], o8[:, j, :], ident)
                    tr.then_inc(s["ot_tr"], 1)
                    pe.wait_ge(s["ot_v"], g(t) + 1)
                    pe.wait_ge(s["ot_s"], g(t) + 1)
                    for c in range(2):
                        for k in range(KT):
                            mm = pe.matmul(S1[:, c * 512:(c + 1) * 512], OT[:, k, :], wout[:, k, c * 512:(c + 1) * 512],
                                           start=k == 0, stop=k == KT - 1)
                        mm.then_inc(s["op_mm"], 1)

                pe.wait_ge(s["u_evac"], NCH * T * (l + 1))
                pe.wait_ge(s["round_evac"], ROUNDS * T * (l + 1))
                pe.wait_ge(s["wout_in"], 16 * (l + 1))
                att(0, NTOK, l == 0)
                with pe.Fori(1, TL) as t:
                    att(t, NTOK, False)
                if l == 0:
                    with pe.Fori(TL, T) as t:
                        att(t, CTX, False)
                if stop == "A":
                    continue
                nt = T if l == 0 else TL
                gend = T * l + nt

                def transposes(m, gi, b):
                    x8 = (hs, xg)[m == "e_"][b].rearrange("p (n k) -> p k n", k=KT)
                    for j in range(KT):
                        tr = pe.transpose(PT[:, j * P:(j + 1) * P], x8[:, j, :], ident)
                    tr.then_inc(s[m + "tr"], 1)

                def ffn(m, gi, b, nxt):
                    e = m == "e_"
                    X = (hT2, XT)[e][b]
                    G = (S0, S1)[b]
                    pe.wait_ge(s[m + "t_v"], gi + 1)
                    pe.wait_ge(s[m + "t_s"], gi + 1)
                    if not e:
                        pe.wait_ge(s["s_lg"], gi)
                        for k in range(KT):
                            mm = pe.matmul(B6[:, 0:NE], X[:, k, :], rw[:, k, :], start=k == 0, stop=k == KT - 1)
                        mm.then_inc(s["s_rt"], 1)
                    for w, name in enumerate(("g", "u")):
                        for k in range(KT):
                            wk = wgu[b][:, w, k * DE:(k + 1) * DE] if e else swgu[:, k, w * DE:(w + 1) * DE]
                            mm = pe.matmul(G[:, 512 * w:512 * w + DE], X[:, k, :], wk, start=k == 0, stop=k == KT - 1)
                        mm.then_inc(s[m + name], 1)
                    nxt()
                    pe.wait_ge(s[m + "hid"], gi + 1)
                    hd = hid[b].rearrange("p (n k) -> p k n", k=2)
                    for j in range(2):
                        tr = pe.transpose(B7[:, j * P:(j + 1) * P], hd[:, j, :], ident)
                    tr.then_inc(s[m + "ht"], 1)
                    pe.wait_ge(s[m + "htv"], gi + 1)
                    for c in range(2):
                        for k in range(2):
                            wk = wdn[b][:, k, c * 512:(c + 1) * 512] if e else swd[:, k, c * 512:(c + 1) * 512]
                            mm = pe.matmul(G[:, c * 512:(c + 1) * 512], hidT[b][:, k, :], wk, start=k == 0, stop=k == 1)
                    mm.then_inc(s[m + "d"], 1)

                pe.wait_ge(s["res_mul"], 2 * gend)
                pe.wait_ge(s["s_w_in"], 16 * 7 * (l + 1))
                def s_next(t, b, first):
                    pe.wait_ge(s[f"hs_in{b}"], hs_count(t, b))
                    if not first:
                        pe.wait_ge(s["s_t_v"], g(t))
                        pe.wait_ge(s["s_t_s"], g(t))
                    transposes("s_", g(t), b)

                def hs_count(t, b):
                    return 8 * (t - b) + 16 + 8 * T * l

                s_next(0, 0, l == 0)
                def s_block(t, b, more, first):
                    if not first:
                        pe.wait_ge(s["s_ob"], g(t) - 1)
                    ffn("s_", g(t), b, (lambda: s_next(t + 1, 1 - b, False)) if more else (lambda: None))
                for b in range(2):
                    s_block(b, b, True, l == 0)
                for i in range(1, nt // 2 - 1):
                    for b in range(2):
                        s_block(2 * i + b, b, True, False)
                for b in range(2):
                    s_block(nt - 2 + b, b, b == 0, False)
                pe.wait_ge(s["r_mat"], l + 1)
                pe.matmul(B6[:, 0:nt * NE], C("before"), both[:, 0:nt, :].rearrange("p a b -> p (a b)"), start=True, stop=True)
                pe.matmul(B7[:, 0:nt * NE], ones, both[:, 0:nt, :].rearrange("p a b -> p (a b)"), start=True, stop=True).then_inc(s["r_cum"], 1)
                nb = NBK[l]
                ge = lambda b: b + NBK[0] * l
                pe.wait_ge(s["s_ob"], gend)

                def e_next(blk, u, b, first):
                    pe.wait_ge(s[f"e_x_in{b}"], 16 * (u + 1 + NBK[0] // 2 * l))
                    if not first:
                        pe.wait_ge(s["e_t_v"], ge(blk))
                        pe.wait_ge(s["e_t_s"], ge(blk))
                    transposes("e_", ge(blk), b)

                def e_block(blk, u, b, more, first):
                    pe.wait_ge(s[f"e_w_in{b}"], 48 * (u + 1 + NBK[0] // 2 * l))
                    if not first:
                        pe.wait_ge(s["e_y_v"], ge(blk) - 1)
                        pe.wait_ge(s["e_y_s"], ge(blk) - 1)
                    ffn("e_", ge(blk), b, (lambda: e_next(blk + 1, u + b, 1 - b, False)) if more else (lambda: None))

                e_next(0, 0, 0, l == 0)
                for b in range(2):
                    e_block(b, 0, b, True, l == 0)
                with pe.Fori(1, nb // 2 - 1) as i:
                    for b in range(2):
                        e_block(2 * i + b, i, b, True, False)
                for b in range(2):
                    e_block(nb - 2 + b, nb // 2 - 1, b, b == 0, False)

        @block.gpsimd
        def _(pool):
            pool.memset(halfs[:, 0:8], -0.5).then_inc(halfs_set, 1)
            pool.memset(halfs[:, 8:14], 1.0 / 64).then_inc(halfs_set, 1)
            pool.memset(halfs[:, 14:16], 1.0).then_inc(halfs_set, 1)
            pool.memset(halfs[:, 16:24], EPS).then_inc(halfs_set, 1)
            pool.wait_ge(halfs_set, 4)
            for l in range(1 if stop in ("P", "A") else DEPTH):
                g = lambda t: t + T * l

                def rstd_of(t):
                    pool.wait_ge(s["ssq"], g(t) + 1)
                    pool.tensor_tensor(meansq[:, 0:1], sumsq[:, 0:1], eps8[:, 0:1], ALU.add).then_inc(s["mean_x"], 1)
                    pool.wait_ge(s["mean_x"], g(t) + 1)
                    pool.tensor_tensor(rstd[:, 0:1], meansq[:, 0:1], halfs[:, 0:1], ALU.pow).then_inc(s["rstd_ready"], 1)

                def prep(t):
                    pool.wait_ge(s["u_evac"], NCH * g(t) + NCH)
                    vt = vals[:, span(t, 1), :]
                    pool.tensor_copy(vt[:, :, V_A:V_A + 128], U[:, AV:AV + 128].unsqueeze(1))
                    pool.tensor_copy(vt[:, :, V_N:V_N + 256], U[:, NV:NV + 256].unsqueeze(1))
                    pool.tensor_copy(vt[:, :, V_D:V_D + 256], U[:, DV:DV + 256].unsqueeze(1)).then_inc(s["v_copied"], 1)
                    pool.wait_ge(s["stats"], g(t) + 1)
                    ch = Count(pool, s["g_prep"], 2 * g(t))
                    ch.done(pool.tensor_tensor(m8[:, :], s8[:, :], inv8, ALU.mult)).sync()
                    ch.done(pool.tensor_tensor(m8[:, :], m8[:, :], eps8, ALU.add)).sync()
                    assert ch.n == 2
                    pool.tensor_tensor(r8[:, :], m8[:, :], halfs[:, 0:8], ALU.pow).then_inc(s["r8_ready"], 1)

                rstd_of(0)
                rstd_of(1)
                with pool.Fori(0, T - 2) as t:
                    prep(t)
                    rstd_of(t + 2)
                prep(T - 2)
                prep(T - 1)

                if stop == "P":
                    continue
                pool.wait_ge(s["bias_in"], 16 * 8 * (l + 1))
                bt = bias_t.rearrange("p h (j c) -> p (h j) c", c=GRID_W)
                pool.wait_ge(s["r8_ready"], T * (l + 1))
                pool.tensor_tensor(bt, bt, C("window").unsqueeze(1).to_broadcast([P, 64, GRID_W]), ALU.add).then_inc(s["bias_ready"], 1)

                def att(t, gains_at, first):
                    pool.wait_ge(s["d_stat"], g(t) + 1)
                    ch = Count(pool, s["g_att"], 5 * g(t))
                    ch.done(pool.tensor_tensor(dstat[:, 4:8], dstat[:, 0:4], eps8[:, 0:4], ALU.add)).sync()
                    pool.tensor_tensor(dstat[:, 4:8], dstat[:, 4:8], halfs[:, 0:4], ALU.pow).then_inc(s["d_rs"], 1)
                    pool.wait_ge(s["xa_in"], 16 * g(t) + 16)
                    pool.wait_ge(s["res_mul"], 2 * g(t) + 2)
                    pool.tensor_tensor(xb, xb, xa, ALU.add).then_inc(s["x1_ready"], 1)
                    pool.wait_ge(s["x1_sq"], g(t) + 1)
                    ch.done(pool.tensor_tensor(h2s[:, 1:2], h2s[:, 0:1], eps8[:, 0:1], ALU.add)).sync()
                    ch.done(pool.tensor_tensor(h2s[:, 1:2], h2s[:, 1:2], halfs[:, 0:1], ALU.pow)).sync()
                    ch.done(pool.tensor_tensor(h2b, xb, h2s[:, 1:2].to_broadcast([P, D]), ALU.mult)).sync()
                    ch.done(pool.tensor_tensor(h2b, h2b, vec[:, gains_at + 1, :], ALU.mult)).sync()
                    pool.tensor_tensor(h2b, h2b, vec[:, gains_at + 2, :], ALU.add).then_inc(s["h2_ready"], 1)
                    assert ch.n == 5

                pool.wait_ge(s["vec_in"], 16 * 6 * (l + 1))
                with pool.Fori(0, TL) as t:
                    att(t, 0, False)
                if l == 0:
                    with pool.Fori(TL, T) as t:
                        att(t, 3, False)
                if stop == "A":
                    continue
                nt = T if l == 0 else TL
                gend = T * l + nt

                def s_sum(t, u, b):
                    pool.wait_ge(s["s_ob"], g(t) + 1)
                    pool.wait_ge(s[f"x1_in{b}"], 16 * (u + 1 + T // 2 * l))
                    pool.tensor_tensor(ob[b], ob[b], x1b[b], ALU.add).then_inc(s["s_x2"], 1)
                with pool.Fori(0, nt // 2) as i:
                    for b in range(2):
                        s_sum(2 * i + b, i, b)
                if l == 0:
                    pool.wait_ge(zeros_stored, 16 * DEPTH)
                pool.wait_ge(s["r_slots"], l + 1)
                for t in range(nt):
                    for j in range(TOPK):
                        pool.indirect_dma_start(out=slot_tok[l], out_offset=bass.IndirectOffsetOnAxis(ap=slots[:, t, j:j + 1], axis=0),
                                                in_=tok_u[:, t:t + 1], in_offset=None).then_inc(s["r_scat"], 16)
                pool.wait_ge(s["r_scat"], 16 * TOPK * gend)
                nb = NBK[l]
                pool.dma_start(table_u[:, 0:nb], slot_tok[l][0:nb * P, :].rearrange("(b p) o -> p (b o)", p=P),
                               allow_slow_non_contiguous=True).then_inc(s["r_tab"], 16)
                pool.wait_ge(s["r_tab"], 16 * (l + 1))
                ge = lambda b: b + NBK[0] * l

                def e_gather(blk, b, first):
                    if not first:
                        pool.wait_ge(s["e_tr"], ge(blk) - 1)
                    pool.tensor_copy(idx1[b], table_u[:, span(blk, 1)]).then_inc(s["e_idx"], 1)
                    pool.wait_ge(s["e_idx"], ge(blk) + 1)
                    pool.sem_inc(s["idx_seen"], 1)
                    pool.indirect_dma_start(out=xg[b], out_offset=None, in_=h2_d[l],
                                            in_offset=bass.IndirectOffsetOnAxis(ap=idx1[b], axis=0)).then_inc(s[f"e_x_in{b}"], 16)
                for b in range(2):
                    e_gather(b, b, l == 0)
                with pool.Fori(1, nb // 2) as i:
                    for b in range(2):
                        e_gather(2 * i + b, b, False)
                for b in range(2):
                    pool.wait_ge(s[f"e_stored{b}"], 16 * ((nb + NBK[0] * l) // 2))

                def c_gather(t, b, first):
                    if not first:
                        pool.wait_ge(s["c_x3"], g(t) - 1)
                    pool.tensor_copy(idx2[b].unsqueeze(1), slots[:, span(t, 1), :]).then_inc(s["c_idx"], 1)
                    pool.wait_ge(s["c_idx"], g(t) + 1)
                    pool.sem_inc(s["idx_seen"], 1)
                    for j in range(TOPK):
                        pool.indirect_dma_start(out=y12[b][:, j, :], out_offset=None, in_=y_d[l],
                                                in_offset=bass.IndirectOffsetOnAxis(ap=idx2[b][:, j:j + 1], axis=0)).then_inc(s[f"c_y_in{b}"], 16)
                for b in range(2):
                    c_gather(b, b, l == 0)
                if l < DEPTH - 1:
                    with pool.Fori(1, nt // 2) as i:
                        for b in range(2):
                            c_gather(2 * i + b, b, False)
                else:
                    for t in range(TL):
                        pool.wait_ge(s["c_sq"], t + 1)
                        pool.tensor_tensor(h2s[:, 3:4], h2s[:, 2:3], eps8[:, 0:1], ALU.add).then_inc(s["c_mean"], 1)
                        pool.wait_ge(s["c_mean"], t + 1)
                        pool.tensor_tensor(h2s[:, 3:4], h2s[:, 3:4], halfs[:, 0:1], ALU.pow).then_inc(s["c_rs"], 1)
                        if t + 2 < TL:
                            c_gather(t + 2, t % 2, False)

        @block.vector
        def _(dve):
            dve.memset(cs[:, :, :], 0.0).then_inc(cs_ready, 1)
            dve.memset(relpad, 0.0).then_inc(relpad_set, 1)
            dve.memset(zeros_u, 0).then_inc(relpad_set, 1)
            R_START = [0]
            dve.wait_ge(exp_c, 1)
            ch = Count(dve, v_init, 0)
            ch.done(dve.tensor_scalar(ctmp[:, :, :], ctmp[:, :, :], 1.0, None, ALU.add)).sync()
            ch.done(dve.reciprocal(ctmp[:, :, :], ctmp[:, :, :])).sync()
            dve.wait_ge(cs_ready, 1)
            for r in range(2):
                dve.tensor_tensor(cs[:, :, r], csrc[:, r, :], ctmp[:, r, :], ALU.mult).then_inc(cs_ready, 1)
            dve.wait_ge(consts_in, 16)
            for l in range(1 if stop in ("P", "A") else DEPTH):
                g = lambda t: t + T * l
                row_ps = (S0[0:2, 0:512], S0[0:2, 512:1024])

                def mod_chunk(i):
                    for b in range(2):
                        n = 2 * i + b
                        dve.wait_ge(s["mod_mm"], n + 1 + NMCH * l)
                        dve.tensor_copy(part[b], (B6, B7)[b][:, :]).then_inc(s["mod_part"], 1)
                        dve.wait_ge(s["mod_sel"], n + 1 + NMCH * l)
                        cols = span(n * MCH, MCH)
                        dve.tensor_tensor(modrow[:, cols], row_ps[b], brow[:, cols], ALU.add).then_inc(s["mod_row"], 1)

                dve.wait_ge(s["mod_rows_in"], 16 * 6 * (l + 1))
                with dve.Fori(0, NMCH // 2) as i:
                    mod_chunk(i)
                dve.wait_ge(s["mod_row"], NMCH * (l + 1))
                for w, n in ((1, 0), (4, 1)):
                    a = modrow[:, w * D:(w + 1) * D]
                    dve.scalar_tensor_tensor(a, a, 1.0, nrow[:, n, :], ALU.add, ALU.mult).then_inc(s["mod_gain"], 1)

                def normalise(t):
                    dve.wait_ge(s["rstd_ready"], g(t) + 1)
                    dve.tensor_scalar(xt, xt, rstd[:, 0:1], None, ALU.mult).then_inc(s["xn_done"], 1)

                def rope(ch, x, t, rot, heads, outs):
                    q = rot // 4
                    ctab = cos[rot][:, span(t, 1), :]
                    stab = sin[rot][:, span(t, 1), :].rearrange("p o (a h c) -> p (o a) h c", a=2, h=2)
                    a3 = tmpA[:, 0:heads * rot].rearrange("p (h c) -> p h c", h=heads)
                    ch.done(dve.tensor_tensor(a3, x, ctab.to_broadcast([P, heads, rot]), ALU.mult))
                    x5 = x.rearrange("p h (a b c) -> p h a b c", a=2, b=2)
                    b5 = tmpB[:, 0:heads * rot].rearrange("p (h a b c) -> p h a b c", h=heads, a=2, b=2)
                    for half in range(2):
                        tab = stab[:, :, half, :].unsqueeze(1).to_broadcast([P, heads, 2, q])
                        ch.done(dve.tensor_tensor(b5[:, :, :, half, :], x5[:, :, :, 1 - half, :], tab, ALU.mult))
                    ch.sync()
                    b3 = tmpB[:, 0:heads * rot].rearrange("p (h c) -> p h c", h=heads)
                    for h0, h1, o in outs:
                        ai, bi = a3[:, h0:h1, :], b3[:, h0:h1, :]
                        if o.ndim == 4:
                            ai = ai.rearrange("p (a b) c -> p a b c", b=o.shape[2])
                            bi = bi.rearrange("p (a b) c -> p a b c", b=o.shape[2])
                        ch.done(dve.tensor_tensor(o, ai, bi, ALU.add))

                heads_of = lambda a, n: a.rearrange("p (h c) -> p h c", h=n)

                def evac_round(t, r, src, dst):
                    dve.wait_ge(s["round_tr"], ROUNDS * g(t) + r + 1)
                    dve.tensor_copy(dst, src).then_inc(s["round_evac"], 1)

                def to_qk(t, r, slot, n, rows=P):
                    evac_round(t, r, B7[0:rows, 0:n * P].rearrange("p (n c) -> p n c", n=n),
                               qk[0:rows, slot:slot + n, span(t * P, P)])

                N_PREP = 30

                def prep(t):
                    ch = Count(dve, s["v_prep"], N_PREP * g(t))
                    dve.wait_ge(s["u_evac"], NCH * g(t) + NCH)
                    ch.done(dve.tensor_tensor(tmpA[:, 0:384], U[:, AQ:AQ + 384], U[:, AQ:AQ + 384], ALU.mult))
                    ch.done(dve.tensor_tensor_reduce(tmpB[:, 0:192], U[:, CQ:CQ + 192], U[:, CQ:CQ + 192], 1.0 / 192, 0.0,
                                                     ALU.mult, ALU.add, s8[:, 6:7]))
                    ch.done(dve.tensor_tensor_reduce(tmpB[:, 192:320], U[:, CKV:CKV + 128], U[:, CKV:CKV + 128], 1.0 / 128, 0.0,
                                                     ALU.mult, ALU.add, s8[:, 7:8]))
                    ch.sync()
                    dve.tensor_reduce(s8[:, 0:6], heads_of(tmpA[:, 0:384], 6), AX.X, ALU.add).then_inc(s["stats"], 1)
                    dve.wait_ge(s["stats"], g(t) + 1)
                    rope(ch, heads_of(U[:, DQ:DQ + 512], 16), t, 32, 16,
                         [(0, 8, heads_of(st[:, ST_DQ:ST_DQ + 256], 8)), (8, 16, heads_of(st[:, ST_DK:ST_DK + 256], 8))])
                    to_qk(t, 0, SL_NK, 4)
                    dve.wait_ge(s["r8_ready"], g(t) + 1)
                    ch.done(dve.scalar_tensor_tensor(lor[:, 0:192], U[:, CQ:CQ + 192], r8[:, 6:7], lgain[:, 0:192], ALU.mult, ALU.mult))
                    ch.done(dve.scalar_tensor_tensor(lor[:, 192:320], U[:, CKV:CKV + 128], r8[:, 7:8], lgain[:, 192:320], ALU.mult, ALU.mult))
                    ch.sync()
                    dve.sem_inc(s["lor_ready"], 1)
                    rope(ch, heads_of(U[:, KPE:KPE + 32], 1), t, 32, 1, [(0, 1, heads_of(kper, 1))])
                    ch.sync()
                    dve.wait_ge(s["round_tr"], ROUNDS * g(t) + 2)
                    ch.done(dve.tensor_copy(lorT[0:96, 0:2, :], B7[0:96, 0:256].rearrange("p (n c) -> p n c", n=2)))
                    ch.sync()
                    dve.tensor_copy(lorT[:, 2, :], B7[:, 256:384]).then_inc(s["round_evac"], 1)
                    a3 = heads_of(tmpA[:, 0:384], 6)
                    g3 = heads_of(st[:, ST_MK:ST_MK + 384], 6)
                    ch.done(dve.tensor_tensor(a3, heads_of(U[:, AQ:AQ + 384], 6), r8[:, 0:6].unsqueeze(2).to_broadcast([P, 6, 64]), ALU.mult))
                    ch.sync()
                    ch.done(dve.tensor_tensor(g3, a3, gains[:, :, :], ALU.mult))
                    ch.sync()
                    dve.sem_inc(s["u_used"], 1)
                    rope(ch, g3, t, 64, 6,
                         [(0, 4, st[:, ST_AQ:ST_AQ + 256].rearrange("p (b a c) -> p a b c", b=2, a=2)),
                          (4, 6, heads_of(st[:, ST_AK:ST_AK + 128], 2))])
                    ch.sync()
                    dve.sem_inc(s["st_ready"], 1)
                    dve.wait_ge(s["round_tr"], ROUNDS * g(t) + 3)
                    q3, k3 = heads_of(B7[:, 0:384], 4), heads_of(B7[:, 0:512], 4)
                    mq, mk = heads_of(st[:, ST_MQ:ST_MQ + 384], 4), heads_of(st[:, ST_MK:ST_MK + 384], 4)
                    ch.done(dve.tensor_copy(mq[:, :, 0:64], q3[:, :, 0:64]))
                    rope(ch, q3[:, :, 64:96], t, 32, 4, [(0, 4, mq[:, :, 64:96])])
                    ch.sync()
                    dve.sem_inc(s["round_evac"], 1)
                    dve.wait_ge(s["round_tr"], ROUNDS * g(t) + 4)
                    ch.done(dve.tensor_copy(mk[:, :, 0:64], k3[:, :, 0:64]))
                    ch.done(dve.tensor_copy(mk[:, :, 64:96], kper.unsqueeze(1).to_broadcast([P, 4, 32])))
                    ch.done(dve.tensor_copy(vals[:, span(t, 1), V_M:V_M + 256].rearrange("p o (h c) -> p (o h) c", h=4), k3[:, :, 64:128]))
                    ch.sync()
                    dve.sem_inc(s["round_evac"], 1)
                    dve.sem_inc(s["st_m_ready"], 1)
                    to_qk(t, 4, SL_AK, 4)
                    to_qk(t, 5, SL_AQ + 1, 3)
                    to_qk(t, 6, SL_MK, 4, 96)
                    to_qk(t, 7, SL_MQ, 4, 96)
                    assert ch.n == N_PREP, ch.n

                normalise(0)
                normalise(1)
                with dve.Fori(0, T - 2) as t:
                    prep(t)
                    normalise(t + 2)
                prep(T - 2)
                prep(T - 1)

                if stop == "P":
                    continue
                nt = T if l == 0 else TL
                gend = T * l + nt
                lam_init = 0.8 - 0.6 * math.exp(-0.3 * l)
                dve.wait_ge(s["lam_in"], 16 * 5 * (l + 1))
                ch = Count(dve, s["v_lam"], 6 * l)
                ch.done(dve.tensor_tensor_reduce(dtmp[:, 0:32], lamb[:, 0, :], lamb[:, 1, :], 1.0, 0.0, ALU.mult, ALU.add, nlam[:, 2:3]))
                ch.done(dve.tensor_tensor_reduce(dtmp[:, 32:64], lamb[:, 2, :], lamb[:, 3, :], 1.0, 0.0, ALU.mult, ALU.add, nlam[:, 3:4]))
                ch.done(dve.tensor_scalar(subg[:, :], subg[:, :], 1.0 - lam_init, None, ALU.mult))
                ch.sync()
                dve.sem_inc(s["lam_sum"], 1)
                dve.wait_ge(s["lam_exp"], l + 1)
                ch.done(dve.tensor_tensor(nlam[:, 2:3], nlam[:, 1:2], nlam[:, 0:1], ALU.subtract)).sync()
                ch.done(dve.tensor_scalar(nlam[:, 2:3], nlam[:, 2:3], -lam_init, None, ALU.add)).sync()
                N_O = 36

                def queries(t):
                    cols = span(t * P, P)
                    for m in range(4):
                        r = slice(32 * m, 32 * m + 32)
                        dst = Qs[r, 0:8, :].rearrange("p (a m) c -> p a m c", a=2)[:, :, m, :]
                        dve.tensor_scalar(dst, qk[r, SL_DQ:SL_DQ + 2, cols], 32 ** -0.5, None, ALU.mult)
                    for m in range(2):
                        r = slice(64 * m, 64 * m + 64)
                        dve.tensor_scalar(Qs[r, 8 + 2 * m:10 + 2 * m, :], qk[r, SL_AQ:SL_AQ + 2, cols], 64 ** -0.5, None, ALU.mult)
                        dst = Qs[r, 16:20, :].rearrange("p (a m) c -> p a m c", a=2)[:, :, m, :]
                        dve.tensor_scalar(dst, qk[r, SL_NQ:SL_NQ + 2, cols], 64 ** -0.5, None, ALU.mult)
                    dve.tensor_scalar(Qs[0:96, 12:16, :], qk[0:96, SL_MQ:SL_MQ + 4, cols], 96 ** -0.5, None,
                                      ALU.mult).then_inc(s["qs_ready"], 1)

                def att(t, nk, masked, last=False):
                    n0 = HEADS * g(t)
                    ch = Count(dve, s["v_o"], N_O * g(t))
                    for k in range(HEADS + 2):
                        if k < HEADS:
                            Sk = (S0, S1)[k % 2]
                            dve.wait_ge(s["scored"], n0 + k + 1)
                            if masked and k >= 16:
                                h = k - 16
                                bt = bias_t[:, h:h + 1, span((7 - 2 * t) * GRID_W, SEQ)]
                                ch.done(dve.tensor_tensor(Sk[:, 0:SEQ].unsqueeze(1), Sk[:, 0:SEQ].unsqueeze(1), bt, ALU.add)).sync()
                            dve.tensor_reduce(nmax[:, k:k + 1], Sk[:, 0:nk], AX.X, ALU.max, negate=True).then_inc(s["neg_max"], 1)
                        if 1 <= k <= HEADS:
                            u = k - 1
                            h = 4 if nk == NTOK else 1
                            dve.wait_ge(s["exp_done"], n0 + u + 3)
                            ch.done(dve.reciprocal(rinv[:, u:u + 1], rsum[:, u:u + 1]))
                            dve.wait_ge(s["p_tr"], n0 + u + 3)
                            dve.wait_ge(s["pv_done"], n0 + u + 1)
                            dve.tensor_copy(PTs[u % 2][:, 0:h, :].rearrange("p a b -> p (a b)"), PT[:, 0:h * P]).then_inc(s["pt_v"], 1)
                        if k == 2:
                            dve.wait_ge(s["ot_tr"], g(t))
                        if k >= 2:
                            u = k - 2
                            dve.wait_ge(s["pv_done"], n0 + u + 3)
                            ch.sync()
                            pv = (B6, B7)[u % 2][:, 0:64]
                            if u < 8 and u % 2 == 0:
                                dve.tensor_scalar(dtmp[:, 0:64], pv, rinv[:, u:u + 1], None, ALU.mult).then_inc(s["o_evac"], 1)
                            elif u < 8:
                                o = O[:, 512 + 32 * (u - 1):512 + 32 * (u - 1) + 64]
                                ch.done(dve.tensor_tensor(rinv[:, u:u + 1], rinv[:, u:u + 1], nlam[:, 2:3], ALU.mult)).sync()
                                dve.wait_ge(s["o_evac"], n0 + u + 2)
                                dve.scalar_tensor_tensor(o, pv, rinv[:, u:u + 1], dtmp[:, 0:64], ALU.mult, ALU.add).then_inc(s["o_evac"], 1)
                                dve.wait_ge(s["o_evac"], n0 + u + 3)
                                ins = dve.tensor_tensor_reduce(dtmp[:, 64:128], o, o, 1.0 / 64, 0.0, ALU.mult, ALU.add,
                                                               dstat[:, u // 2:u // 2 + 1])
                                if u == 7:
                                    ins.then_inc(s["d_stat"], 1)
                            else:
                                base = {2: 0, 3: 768, 4: 256}[u // 4]
                                dve.tensor_scalar(O[:, base + 64 * (u % 4):base + 64 * (u % 4) + 64], pv, rinv[:, u:u + 1], None,
                                                  ALU.mult).then_inc(s["o_evac"], 1)
                        if k == 14:
                            dve.wait_ge(s["d_rs"], g(t) + 1)
                            o4 = O[:, 512:768].rearrange("p (h c) -> p h c", h=4)
                            ch.done(dve.tensor_tensor(o4, o4, dstat[:, 4:8].unsqueeze(2).to_broadcast([P, 4, 64]), ALU.mult)).sync()
                            ch.done(dve.tensor_tensor(o4, o4, subg[:, :].unsqueeze(1).to_broadcast([P, 4, 64]), ALU.mult))
                    ch.sync()
                    dve.wait_ge(s["o_evac"], n0 + HEADS + 2)
                    dve.sem_inc(s["o_all"], 1)
                    dve.wait_ge(s["ot_tr"], g(t) + 1)
                    dve.tensor_copy(OT[:, 0:4, :].rearrange("p a b -> p (a b)"), PT[:, 0:512]).then_inc(s["ot_v"], 1)
                    if not last:
                        queries(t + 1)
                    v = 0 if masked else 3
                    dve.wait_ge(s["x1_stored"], 16 * g(t))
                    dve.wait_ge(s["h2_ready"], g(t))
                    for c in range(2):
                        dve.wait_ge(s["op_mm"], 2 * g(t) + c + 1)
                        dve.tensor_tensor(xb[:, c * 512:(c + 1) * 512], S1[:, c * 512:(c + 1) * 512], vec[:, v, c * 512:(c + 1) * 512],
                                          ALU.mult).then_inc(s["res_mul"], 1)
                    return ch.n

                dve.wait_ge(s["vec_in"], 16 * 6 * (l + 1))
                dve.wait_ge(s["bias_ready"], l + 1)
                dve.wait_ge(s["round_evac"], ROUNDS * T * (l + 1))
                ch.done(dve.memset(Qs, 0.0)).sync()
                queries(0)

                def att_counted(t, nk, masked, last=False):
                    n_ops = att(t, nk, masked, last)
                    assert n_ops <= N_O, n_ops
                    if n_ops < N_O:
                        dve.sem_inc(s["v_o"], N_O - n_ops)
                if l == 0:
                    with dve.Fori(0, TL) as t:
                        att_counted(t, NTOK, True)
                    with dve.Fori(TL, T - 1) as t:
                        att_counted(t, CTX, False)
                    att_counted(T - 1, CTX, False, True)
                else:
                    with dve.Fori(0, TL - 1) as t:
                        att_counted(t, NTOK, True)
                    att_counted(TL - 1, NTOK, True, True)
                if stop == "A":
                    continue

                def x_half(m, b):
                    return (hT2, XT)[m == "e_"][b][:, 0:4, :].rearrange("p a b -> p (a b)")

                def first_T(m, gi, b):
                    dve.wait_ge(s[m + "tr"], gi + 1)
                    dve.tensor_copy(x_half(m, b), PT[:, 0:512]).then_inc(s[m + "t_v"], 1)

                def ffn(m, gi, b, more):
                    ch = Count(dve, s["v_" + m[0]], 3 * gi)
                    G = (S0, S1)[b]
                    dve.wait_ge(s[m + "ex"], gi + 1)
                    ch.done(dve.tensor_scalar(gex[b], gex[b], 1.0, None, ALU.add)).sync()
                    ch.done(dve.reciprocal(gex[b], gex[b])).sync()
                    ch.done(dve.tensor_tensor(gex[b], G[:, 0:DE], gex[b], ALU.mult)).sync()
                    dve.wait_ge(s[m + "u"], gi + 1)
                    dve.tensor_tensor(hid[b], G[:, 512:512 + DE], gex[b], ALU.mult).then_inc(s[m + "hid"], 1)
                    if more:
                        dve.wait_ge(s[m + "tr"], gi + 2)
                        dve.tensor_copy(x_half(m, 1 - b), PT[:, 0:512]).then_inc(s[m + "t_v"], 1)
                    dve.wait_ge(s[m + "ht"], gi + 1)
                    dve.tensor_copy(hidT[b].rearrange("p a b -> p (a b)"), B7[:, 0:256]).then_inc(s[m + "htv"], 1)
                    dve.wait_ge(s[m + "d"], gi + 1)

                def s_block(t, u, b, more, first, stream):
                    dve.wait_ge(s["s_rt"], g(t) + 1)
                    dve.tensor_copy(lg[:, span(t, 1), :], B6[:, 0:NE].unsqueeze(1)).then_inc(s["s_lg"], 1)
                    ffn("s_", g(t), b, more)
                    if not first:
                        dve.wait_ge(s[f"s_stored{b}"], 16 * (u + T // 2 * l))
                    dve.tensor_tensor(ob[b], (S0, S1)[b][:, :], g2[:, stream, :], ALU.mult).then_inc(s["s_ob"], 1)

                first_T("s_", g(0), 0)
                for b in range(2):
                    s_block(b, 0, b, True, l == 0, 0)
                if l == 0:
                    for b in range(2):
                        s_block(2 + b, 1, b, True, False, 0)
                    for b in range(2):
                        s_block(4 + b, 2, b, b == 0, False, 1)
                else:
                    for b in range(2):
                        s_block(2 + b, 1, b, b == 0, False, 0)

                ch = Count(dve, s["v_r"], R_START[0])
                row = lambda a: a.rearrange("p a b -> p (a b)")
                sc_, sel_ = score[:, 0:nt, :], selb[:, 0:nt, :]
                step = lambda ins: ch.done(ins).sync()
                dve.wait_ge(s["r_exp"], l + 1)
                step(dve.tensor_scalar(sc_, sc_, 1.0, None, ALU.add))
                step(dve.reciprocal(sc_, sc_))
                step(dve.tensor_tensor(sel_, sc_, rb.unsqueeze(1).to_broadcast([P, nt, NE]), ALU.add))
                q = row(sel_).rearrange("p (a b) -> p a b", b=4)
                ng = nt * NG
                pr = lambda n: pair[:, n, 0:ng]
                ch.done(dve.tensor_tensor(pr(0), q[:, :, 0], q[:, :, 1], ALU.max))
                ch.done(dve.tensor_tensor(pr(1), q[:, :, 2], q[:, :, 3], ALU.max))
                ch.done(dve.tensor_tensor(pr(2), q[:, :, 0], q[:, :, 1], ALU.min))
                ch.done(dve.tensor_tensor(pr(3), q[:, :, 2], q[:, :, 3], ALU.min)).sync()
                step(dve.tensor_tensor(pr(3), pr(2), pr(3), ALU.max))
                step(dve.tensor_tensor(pr(4), pr(0), pr(1), ALU.min))
                step(dve.tensor_tensor(pr(3), pr(3), pr(4), ALU.max))
                step(dve.tensor_tensor(pr(0), pr(0), pr(1), ALU.max))
                ch.done(dve.memset(gs8[:, 0:nt, 4:8], -BIG))
                step(dve.tensor_tensor(gs8[:, 0:nt, 0:4], pr(0).rearrange("p (a b) -> p a b", b=4), pr(3).rearrange("p (a b) -> p a b", b=4), ALU.add))

                def best(src):
                    for t in range(nt):
                        ch.done(dve.max(mx8[:, t, :], src[:, t, :]))
                    ch.sync()
                    for t in range(nt):
                        ch.done(dve.max_index(ix8[:, t, :], mx8[:, t, :], src[:, t, :]))
                    ch.sync()
                best(gs8)
                step(dve.tensor_copy(gidx[:, 0:nt].unsqueeze(2), ix8[:, 0:nt, 0:1]))
                grp = C("group_of").unsqueeze(1).to_broadcast([P, nt, NE])
                step(dve.tensor_tensor(tmp16[:, 0:nt, :], grp, gidx[:, 0:nt].unsqueeze(2).to_broadcast([P, nt, NE]), ALU.is_equal))
                step(dve.tensor_scalar(tmp16[:, 0:nt, :], tmp16[:, 0:nt, :], 1.0, BIG, ALU.subtract, ALU.mult))
                step(dve.tensor_tensor(sel_, sel_, tmp16[:, 0:nt, :], ALU.add))
                best(selb)
                step(dve.tensor_copy(eidx[:, 0:nt, :], ix8[:, 0:nt, 0:TOPK]))
                exi = C("expert").unsqueeze(1).to_broadcast([P, nt, NE])
                ohs = (oh0, oh1)
                for j in range(TOPK):
                    ch.done(dve.tensor_tensor(ohs[j][:, 0:nt, :], exi, eidx[:, 0:nt, j:j + 1].to_broadcast([P, nt, NE]), ALU.is_equal))
                ch.sync()
                dve.tensor_tensor(both[:, 0:nt, :], oh0[:, 0:nt, :], oh1[:, 0:nt, :], ALU.add).then_inc(s["r_mat"], 1)
                for j in range(TOPK):
                    step(dve.tensor_tensor(tmp16[:, 0:nt, :], sc_, ohs[j][:, 0:nt, :], ALU.mult))
                    step(dve.tensor_reduce(wts[:, 0:nt, j], tmp16[:, 0:nt, :], AX.X, ALU.add))
                step(dve.tensor_reduce(wsum[:, 0:nt], wts[:, 0:nt, :], AX.X, ALU.add))
                step(dve.reciprocal(wsum[:, 0:nt], wsum[:, 0:nt]))
                step(dve.tensor_tensor(wts[:, 0:nt, :], wts[:, 0:nt, :], wsum[:, 0:nt].unsqueeze(2).to_broadcast([P, nt, TOPK]), ALU.mult))
                dve.wait_ge(s["r_cum"], l + 1)
                ch.done(dve.memset(offs[:, 0, :], 0.0))
                step(dve.tensor_copy(row(tots[:, 0:nt, :]), B7[:, 0:nt * NE]))
                for t in range(1, nt):
                    step(dve.tensor_tensor(offs[:, t, :], offs[:, t - 1, :], tots[:, t - 1, :], ALU.add))
                step(dve.tensor_tensor(count_e, offs[:, nt - 1, :], tots[:, nt - 1, :], ALU.add))
                step(dve.tensor_tensor(cmp6[:, :, 0:nt], count_e.unsqueeze(2).to_broadcast([P, NE, nt]),
                                       C("tile_start")[:, 0:nt].unsqueeze(1).to_broadcast([P, NE, nt]), ALU.is_gt))
                step(dve.tensor_reduce(nblk, cmp6[:, :, 0:nt], AX.X, ALU.add))
                step(dve.tensor_tensor_scan(bend, ones[:, 0:NE], nblk, 0.0, ALU.mult, ALU.add))
                step(dve.tensor_tensor(bbase, bend, nblk, ALU.subtract))
                step(dve.tensor_scalar(bbase, bbase, float(P), None, ALU.mult))
                step(dve.tensor_tensor(row(posn[:, 0:nt, :]), B6[:, 0:nt * NE], row(offs[:, 0:nt, :]), ALU.add))
                step(dve.tensor_tensor(posn[:, 0:nt, :], posn[:, 0:nt, :], bbase.unsqueeze(1).to_broadcast([P, nt, NE]), ALU.add))
                for j in range(TOPK):
                    step(dve.tensor_tensor(tmp16[:, 0:nt, :], posn[:, 0:nt, :], ohs[j][:, 0:nt, :], ALU.mult))
                    step(dve.tensor_reduce(slotf[:, 0:nt, j], tmp16[:, 0:nt, :], AX.X, ALU.add))
                ch.done(dve.tensor_copy(tok_u, C("token")))
                step(dve.tensor_copy(slots[:, 0:nt, :], slotf[:, 0:nt, :]))
                dve.sem_inc(s["r_slots"], 1)
                nb = NBK[l]
                step(dve.tensor_tensor(cmpb[:, 0:nb, :], bend.unsqueeze(1).to_broadcast([P, nb, NE]),
                                       C("block")[:, 0:nb].unsqueeze(2).to_broadcast([P, nb, NE]), ALU.is_le))
                step(dve.tensor_reduce(bexp[:, 0:nb], cmpb[:, 0:nb, :], AX.X, ALU.add))
                step(dve.tensor_scalar(bexp[:, 0:nb], bexp[:, 0:nb], float(NE - 1), None, ALU.min))
                step(dve.tensor_copy(bexp_i[:, 0:nb], bexp[:, 0:nb]))
                dve.sem_inc(s["r_ready"], 1)
                R_START[0] += ch.n
                ge = lambda b: b + NBK[0] * l
                first_T("e_", ge(0), 0)

                def e_block(blk, u, b, more, first):
                    ffn("e_", ge(blk), b, more)
                    if not first:
                        dve.wait_ge(s[f"e_stored{b}"], 16 * (u + NBK[0] // 2 * l))
                    dve.tensor_copy(yb[b][:, 0:512], (S0, S1)[b][:, 0:512]).then_inc(s["e_y_v"], 1)

                for b in range(2):
                    e_block(b, 0, b, True, l == 0)
                with dve.Fori(1, nb // 2 - 1) as i:
                    for b in range(2):
                        e_block(2 * i + b, i, b, True, False)
                for b in range(2):
                    e_block(nb - 2 + b, nb // 2 - 1, b, b == 0, False)
                def c_tile(t, u, b, stream, first):
                    ch = Count(dve, s["v_c"], 3 * g(t))
                    dve.wait_ge(s[f"c_y_in{b}"], 16 * TOPK * (u + 1 + T // 2 * l))
                    w = lambda j: wts[:, span(t, 1), j]
                    y1, y2 = y12[b][:, 0, :], y12[b][:, 1, :]
                    ch.done(dve.tensor_scalar(y1, y1, w(0), None, ALU.mult)).sync()
                    ch.done(dve.scalar_tensor_tensor(y1, y2, w(1), y1, ALU.mult, ALU.add)).sync()
                    ch.done(dve.tensor_tensor(y1, y1, g2[:, stream, :], ALU.mult)).sync()
                    assert ch.n == 3
                    dve.wait_ge(s[f"c_x_in{b}"], 16 * (u + 1 + T // 2 * l))
                    if not first:
                        dve.wait_ge(s[f"c_stored{b}"], 16 * (u + T // 2 * l))
                    if l < DEPTH - 1:
                        dve.tensor_tensor(x3b[b], y1, x2b[b], ALU.add).then_inc(s["c_x3"], 1)
                    else:
                        dve.tensor_tensor(x3b[b], y1, x2b[b], ALU.add).then_inc(c_sum, 1)
                        dve.wait_ge(s["c_rs"], t + 1)
                        dve.scalar_tensor_tensor(x3b[b], x3b[b], h2s[:, 3:4], fgain, ALU.mult, ALU.mult).then_inc(s["c_x3"], 1)
                if l < DEPTH - 1:
                    for b in range(2):
                        c_tile(b, 0, b, 0, True)
                    for t in range(2, nt):
                        c_tile(t, t // 2, t % 2, int(t >= TL), False)
                else:
                    dve.wait_ge(fgain_in, 16)
                    for t in range(nt):
                        c_tile(t, t // 2, t % 2, 0, False)


_INS = ["x", "c", "ctx", "c_ctx", "w_mod", "b_mod", "norm_mix", "norm_ffn", "w_in", "w_out",
        "gqa_q_norm", "gqa_k_norm", "na_rel_bias", "diff_lq1", "diff_lk1", "diff_lq2", "diff_lk2", "diff_subln",
        "mla_q_norm", "mla_w_q_up", "mla_kv_norm", "mla_w_kv_up", "router_w", "router_b",
        "moe_w_gate", "moe_w_up", "moe_w_down", "shared_w_gate", "shared_w_up", "shared_w_down", "final_norm"]


def kernel(**inputs):
    import concourse.bacc as bacc
    from concourse.bass_utils import run_bass_kernel_spmd

    nc = bacc.Bacc("TRN2", target_bir_lowering=False, num_devices=1)
    arrays, A = {}, {}
    for name in _INS:
        a = np.ascontiguousarray(inputs[name])
        arrays[f"in_{name}"] = a
        A[name] = nc.dram_tensor(f"in_{name}", a.shape, mybir.dt.from_np(a.dtype), kind="ExternalInput").ap()
    out = nc.dram_tensor("out", (1, SEQ, D), F32, kind="ExternalOutput").ap()
    program(nc, A, out)
    return run_bass_kernel_spmd(nc, [arrays], core_ids=[0]).results[0]["out"]
```

```python
import math
from contextlib import ExitStack

import numpy as np
import concourse.bass as bass
from concourse import mybir

ALU = mybir.AluOpType
ACT = mybir.ActivationFunctionType
AX = mybir.AxisListType
F32 = mybir.dt.float32
BF16 = mybir.dt.bfloat16
I32 = mybir.dt.int32
U32 = mybir.dt.uint32

P = 128
D = 1024
DEPTH = 2
SEQ = 512
CTX = 256
NTOK = SEQ + CTX
T = NTOK // P
TL = SEQ // P
TC = CTX // P
KT = D // P
GRID_W = 64
GRID_H = SEQ // GRID_W
EPS = 1e-6
IN_COLS = 2400
UCH = 480
NCH = IN_COLS // UCH
MCH = 512
NMCH = 6 * D // MCH
NE = 16
NG = 4
DE = 256
BIG = 1e30
TOPK = 2
NBK = [-(-((TOPK * n + NE * (P - 1)) // P) // 2) * 2 for n in (NTOK, SEQ)]
HEADS = 20

AQ, AK, AV, NQ, NK_, NV, DQ, DK, DV, CQ, CKV, KPE = (
    0, 256, 384, 512, 768, 1024, 1280, 1536, 1792, 2048, 2240, 2368)
ST_AK, ST_DK, ST_AQ, ST_DQ, ST_MK, ST_MQ, ST_W = 0, 128, 384, 640, 896, 1280, 1664
SL_NK, SL_NQ, SL_AK, SL_DK, SL_AQ, SL_DQ, SL_MK, SL_MQ, NSL = 0, 2, 4, 5, 7, 9, 11, 15, 19
V_A, V_N, V_D, V_M, V_W = 0, 128, 384, 640, 896
PROD = {1: 0, 3: 1, 5: 2, 7: 3, **{m: m - 4 for m in range(8, HEADS)}}
NP = len(PROD)
ROUNDS = 8


def constants():
    parts, at = [], {}
    width = 0

    def add(name, a):
        nonlocal width
        a = np.asarray(a, np.float32).reshape(P, -1)
        at[name] = (width, width + a.shape[1])
        parts.append(a)
        width += a.shape[1]

    p = np.arange(P)
    add("ident", np.eye(P))
    add("ones", np.ones((P, P)))
    add("before", p[:, None] < p[None, :])
    for rot, heads in ((64, "64"), (32, "32")):
        half = rot // 2
        freqs = (np.float32(10000.0) ** (-np.arange(0, half, 2, dtype=np.float32) / np.float32(half))).astype(np.float32)
        cos = np.ones((NTOK, rot), np.float32)
        sin = np.zeros((NTOK, rot), np.float32)
        tok = np.arange(SEQ)
        for a, place in enumerate((tok // GRID_W, tok % GRID_W)):
            ang = place.astype(np.float32)[:, None] * freqs
            n = freqs.size
            o = a * half
            cos[:SEQ, o:o + n] = cos[:SEQ, o + n:o + 2 * n] = np.cos(ang)
            sin[:SEQ, o:o + n] = -np.sin(ang)
            sin[:SEQ, o + n:o + 2 * n] = np.sin(ang)
        add("cos" + heads, cos.reshape(T, P, rot).transpose(1, 0, 2))
        add("sin" + heads, sin.reshape(T, P, rot).transpose(1, 0, 2))
    col = p % GRID_W
    lo = np.clip(col - 8, 0, GRID_W - 16)[:, None]
    keys = np.arange(GRID_W)[None, :]
    add("window", np.where((keys >= lo) & (keys < lo + 16), 0.0, -BIG))
    add("pick", (p[:, None] % 32) == np.arange(2)[None, :])
    add("expert", np.broadcast_to(np.arange(NE), (P, NE)))
    add("group_of", np.broadcast_to(np.arange(NE) // (NE // NG), (P, NE)))
    add("block", np.broadcast_to(np.arange(NBK[0] + 1), (P, NBK[0] + 1)))
    add("tile_start", np.broadcast_to(P * np.arange(T), (P, T)))
    add("token", np.arange(T)[None, :] * P + p[:, None])
    return np.concatenate(parts, 1), at


def span(start, size):
    return slice(start, start + size) if isinstance(start, int) else bass.ds(start, size)


class Count:

    def __init__(self, eng, sem, start):
        self.eng, self.sem, self.start, self.n = eng, sem, start, 0

    def done(self, ins):
        ins.then_inc(self.sem, 1)
        self.n += 1
        return self

    def sync(self):
        self.eng.wait_ge(self.sem, self.start + self.n)


def program(nc, A, out, stop=None):
    table, at = constants()
    cst_d = nc.inline_tensor(table, name="shape_constants").ap()
    dram = lambda n, s, d=F32: nc.dram_tensor(n, s, d, kind="Internal").ap()
    x_in = [dram(f"x_in{l}", (NTOK, D)) for l in range(DEPTH)]
    x_mix = [dram(f"x_mix{l}", ((NTOK, SEQ)[l], D)) for l in range(DEPTH)]
    h2_d = [dram(f"h2_{l}", ((NTOK, SEQ)[l], D)) for l in range(DEPTH)]
    x_ffn = [dram(f"x_ffn{l}", ((NTOK, SEQ)[l], D)) for l in range(DEPTH)]
    y_d = [dram(f"y{l}", (NBK[l] * P, D)) for l in range(DEPTH)]
    slot_tok = [dram(f"slot_tok{l}", ((NBK[l] + 1) * P, 1), U32) for l in range(DEPTH)]
    REL_ROW = DEPTH * P
    REL_COPY = (4 * 15 + 2) * REL_ROW
    rel_d = dram("rel_padded", (1, REL_COPY))
    rel_copies = dram("rel_copies", (GRID_W, REL_COPY))
    mod_d = [dram(f"mod{l}", (2, 6 * D)) for l in range(DEPTH)]

    with ExitStack() as ctx:
        sb = lambda n, s, d=F32: ctx.enter_context(nc.sbuf_tensor(n, s, d))
        pb = lambda n, s: ctx.enter_context(nc.psum_tensor(n, s, F32))
        sem = lambda n: ctx.enter_context(nc.semaphore(n))

        cst = sb("cst", [P, table.shape[1]])
        C = lambda n: cst[:, at[n][0]:at[n][1]]
        ident, ones = C("ident"), C("ones")
        cos = {64: C("cos64").rearrange("p (t c) -> p t c", t=T), 32: C("cos32").rearrange("p (t c) -> p t c", t=T)}
        sin = {64: C("sin64").rearrange("p (t c) -> p t c", t=T), 32: C("sin32").rearrange("p (t c) -> p t c", t=T)}
        csrc = sb("csrc", [P, 2, KT])
        ctmp = sb("ctmp", [P, 2, KT])
        cs = sb("cs", [P, KT, 32])
        modcol = sb("modcol", [P, T, 2, KT])
        gains = sb("gains", [P, 6, 64])
        lgain = sb("lgain", [P, 320])
        sumsq = sb("sumsq", [P, 2])
        meansq = sb("meansq", [P, 2])
        rstd = sb("rstd", [P, 2])
        s8 = sb("s8", [P, 8])
        m8 = sb("m8", [P, 8])
        r8 = sb("r8", [P, 8])
        halfs = sb("halfs", [P, 24])
        inv8, eps8 = halfs[:, 8:16], halfs[:, 16:24]
        nmax = sb("nmax", [P, HEADS])
        rsum = sb("rsum", [P, HEADS])
        rinv = sb("rinv", [P, HEADS])
        nlam = sb("nlam", [P, 4])
        dtmp = sb("dtmp", [P, 128])
        dstat = sb("dstat", [P, 8])
        ratio = sb("ratio", [P, 4])
        subg = sb("subg", [P, 64])
        h2s = sb("h2s", [P, 4])

        ARENA = 49928
        arena = sb("arena", [P, ARENA])

        def region(start):
            at_ = [start]

            def take(*shape, parts=P, dt=None):
                n = int(np.prod(shape))
                a = arena[0:parts, at_[0]:at_[0] + n]
                at_[0] += n
                assert at_[0] <= ARENA, (shape, at_[0])
                if len(shape) == 2:
                    a = a.rearrange("p (a b) -> p a b", a=shape[0])
                return a
            take.at = at_
            return take

        take = region(0)
        win = take(KT, IN_COLS)
        WIN_END = take.at[0]
        qk = take(NSL, NTOK)
        vals = take(T, V_W)
        QKV_END = take.at[0]
        U = take(IN_COLS)
        st = take(ST_W)
        xt = take(D)
        junk = take(D // 2).bitcast(BF16)
        hT = [take(KT, P) for _ in range(2)]
        tmpA, tmpB = take(512), take(512)
        lor = take(320)
        lorT = take(3, P)
        wqu = take(2, 384)
        wkvu = take(512)
        kper = take(32)
        take = region(WIN_END)
        wm = [take(KT, MCH) for _ in range(2)]
        part = [take(MCH) for _ in range(2)]
        modrow = take(6 * D, parts=2)
        brow = take(6 * D, parts=2)
        nrow = take(2, D, parts=2)

        relpad = arena[0:62, 45000:45000 + DEPTH * P]
        zeros_u = arena[:, 45400:45400 + NBK[0] + 1].bitcast(U32)
        take = region(0)
        wout = take(KT, D)
        vec = take(6, D)
        bias_t = take(4, 16 * GRID_W)
        Pb = [take(NTOK)]
        assert take.at[0] <= WIN_END
        take = region(QKV_END)
        Qs = take(HEADS, P)
        Pb += [take(NTOK) for _ in range(2)]
        PTs = [take(T, P) for _ in range(2)]
        O = take(D)
        OT = take(KT, P)
        xa, xb, h2b = take(D), take(D), take(D)
        lamb = O[:, 0:128].rearrange("p (a b) -> p a b", a=4)
        take = region(WIN_END)
        swgu = take(KT, 512)
        swd = take(2, D)
        hs = [take(D) for _ in range(2)]
        hT2 = [take(KT, P) for _ in range(2)]
        gex = [take(DE) for _ in range(2)]
        hid = [take(DE) for _ in range(2)]
        hidT = [take(2, P) for _ in range(2)]
        x1b = [take(D) for _ in range(2)]
        ob = [take(D) for _ in range(2)]
        g2 = take(2, D)
        rw = take(KT, NE)
        rb = take(NE)
        take = region(take.at[0])
        wgu = [take(2, KT * DE) for _ in range(2)]
        wdn = [take(2, D) for _ in range(2)]
        take = region(0)
        xg = [take(D) for _ in range(2)]
        XT = [take(KT, P) for _ in range(2)]
        yb = [take(D) for _ in range(2)]
        y12 = [take(2, D) for _ in range(2)]
        x2b = [take(D) for _ in range(2)]
        x3b = [take(D) for _ in range(2)]
        fgain = take(D)
        lg = take(T, NE)
        score, selb, oh0, oh1, both, tmp16, tots, offs, posn = [take(T, NE) for _ in range(9)]
        gs8, mx8 = take(T, 8), take(T, 8)
        ix8 = take(T, 8).bitcast(U32)
        pair = take(5, T * NG)
        gidx = take(T)
        eidx = take(T, 2)
        wts = take(T, 2)
        wsum = take(T)
        slotf = take(T, 2)
        slots = take(T, 2).bitcast(U32)
        nblk, bend, bbase, count_e = take(NE), take(NE), take(NE), take(NE)
        cmp6 = take(NE, T)
        cmpb = take(NBK[0] + 1, NE)
        bexp = take(NBK[0] + 1)
        bexp_i = take(NBK[0] + 1).bitcast(I32)
        npair_f = take(3)
        npair_i = take(3).bitcast(I32)
        tok_u = take(T).bitcast(U32)
        table_u = take(NBK[0] + 1).bitcast(U32)
        idx1 = [take(1).bitcast(U32) for _ in range(2)]
        idx2 = [take(2).bitcast(U32) for _ in range(2)]
        assert take.at[0] <= WIN_END, take.at[0]

        S0, S1, PT = pb("S0", [P, 1024]), pb("S1", [P, 1024]), pb("PT", [P, 1024])
        B6, B7 = pb("B6", [P, 512]), pb("B7", [P, 512])
        ubank = [S0[:, 0:512], S0[:, 512:1024], S1[:, 0:512], S1[:, 512:1024], B6[:, :]]

        consts_in, inputs_copied, cond_in = sem("consts_in"), sem("inputs_copied"), sem("cond_in")
        exp_c, cs_ready = sem("exp_c"), sem("cs_ready")
        halfs_set = sem("halfs_set")
        relpad_set, relpad_in, rel_stored, zeros_stored, fgain_in = (
            sem("relpad_set"), sem("relpad_in"), sem("rel_stored"), sem("zeros_stored"), sem("fgain_in"))
        c_sum = sem("c_sum")
        UNITS = ["exp_done", "p_tr", "pt_v", "pt_s", "pv_done", "o_evac"]
        v_init = sem("v_init")
        NAMES = ["mod_w_in0", "mod_w_in1", "mod_rows_in", "mod_mm", "mod_part", "mod_sel", "mod_row", "mod_gain", "mod_stored",
                 "modcol_in", "wsmall_in", "x_in", "ssq", "rstd_ready", "xn_done", "hT_tr", "hT_evac", "u_mm", "u_evac",
                 "v_copied", "u_used", "stats", "r8_ready", "lor_ready", "st_ready", "st_m_ready", "round_tr", "round_evac",
                 "v_prep", "g_prep", "mean_x",
                 "bias_in", "lam_in", "bias_ready", "wout_in", "vec_in", "lam_sum", "lam_exp", "lam_ready", "v_lam",
                 "xa_in", "qs_ready", "scored", "neg_max", "exp_done", "p_tr", "pt_v", "pt_s", "pv_done", "o_evac", "v_bias",
                 "v_o", "d_stat", "d_rs", "g_att", "o_all", "ot_tr", "ot_v", "ot_s", "op_mm", "res_mul", "x1_ready", "x1_sq",
                 "h2_ready", "x1_stored", "h2_stored",
                 "s_w_in", "hs_in0", "hs_in1", "x1_in0", "x1_in1", "s_tr", "s_t_v", "s_t_s", "s_rt", "s_lg", "s_g", "s_u", "s_ex",
                 "v_s", "s_hid", "s_ht", "s_htv", "s_d", "s_ob", "s_x2", "s_stored0", "s_stored1",
                 "r_exp", "v_r", "r_mat", "r_cum", "r_slots", "r_scat", "comb_done", "g_x", "r_tab", "r_ready",
                 "e_w_in0", "e_w_in1", "e_idx", "spare_seen", "e_filled", "e_tr", "e_t_v", "e_t_s", "e_g", "e_u", "e_ex", "v_e",
                 "e_hid", "e_ht", "e_htv", "e_d", "e_y_v", "e_y_s", "e_stored0", "e_stored1",
                 "c_idx", "idx_seen", "c_y_in0", "c_y_in1", "c_x_in0", "c_x_in1", "v_c", "c_x3", "c_stored0", "c_stored1", "c_sq", "c_mean",
                 "c_rs"]
        s = {n: sem(n) for n in NAMES}
        e_x_in = [[sem(f"e_x_in{b}_{l}") for b in range(2)] for l in range(DEPTH)]
        s["win_in"] = [sem(f"win_in{c}") for c in range(NCH)]

        def over_tiles(eng, l, att):
            att(0, NTOK, None, False)
            with eng.Fori(1, TL if l == 0 else TL - 1) as t:
                att(t, NTOK, NTOK, False)
            if l == 0:
                att(TL, CTX, NTOK, False)
                for t in range(TL + 1, T):
                    att(t, CTX, CTX, t == T - 1)
                att(T, None, CTX, False)
            else:
                att(TL - 1, NTOK, NTOK, True)
                att(TL, None, NTOK, False)

        def pair_counts(eng, l):
            eng.wait_ge(s["r_ready"], l + 1)
            least = TOPK * (NTOK, SEQ)[l] // P // 2
            return [eng.value_load(npair_i[0:1, n:n + 1], min_val=least - n, max_val=NBK[l] // 2 - n) for n in range(3)]

        def spare_pairs(eng, l, pairs, counts):
            eng.sem_inc(s["spare_seen"], 1)
            with eng.Fori(pairs, NBK[l] // 2):
                for name, n in counts:
                    eng.sem_inc(s[name], n)

        def product_at(k, lag, nk, prev):
            m = k - lag
            if m < 0 and prev:
                return PROD[HEADS + m] - NP, HEADS + m, prev
            if m >= 0 and nk and m in PROD:
                return PROD[m], m, nk
            return None

        block = ctx.enter_context(nc.Block())

        @block.sync
        def _(sp):
            sp.dma_start(cst[:, :], cst_d).then_inc(consts_in, 16)
            sp.dma_start(csrc[:, 0, :], A["c"].rearrange("a (p k) -> (a p) k", k=KT)).then_inc(cond_in, 16)
            sp.dma_start(csrc[:, 1, :], A["c_ctx"].rearrange("(p k) -> p k", k=KT)).then_inc(cond_in, 16)
            sp.dma_start(x_in[0][0:SEQ, :], A["x"][0]).then_inc(inputs_copied, 16)
            sp.dma_start(x_in[0][SEQ:NTOK, :], A["ctx"][0]).then_inc(inputs_copied, 16)
            sp.wait_ge(relpad_set, 2)
            for l in range(DEPTH):
                sp.dma_start(relpad[1:61, l * P + 48:l * P + 79], A["na_rel_bias"][l].rearrange("h a b -> (h a) b")).then_inc(relpad_in, 16)
                sp.dma_start(slot_tok[l].rearrange("(p b) o -> p (b o)", p=P), zeros_u[:, 0:NBK[l] + 1]).then_inc(zeros_stored, 16)
            sp.wait_ge(relpad_in, 16 * DEPTH)
            sp.dma_start(rel_d.rearrange("o (a c) -> (o a) c", c=REL_ROW), relpad).then_inc(rel_stored, 16)
            for u in range(2):
                for n in UNITS:
                    sp.sem_inc(s[n], 1)
            for l in range(1 if stop in ("P", "A") else DEPTH):
                g = lambda t: t + T * l
                wmod = A["w_mod"][l].rearrange("(p k) n -> p k n", k=KT)

                def mod_load(i, first):
                    for b in range(2):
                        if not first:
                            sp.wait_ge(s["mod_mm"], 2 * i + b - 1 + NMCH * l)
                        sp.dma_start(wm[b], wmod[:, :, span((2 * i + b) * MCH, MCH)]).then_inc(s[f"mod_w_in{b}"], 16)
                for r in range(2):
                    sp.dma_start(brow[r:r + 1, :], A["b_mod"][l:l + 1, :]).then_inc(s["mod_rows_in"], 16)
                    sp.dma_start(nrow[r:r + 1, 0, :], A["norm_mix"][l:l + 1, :]).then_inc(s["mod_rows_in"], 16)
                    sp.dma_start(nrow[r:r + 1, 1, :], A["norm_ffn"][l:l + 1, :]).then_inc(s["mod_rows_in"], 16)
                mod_load(0, True)
                with sp.Fori(1, NMCH // 2) as i:
                    mod_load(i, False)
                win_d = A["w_in"][l].rearrange("(p k) n -> p k n", k=KT)
                for c in range(NCH):
                    sp.dma_start(win[:, :, c * UCH:(c + 1) * UCH], win_d[:, :, c * UCH:(c + 1) * UCH]).then_inc(s["win_in"][c], 16)
                sp.wait_ge(s["mod_gain"], 2 * (l + 1))
                sp.dma_start(mod_d[l], modrow).then_inc(s["mod_stored"], 16)
                sp.wait_ge(s["mod_stored"], 16 * (l + 1))
                for t in range(T):
                    src = mod_d[l][int(t >= TL), 0:2 * D].rearrange("(w p k) -> p w k", w=2, k=KT)
                    sp.dma_start(modcol[:, t], src).then_inc(s["modcol_in"], 16)
                small = 0
                for h in range(6):
                    gain = A["gqa_q_norm"] if h < 4 else A["gqa_k_norm"]
                    sp.dma_start(gains[:, h, :], gain[l].partition_broadcast(P)).then_inc(s["wsmall_in"], 16)
                sp.dma_start(lgain[:, 0:192], A["mla_q_norm"][l].partition_broadcast(P)).then_inc(s["wsmall_in"], 16)
                sp.dma_start(lgain[:, 192:320], A["mla_kv_norm"][l].partition_broadcast(P)).then_inc(s["wsmall_in"], 16)
                sp.dma_start(wqu[0:96], A["mla_w_q_up"][l].rearrange("(k p) n -> p k n", p=96)).then_inc(s["wsmall_in"], 16)
                sp.dma_start(wkvu, A["mla_w_kv_up"][l]).then_inc(s["wsmall_in"], 16)
                if l == 0:
                    sp.wait_ge(inputs_copied, 32)

                def x_load(t, first):
                    if not first:
                        sp.wait_ge(s["hT_tr"], g(t))
                    sp.dma_start(xt, x_in[l][span(t * P, P), :]).then_inc(s["x_in"], 16)
                x_load(0, True)
                if l == 0:
                    sp.wait_ge(rel_stored, 16)
                    sp.dma_start(rel_copies, rel_d[0].partition_broadcast(GRID_W)).then_inc(rel_stored, 16)
                with sp.Fori(1, T) as t:
                    x_load(t, False)

                if stop == "P":
                    continue
                sp.wait_ge(s["u_mm"], NCH * T * (l + 1))
                if l == 0:
                    sp.wait_ge(rel_stored, 32)
                for h in range(4):
                    for r2 in range(2):
                        src = bass.AP(rel_copies.tensor, (1 + h * 15 - r2) * REL_ROW + l * P + GRID_W - 1,
                                      [[REL_COPY - 1, GRID_W], [REL_ROW, 16], [1, GRID_W]])
                        dst = bias_t[r2 * GRID_W:(r2 + 1) * GRID_W, h, :]
                        sp.dma_start(dst.rearrange("p (j c) -> p j c", c=GRID_W), src).then_inc(s["bias_in"], 16)
                sp.dma_start(wout, A["w_out"][l].rearrange("(p k) n -> p k n", k=KT)).then_inc(s["wout_in"], 16)
                for stream in range(2):
                    for n, w in enumerate((2, 4, 3)):
                        sp.dma_start(vec[:, 3 * stream + n, :], mod_d[l][stream, w * D:(w + 1) * D].partition_broadcast(P)).then_inc(s["vec_in"], 16)
                sp.wait_ge(s["round_evac"], ROUNDS * T * (l + 1))
                for n, w in enumerate(("diff_lq1", "diff_lk1", "diff_lq2", "diff_lk2")):
                    sp.dma_start(lamb[:, n, :], A[w][l].partition_broadcast(P)).then_inc(s["lam_in"], 16)
                sp.dma_start(subg[:, :], A["diff_subln"][l].partition_broadcast(P)).then_inc(s["lam_in"], 16)

                def att_rows(t, first):
                    rows = span(t * P, P)
                    if not first:
                        sp.wait_ge(s["x1_ready"], g(t))
                    sp.dma_start(xa, x_in[l][rows, :]).then_inc(s["xa_in"], 16)
                    sp.wait_ge(s["x1_ready"], g(t) + 1)
                    sp.dma_start(x_mix[l][rows, :], xb).then_inc(s["x1_stored"], 16)
                    sp.wait_ge(s["h2_ready"], g(t) + 1)
                    sp.dma_start(h2_d[l][rows, :], h2b).then_inc(s["h2_stored"], 16)

                att_rows(0, l == 0)
                with sp.Fori(1, T if l == 0 else TL) as t:
                    att_rows(t, False)
                if stop == "A":
                    continue
                nt = T if l == 0 else TL
                gend = T * l + nt
                sp.wait_ge(s["pv_done"], NP * gend + 2)
                for w, (name, e0) in enumerate((("shared_w_gate", 0), ("shared_w_up", DE))):
                    sp.dma_start(swgu[:, :, e0:e0 + DE], A[name][l].rearrange("(p k) n -> p k n", k=KT)).then_inc(s["s_w_in"], 16)
                sp.dma_start(swd, A["shared_w_down"][l].rearrange("(p k) n -> p k n", k=2)).then_inc(s["s_w_in"], 16)
                sp.dma_start(rw, A["router_w"].rearrange("(p k) n -> p k n", k=KT)).then_inc(s["s_w_in"], 16)
                sp.dma_start(rb, A["router_b"].partition_broadcast(P)).then_inc(s["s_w_in"], 16)
                for stream in range(2):
                    sp.dma_start(g2[:, stream, :], mod_d[l][stream, 5 * D:6 * D].partition_broadcast(P)).then_inc(s["s_w_in"], 16)
                sp.wait_ge(s["h2_stored"], 16 * gend)
                sp.wait_ge(s["x1_stored"], 16 * gend)

                def s_load(t, u, b, first):
                    if not first:
                        sp.wait_ge(s["s_tr"], g(t) - 1)
                    sp.dma_start(hs[b], h2_d[l][span(t * P, P), :]).then_inc(s[f"hs_in{b}"], 16)
                    if not first:
                        sp.wait_ge(s["s_x2"], g(t) - 1)
                    sp.dma_start(x1b[b], x_mix[l][span(t * P, P), :]).then_inc(s[f"x1_in{b}"], 16)

                def s_store(t, b):
                    sp.wait_ge(s["s_x2"], g(t) + 1)
                    sp.dma_start(x_ffn[l][span(t * P, P), :], ob[b]).then_inc(s[f"s_stored{b}"], 16)

                s_load(0, 0, 0, l == 0)
                s_load(1, 0, 1, l == 0)
                with sp.Fori(0, nt // 2 - 1) as i:
                    for b in range(2):
                        s_store(2 * i + b, b)
                        s_load(2 * i + 2 + b, i + 1, b, False)
                for b in range(2):
                    s_store(nt - 2 + b, b)
                pairs, pairs_1, pairs_2 = pair_counts(sp, l)
                nb = NBK[l]
                ge = lambda b: b + NBK[0] * l

                def w_load(blk, b, first):
                    if not first:
                        sp.wait_ge(s["e_d"], ge(blk) - 1)
                    e = sp.value_load(bexp_i[0:1, span(blk, 1)], min_val=0, max_val=NE - 1)
                    for n, name in enumerate(("moe_w_gate", "moe_w_up")):
                        src = A[name][l].rearrange("e (p k) n -> e p (k n)", k=KT)[bass.ds(e, 1)].rearrange("o p n -> (o p) n")
                        sp.dma_start(wgu[b][:, n, :], src).then_inc(s[f"e_w_in{b}"], 16)
                    src = A["moe_w_down"][l].rearrange("e (p k) n -> e p (k n)", k=2)[bass.ds(e, 1)].rearrange("o p n -> (o p) n")
                    sp.dma_start(wdn[b].rearrange("p a b -> p (a b)"), src).then_inc(s[f"e_w_in{b}"], 16)

                def y_store(blk, b):
                    sp.wait_ge(s["e_y_v"], ge(blk) + 1)
                    sp.wait_ge(s["e_y_s"], ge(blk) + 1)
                    sp.dma_start(y_d[l][span(blk * P, P), :], yb[b]).then_inc(s[f"e_stored{b}"], 16)

                w_load(0, 0, l == 0)
                w_load(1, 1, l == 0)
                with sp.Fori(pairs, nb // 2) as i:
                    for b in range(2):
                        sp.dma_start(y_d[l][span((2 * i + b) * P, P), :], g2[:, 0, :]).then_inc(s["e_filled"], 16)
                with sp.Fori(0, pairs_1) as i:
                    for b in range(2):
                        w_load(2 * i + 2 + b, b, False)
                        y_store(2 * i + b, b)
                for b in range(2):
                    y_store(2 * pairs_2 + 2 + b, b)
                for b in range(2):
                    sp.wait_ge(s[f"e_stored{b}"], 16 * (pairs_1 + 1 + NBK[0] // 2 * l))
                    sp.sem_inc(s["spare_seen"], 1)
                spare_pairs(sp, l, pairs, [("e_w_in0", 48), ("e_w_in1", 48), ("e_stored0", 16), ("e_stored1", 16)])
                with sp.Fori(0, pairs):
                    sp.sem_inc(s["e_filled"], 32)
                sp.wait_ge(s["e_filled"], 16 * (nb + NBK[0] * l))
                for b in range(2):
                    sp.wait_ge(s[f"s_stored{b}"], 8 * gend if l == 0 else 16 * (T // 2 + TL // 2))
                gc = lambda t: t + T * l
                for b in range(2):
                    sp.dma_start(x2b[b], x_ffn[l][b * P:(b + 1) * P, :]).then_inc(s[f"c_x_in{b}"], 16)
                if l == DEPTH - 1:
                    sp.dma_start(fgain, A["final_norm"].partition_broadcast(P)).then_inc(fgain_in, 16)
                dst = (lambda rows: x_in[l + 1][rows, :]) if l < DEPTH - 1 else (lambda rows: out[0, rows, :])

                def c_store(t, b):
                    sp.wait_ge(s["c_x3"], gc(t) + 1)
                    sp.dma_start(dst(span(t * P, P)), x3b[b]).then_inc(s[f"c_stored{b}"], 16)

                with sp.Fori(0, nt // 2 - 1) as i:
                    for b in range(2):
                        c_store(2 * i + b, b)
                        sp.dma_start(x2b[b], x_ffn[l][span((2 * i + 2 + b) * P, P), :]).then_inc(s[f"c_x_in{b}"], 16)
                for b in range(2):
                    c_store(nt - 2 + b, b)
                for b in range(2):
                    sp.wait_ge(s[f"c_stored{b}"], 16 * (gend // 2))

        @block.scalar
        def _(act):
            act.wait_ge(cond_in, 32)
            act.activation(ctmp[:, :, :], csrc[:, :, :], ACT.Exp, scale=-1.0).then_inc(exp_c, 1)
            for l in range(1 if stop in ("P", "A") else DEPTH):
                g = lambda t: t + T * l

                def square(t, first):
                    b = 0
                    act.wait_ge(s["x_in"], 16 * g(t) + 16)
                    if not first:
                        act.wait_ge(s["rstd_ready"], g(t))
                    act.activation(junk, xt, ACT.Square, scale=D ** -0.5, accum_out=sumsq[:, 0:1]).then_inc(s["ssq"], 1)

                def evac_hT(t, b):
                    act.wait_ge(s["hT_tr"], g(t) + 1)
                    for j in range(KT):
                        ins = act.activation(hT[b][:, j, :], PT[:, j * P:(j + 1) * P], ACT.Identity,
                                             bias=modcol[:, span(t, 1), 0, j], scale=modcol[:, span(t, 1), 1, j])
                    ins.then_inc(s["hT_evac"], 1)

                def evac_u(t, c, first):
                    act.wait_ge(s["u_mm"], NCH * g(t) + c + 1)
                    if c == 0 and not first:
                        act.wait_ge(s["u_used"], g(t))
                        act.wait_ge(s["v_copied"], g(t))
                        act.wait_ge(s["round_tr"], ROUNDS * (g(t) - 1) + 1)
                    act.activation(U[:, c * UCH:(c + 1) * UCH], ubank[c][:, 0:UCH], ACT.Copy).then_inc(s["u_evac"], 1)

                def tile(t, b, first, last):
                    if not last:
                        square(t + 1, False)
                    for c in range(NCH - 1):
                        evac_u(t, c, first)
                    if not last:
                        evac_hT(t + 1, 1 - b)
                    evac_u(t, NCH - 1, first)

                act.wait_ge(s["modcol_in"], 16 * T * (l + 1))
                square(0, l == 0)
                evac_hT(0, 0)
                tile(0, 0, True, False)
                with act.Fori(0, (T - 2) // 2) as i:
                    tile(2 * i + 1, 1, False, False)
                    tile(2 * i + 2, 0, False, False)
                tile(T - 1, 1, False, True)

                if stop == "P":
                    continue
                act.wait_ge(s["lam_sum"], l + 1)
                act.activation(nlam[:, 0:2], nlam[:, 2:4], ACT.Exp).then_inc(s["lam_exp"], 1)

                def att(t, nk, prev, last):
                    for k in range(HEADS):
                        if nk:
                            act.wait_ge(s["neg_max"], HEADS * g(t) + k + 1)
                            if k >= 3 and k - 3 in PROD:
                                act.wait_ge(s["p_tr"], NP * g(t) + PROD[k - 3] + 3)
                            elif k >= 3:
                                act.wait_ge(s["comb_done"], 4 * g(t) + (k - 3) // 2 + 1)
                            elif prev:
                                act.wait_ge(s["p_tr"], NP * g(t) - NP + PROD[(18, 19, 17)[k]] + 3)
                            act.activation(Pb[k % 3][:, 0:nk], (S0, S1)[k % 2][:, 0:nk], ACT.Exp, bias=nmax[:, k:k + 1],
                                           accum_out=rsum[:, k:k + 1]).then_inc(s["exp_done"], 1)
                        if k == 4 and prev:
                            act.wait_ge(s["ot_tr"], g(t))
                            act.activation(OT[:, 4:8, :].rearrange("p a b -> p (a b)"), PT[:, 512:1024], ACT.Copy).then_inc(s["ot_s"], 1)
                        at_T = product_at(k, 2, nk, prev)
                        if at_T:
                            j, _, n = at_T
                            h = 4 if n == NTOK else 1
                            act.wait_ge(s["p_tr"], NP * g(t) + j + 3)
                            act.wait_ge(s["pv_done"], NP * g(t) + j + 1)
                            act.activation(PTs[j % 2][:, h:n // P, :].rearrange("p a b -> p (a b)"), PT[:, 512:512 + n - h * P],
                                           ACT.Copy).then_inc(s["pt_s"], 1)
                        if k == 18 and prev:
                            act.wait_ge(s["x1_ready"], g(t))
                            act.wait_ge(s["h2_stored"], 16 * (g(t) - 1))
                            act.activation(h2b, xb, ACT.Square, scale=D ** -0.5, accum_out=h2s[:, 0:1]).then_inc(s["x1_sq"], 1)

                over_tiles(act, l, att)
                if stop == "A":
                    continue
                nt = T if l == 0 else TL
                gend = T * l + nt

                def ffn(m, gi, b, more):
                    act.wait_ge(s[m + "g"], gi + 1)
                    act.activation(gex[b], (S0, S1)[b][:, 0:DE], ACT.Exp, scale=-1.0).then_inc(s[m + "ex"], 1)
                    if more:
                        act.wait_ge(s[m + ("tr")], gi + 2)
                        act.activation((hT2, XT)[m == "e_"][1 - b][:, 4:8, :].rearrange("p a b -> p (a b)"), PT[:, 512:1024], ACT.Copy).then_inc(s[m + "t_s"], 1)

                def first_T(m, gi, b):
                    act.wait_ge(s[m + "tr"], gi + 1)
                    act.activation((hT2, XT)[m == "e_"][b][:, 4:8, :].rearrange("p a b -> p (a b)"), PT[:, 512:1024], ACT.Copy).then_inc(s[m + "t_s"], 1)

                first_T("s_", g(0), 0)
                with act.Fori(0, nt // 2 - 1) as i:
                    for b in range(2):
                        ffn("s_", g(2 * i + b), b, True)
                ffn("s_", g(nt - 2), 0, True)
                ffn("s_", g(nt - 1), 1, False)
                act.wait_ge(s["s_lg"], gend)
                act.activation(score[:, 0:nt, :], lg[:, 0:nt, :], ACT.Exp, scale=-1.0).then_inc(s["r_exp"], 1)
                pairs, pairs_1, pairs_2 = pair_counts(act, l)
                ge = lambda b: b + NBK[0] * l
                first_T("e_", ge(0), 0)

                def e_out(blk, b):
                    act.wait_ge(s["e_d"], ge(blk) + 1)
                    act.activation(yb[b][:, 512:1024], (S0, S1)[b][:, 512:1024], ACT.Copy).then_inc(s["e_y_s"], 1)

                def e_block(blk, u, b, more, first):
                    ffn("e_", ge(blk), b, more)
                    if not first:
                        act.wait_ge(s[f"e_stored{b}"], 16 * (u + NBK[0] // 2 * l))
                    e_out(blk, b)

                for b in range(2):
                    e_block(b, 0, b, True, l == 0)
                with act.Fori(1, pairs_1) as i:
                    for b in range(2):
                        e_block(2 * i + b, i, b, True, False)
                for b in range(2):
                    e_block(2 * pairs_2 + 2 + b, pairs_2 + 1, b, b == 0, False)
                act.wait_ge(s["e_y_s"], 2 * pairs_1 + 2 + NBK[0] * l)
                spare_pairs(act, l, pairs, [("e_ex", 2), ("e_t_s", 2), ("e_y_s", 2)])
                if l == DEPTH - 1:
                    for t in range(TL):
                        act.wait_ge(c_sum, t + 1)
                        act.activation(x2b[t % 2], x3b[t % 2], ACT.Square, scale=D ** -0.5, accum_out=h2s[:, 2:3]).then_inc(s["c_sq"], 1)

        @block.tensor
        def _(pe):
            pe.wait_ge(consts_in, 16)
            pe.wait_ge(cs_ready, 3)
            for l in range(1 if stop in ("P", "A") else DEPTH):
                g = lambda t: t + T * l
                mod_ps, row_ps = (B6, B7), (S0[:, 0:512], S0[:, 512:1024])

                def mod_chunk(i, first):
                    for b in range(2):
                        n = 2 * i + b
                        pe.wait_ge(s[f"mod_w_in{b}"], 16 * (i + 1 + NMCH // 2 * l))
                        if not first:
                            pe.wait_ge(s["mod_part"], n - 1 + NMCH * l)
                        for k in range(KT):
                            q = k % 4
                            mm = pe.matmul(mod_ps[b][32 * q:32 * q + 32, :], cs[:, k, :], wm[b][:, k, :],
                                           start=k < 4, stop=k >= 4)
                        mm.then_inc(s["mod_mm"], 1)
                        pe.wait_ge(s["mod_part"], n + 1 + NMCH * l)
                        if not first:
                            pe.wait_ge(s["mod_row"], n - 1 + NMCH * l)
                        pe.matmul(row_ps[b][0:2, :], C("pick"), part[b], start=True, stop=True).then_inc(s["mod_sel"], 1)

                mod_chunk(0, True)
                with pe.Fori(1, NMCH // 2) as i:
                    mod_chunk(i, False)

                def transpose_x(t, first):
                    pe.wait_ge(s["xn_done"], g(t) + 1)
                    if not first:
                        pe.wait_ge(s["hT_evac"], g(t))
                    xs = xt.rearrange("p (n k) -> p k n", k=KT)
                    for j in range(KT):
                        tr = pe.transpose(PT[:, j * P:(j + 1) * P], xs[:, j, :], ident)
                    tr.then_inc(s["hT_tr"], 1)

                def prep_round(t, r):
                    def copies(srcs, width):
                        for n, a in enumerate(srcs):
                            tr = pe.transpose(B7[0:width, n * P:(n + 1) * P], a, ident)
                        tr.then_inc(s["round_tr"], 1)
                    if r == 0:
                        pe.wait_ge(s["u_evac"], NCH * g(t) + NCH)
                    if not (l == 0 and r == 0 and isinstance(t, int) and t == 0):
                        pe.wait_ge(s["round_evac"], ROUNDS * g(t) + r)
                    if r == 0:
                        copies([U[:, a:a + P] for a in (NK_, NK_ + P, NQ, NQ + P)], P)
                    if r == 1:
                        pe.wait_ge(s["lor_ready"], g(t) + 1)
                        pe.transpose(B7[0:96, 0:P], lor[:, 0:96], ident)
                        pe.transpose(B7[0:96, P:2 * P], lor[:, 96:192], ident)
                        pe.transpose(B7[:, 2 * P:3 * P], lor[:, 192:320], ident).then_inc(s["round_tr"], 1)
                    if r == 2:
                        for k in range(2):
                            mm = pe.matmul(B7[:, 0:384], lorT[0:96, k, :], wqu[0:96, k, :], start=k == 0, stop=k == 1)
                        mm.then_inc(s["round_tr"], 1)
                    if r == 3:
                        pe.matmul(B7[:, :], lorT[:, 2, :], wkvu, start=True, stop=True).then_inc(s["round_tr"], 1)
                    if r == 4:
                        pe.wait_ge(s["st_ready"], g(t) + 1)
                        copies([st[:, P * n:P * n + P] for n in range(4)], P)
                    if r == 5:
                        copies([st[:, P * n:P * n + P] for n in range(4, 7)], P)
                    if r == 6:
                        pe.wait_ge(s["st_m_ready"], g(t) + 1)
                        copies([st[:, ST_MK + 96 * n:ST_MK + 96 * n + 96] for n in range(4)], 96)
                    if r == 7:
                        copies([st[:, ST_MQ + 96 * n:ST_MQ + 96 * n + 96] for n in range(4)], 96)

                def tile(t, b, first, last):
                    pe.wait_ge(s["hT_evac"], g(t) + 1)
                    for half in range(2 * NCH):
                        c, k0 = half // 2, (half % 2) * (KT // 2)
                        if k0 == 0:
                            pe.wait_ge(s["win_in"][c], 16 * (l + 1))
                            if not first:
                                pe.wait_ge(s["u_evac"], NCH * (g(t) - 1) + c + 1)
                        for k in range(k0, k0 + KT // 2):
                            mm = pe.matmul(ubank[c][:, 0:UCH], hT[b][:, k, :], win[:, k, c * UCH:(c + 1) * UCH],
                                           start=k == 0, stop=k == KT - 1)
                        if k0:
                            mm.then_inc(s["u_mm"], 1)
                        if not first and half < ROUNDS:
                            prep_round(t - 1, half)
                        if half == 7 and not last:
                            transpose_x(t + 1, False)

                transpose_x(0, True)
                pe.wait_ge(s["wsmall_in"], 16 * 10 * (l + 1))
                pe.wait_ge(s["mod_row"], NMCH * (l + 1))
                tile(0, 0, True, False)
                with pe.Fori(0, (T - 2) // 2) as i:
                    tile(2 * i + 1, 1, False, False)
                    tile(2 * i + 2, 0, False, False)
                tile(T - 1, 1, False, True)
                for r in range(ROUNDS):
                    prep_round(T - 1, r)

                if stop == "P":
                    continue
                units = [(P, SL_DK + m // 4, V_D + 64 * (m // 2)) for m in range(8)]
                units += [(P, SL_AK, V_A + 64 * (h // 2)) for h in range(4)]
                units += [(96, SL_MK + h, V_M + 64 * h) for h in range(4)]
                units += [(P, SL_NK + h // 2, V_N + 64 * h) for h in range(4)]

                def att(t, nk, prev, last):
                    n0, p0 = HEADS * g(t), NP * g(t)
                    o8 = O.rearrange("p (n k) -> p k n", k=KT)
                    for k in range(HEADS):
                        if nk:
                            if k in (0, 8, 12, 16):
                                pe.wait_ge(s["qs_ready"], 4 * g(t) + (0, 8, 12, 16).index(k) + 1)
                            nr, ks, _ = units[k]
                            pe.wait_ge(s["exp_done"], n0 + k + 1)
                            for c0 in range(0, nk, 512):
                                c1 = min(c0 + 512, nk)
                                mm = pe.matmul((S0, S1)[k % 2][:, c0:c1], Qs[0:nr, k, :], qk[0:nr, ks, NTOK - nk + c0:NTOK - nk + c1],
                                               start=True, stop=True)
                            mm.then_inc(s["scored"], 1)
                        if k == 4 and prev:
                            pe.wait_ge(s["o_all"], g(t))
                            pe.wait_ge(s["pt_v"], p0 + (3 if nk else 2))
                            pe.wait_ge(s["pt_s"], p0 + (3 if nk else 2))
                            for j in range(KT):
                                tr = pe.transpose(PT[:, j * P:(j + 1) * P], o8[:, j, :], ident)
                            tr.then_inc(s["ot_tr"], 1)
                        at_T = product_at(k, 2, nk, prev)
                        if at_T:
                            j, m, n = at_T
                            if 0 <= j < 4:
                                pe.wait_ge(s["comb_done"], 4 * g(t) + j + 1)
                            else:
                                pe.wait_ge(s["exp_done"], n0 + m + 3 - (HEADS if j < 0 else 0))
                            pe.wait_ge(s["pt_v"], p0 + j + 2)
                            pe.wait_ge(s["pt_s"], p0 + j + 2)
                            if k == 5 and prev:
                                pe.wait_ge(s["ot_v"], g(t))
                                pe.wait_ge(s["ot_s"], g(t))
                            for i in range(n // P):
                                c0 = i * P if n == NTOK else i * 512
                                tr = pe.transpose(PT[:, c0:c0 + P], Pb[m % 3][:, i * P:(i + 1) * P], ident)
                            tr.then_inc(s["p_tr"], 1)
                        at_V = product_at(k, 3, nk, prev)
                        if at_V:
                            j, m, n = at_V
                            pe.wait_ge(s["pt_v"], p0 + j + 3)
                            pe.wait_ge(s["pt_s"], p0 + j + 3)
                            pe.wait_ge(s["o_evac"], p0 + j + 2)
                            v0 = units[m][2]
                            for i in range(n // P):
                                mm = pe.matmul(B6[:, 0:64], PTs[j % 2][:, i, :], vals[:, (NTOK - n) // P + i, v0:v0 + 64],
                                               start=i == 0, stop=i == n // P - 1)
                            mm.then_inc(s["pv_done"], 1)
                        if prev and (6 <= k < 10 or 11 <= k < 15):
                            c, i = int(k > 10), (k - 6) % 5
                            if k == 6:
                                pe.wait_ge(s["ot_v"], g(t))
                                pe.wait_ge(s["ot_s"], g(t))
                            if i == 0:
                                pe.wait_ge(s["res_mul"], 2 * (g(t) - 1) + c)
                            for q in (2 * i, 2 * i + 1):
                                mm = pe.matmul(B7[:, :], OT[:, q, :], wout[:, q, c * 512:(c + 1) * 512], start=q == 0, stop=q == KT - 1)
                            if i == 3:
                                mm.then_inc(s["op_mm"], 1)

                pe.wait_ge(s["u_evac"], NCH * T * (l + 1))
                pe.wait_ge(s["round_evac"], ROUNDS * T * (l + 1))
                pe.wait_ge(s["wout_in"], 16 * (l + 1))
                over_tiles(pe, l, att)
                if stop == "A":
                    continue
                nt = T if l == 0 else TL
                gend = T * l + nt

                def transposes(m, gi, b):
                    x8 = (hs, xg)[m == "e_"][b].rearrange("p (n k) -> p k n", k=KT)
                    for j in range(KT):
                        tr = pe.transpose(PT[:, j * P:(j + 1) * P], x8[:, j, :], ident)
                    tr.then_inc(s[m + "tr"], 1)

                def ffn(m, gi, b, nxt):
                    e = m == "e_"
                    X = (hT2, XT)[e][b]
                    G = (S0, S1)[b]
                    pe.wait_ge(s[m + "t_v"], gi + 1)
                    pe.wait_ge(s[m + "t_s"], gi + 1)
                    if not e:
                        pe.wait_ge(s["s_lg"], gi)
                        for k in range(KT):
                            mm = pe.matmul(B6[:, 0:NE], X[:, k, :], rw[:, k, :], start=k == 0, stop=k == KT - 1)
                        mm.then_inc(s["s_rt"], 1)
                    for w, name in enumerate(("g", "u")):
                        for k in range(KT):
                            wk = wgu[b][:, w, k * DE:(k + 1) * DE] if e else swgu[:, k, w * DE:(w + 1) * DE]
                            mm = pe.matmul(G[:, 512 * w:512 * w + DE], X[:, k, :], wk, start=k == 0, stop=k == KT - 1)
                        mm.then_inc(s[m + name], 1)
                    nxt()
                    pe.wait_ge(s[m + "hid"], gi + 1)
                    hd = hid[b].rearrange("p (n k) -> p k n", k=2)
                    for j in range(2):
                        tr = pe.transpose(B7[:, j * P:(j + 1) * P], hd[:, j, :], ident)
                    tr.then_inc(s[m + "ht"], 1)
                    pe.wait_ge(s[m + "htv"], gi + 1)
                    for c in range(2):
                        for k in range(2):
                            wk = wdn[b][:, k, c * 512:(c + 1) * 512] if e else swd[:, k, c * 512:(c + 1) * 512]
                            mm = pe.matmul(G[:, c * 512:(c + 1) * 512], hidT[b][:, k, :], wk, start=k == 0, stop=k == 1)
                    mm.then_inc(s[m + "d"], 1)

                pe.wait_ge(s["res_mul"], 2 * gend)
                pe.wait_ge(s["s_w_in"], 16 * 7 * (l + 1))
                def s_next(t, b, first):
                    pe.wait_ge(s[f"hs_in{b}"], hs_count(t, b))
                    if not first:
                        pe.wait_ge(s["s_t_v"], g(t))
                        pe.wait_ge(s["s_t_s"], g(t))
                    transposes("s_", g(t), b)

                def hs_count(t, b):
                    return 8 * (t - b) + 16 + 8 * T * l

                s_next(0, 0, l == 0)
                def s_block(t, b, more, first):
                    if not first:
                        pe.wait_ge(s["s_ob"], g(t) - 1)
                    ffn("s_", g(t), b, (lambda: s_next(t + 1, 1 - b, False)) if more else (lambda: None))
                for b in range(2):
                    s_block(b, b, True, l == 0)
                for i in range(1, nt // 2 - 1):
                    for b in range(2):
                        s_block(2 * i + b, b, True, False)
                for b in range(2):
                    s_block(nt - 2 + b, b, b == 0, False)
                pe.wait_ge(s["r_mat"], l + 1)
                pe.matmul(B6[:, 0:nt * NE], C("before"), both[:, 0:nt, :].rearrange("p a b -> p (a b)"), start=True, stop=True)
                pe.matmul(B7[:, 0:nt * NE], ones, both[:, 0:nt, :].rearrange("p a b -> p (a b)"), start=True, stop=True).then_inc(s["r_cum"], 1)
                pairs, pairs_1, pairs_2 = pair_counts(pe, l)
                ge = lambda b: b + NBK[0] * l
                pe.wait_ge(s["s_ob"], gend)

                def e_next(blk, u, b, first):
                    pe.wait_ge(e_x_in[l][b], 16 * (u + 1))
                    if not first:
                        pe.wait_ge(s["e_t_v"], ge(blk))
                        pe.wait_ge(s["e_t_s"], ge(blk))
                    transposes("e_", ge(blk), b)

                def e_block(blk, u, b, more, first):
                    pe.wait_ge(s[f"e_w_in{b}"], 48 * (u + 1 + NBK[0] // 2 * l))
                    if not first:
                        pe.wait_ge(s["e_y_v"], ge(blk) - 1)
                        pe.wait_ge(s["e_y_s"], ge(blk) - 1)
                    ffn("e_", ge(blk), b, (lambda: e_next(blk + 1, u + b, 1 - b, False)) if more else (lambda: None))

                e_next(0, 0, 0, l == 0)
                for b in range(2):
                    e_block(b, 0, b, True, l == 0)
                with pe.Fori(1, pairs_1) as i:
                    for b in range(2):
                        e_block(2 * i + b, i, b, True, False)
                for b in range(2):
                    e_block(2 * pairs_2 + 2 + b, pairs_2 + 1, b, b == 0, False)
                pe.wait_ge(s["e_d"], 2 * pairs_1 + 2 + NBK[0] * l)
                spare_pairs(pe, l, pairs, [("e_tr", 2), ("e_g", 2), ("e_u", 2), ("e_ht", 2), ("e_d", 2)])

        @block.gpsimd
        def _(pool):
            pool.memset(halfs[:, 0:8], -0.5).then_inc(halfs_set, 1)
            pool.memset(halfs[:, 8:14], 1.0 / 64).then_inc(halfs_set, 1)
            pool.memset(halfs[:, 14:16], 1.0).then_inc(halfs_set, 1)
            pool.memset(halfs[:, 16:24], EPS).then_inc(halfs_set, 1)
            pool.wait_ge(halfs_set, 4)
            for l in range(1 if stop in ("P", "A") else DEPTH):
                g = lambda t: t + T * l

                def rstd_of(t):
                    pool.wait_ge(s["ssq"], g(t) + 1)
                    pool.tensor_tensor(meansq[:, 0:1], sumsq[:, 0:1], eps8[:, 0:1], ALU.add).then_inc(s["mean_x"], 1)
                    pool.wait_ge(s["mean_x"], g(t) + 1)
                    pool.tensor_tensor(rstd[:, 0:1], meansq[:, 0:1], halfs[:, 0:1], ALU.pow).then_inc(s["rstd_ready"], 1)

                def prep(t):
                    pool.wait_ge(s["u_evac"], NCH * g(t) + NCH)
                    vt = vals[:, span(t, 1), :]
                    pool.tensor_copy(vt[:, :, V_A:V_A + 128], U[:, AV:AV + 128].unsqueeze(1))
                    pool.tensor_copy(vt[:, :, V_N:V_N + 256], U[:, NV:NV + 256].unsqueeze(1))
                    pool.tensor_copy(vt[:, :, V_D:V_D + 256], U[:, DV:DV + 256].unsqueeze(1)).then_inc(s["v_copied"], 1)
                    pool.wait_ge(s["stats"], g(t) + 1)
                    ch = Count(pool, s["g_prep"], 2 * g(t))
                    ch.done(pool.tensor_tensor(m8[:, :], s8[:, :], inv8, ALU.mult)).sync()
                    ch.done(pool.tensor_tensor(m8[:, :], m8[:, :], eps8, ALU.add)).sync()
                    assert ch.n == 2
                    pool.tensor_tensor(r8[:, :], m8[:, :], halfs[:, 0:8], ALU.pow).then_inc(s["r8_ready"], 1)

                rstd_of(0)
                rstd_of(1)
                with pool.Fori(0, T - 2) as t:
                    prep(t)
                    rstd_of(t + 2)
                prep(T - 2)
                prep(T - 1)

                if stop == "P":
                    continue
                pool.wait_ge(s["bias_in"], 16 * 8 * (l + 1))
                bt = bias_t.rearrange("p h (j c) -> p (h j) c", c=GRID_W)
                pool.wait_ge(s["r8_ready"], T * (l + 1))
                pool.tensor_tensor(bt, bt, C("window").unsqueeze(1).to_broadcast([P, 64, GRID_W]), ALU.add).then_inc(s["bias_ready"], 1)

                def att(t, nk, prev, last):
                    if nk:
                        pool.wait_ge(s["d_stat"], g(t) + 1)
                        pool.tensor_tensor(dstat[:, 4:8], dstat[:, 0:4], eps8[:, 0:4], ALU.add).then_inc(s["g_att"], 1)
                        pool.wait_ge(s["g_att"], g(t) + 1)
                        pool.tensor_tensor(dstat[:, 4:8], dstat[:, 4:8], halfs[:, 0:4], ALU.pow).then_inc(s["d_rs"], 1)
                    if prev:
                        gp = g(t) - 1
                        w = 0 if prev == NTOK else 3
                        ch = Count(pool, s["g_x"], 4 * gp)
                        pool.wait_ge(s["xa_in"], 16 * gp + 16)
                        pool.wait_ge(s["res_mul"], 2 * gp + 2)
                        pool.tensor_tensor(xb, xb, xa, ALU.add).then_inc(s["x1_ready"], 1)
                        pool.wait_ge(s["x1_sq"], gp + 1)
                        ch.done(pool.tensor_tensor(h2s[:, 1:2], h2s[:, 0:1], eps8[:, 0:1], ALU.add)).sync()
                        ch.done(pool.tensor_tensor(h2s[:, 1:2], h2s[:, 1:2], halfs[:, 0:1], ALU.pow)).sync()
                        ch.done(pool.tensor_tensor(h2b, xb, h2s[:, 1:2].to_broadcast([P, D]), ALU.mult)).sync()
                        ch.done(pool.tensor_tensor(h2b, h2b, vec[:, w + 1, :], ALU.mult)).sync()
                        pool.tensor_tensor(h2b, h2b, vec[:, w + 2, :], ALU.add).then_inc(s["h2_ready"], 1)
                        assert ch.n == 4

                pool.wait_ge(s["vec_in"], 16 * 6 * (l + 1))
                over_tiles(pool, l, att)
                if stop == "A":
                    continue
                nt = T if l == 0 else TL
                gend = T * l + nt

                def s_sum(t, u, b):
                    pool.wait_ge(s["s_ob"], g(t) + 1)
                    pool.wait_ge(s[f"x1_in{b}"], 16 * (u + 1 + T // 2 * l))
                    pool.tensor_tensor(ob[b], ob[b], x1b[b], ALU.add).then_inc(s["s_x2"], 1)
                with pool.Fori(0, nt // 2) as i:
                    for b in range(2):
                        s_sum(2 * i + b, i, b)
                if l == 0:
                    pool.wait_ge(zeros_stored, 16 * DEPTH)
                pool.wait_ge(s["r_slots"], l + 1)
                for t in range(nt):
                    for j in range(TOPK):
                        pool.indirect_dma_start(out=slot_tok[l], out_offset=bass.IndirectOffsetOnAxis(ap=slots[:, t, j:j + 1], axis=0),
                                                in_=tok_u[:, t:t + 1], in_offset=None).then_inc(s["r_scat"], 16)
                pool.wait_ge(s["r_scat"], 16 * TOPK * gend)
                nb = NBK[l]
                pool.dma_start(table_u[:, 0:nb], slot_tok[l][0:nb * P, :].rearrange("(b p) o -> p (b o)", p=P),
                               allow_slow_non_contiguous=True).then_inc(s["r_tab"], 16)
                pool.wait_ge(s["r_tab"], 16 * (l + 1))
                pairs, _, _ = pair_counts(pool, l)
                ge = lambda b: b + NBK[0] * l

                def e_gather(blk, b, first):
                    if not first:
                        pool.wait_ge(s["e_tr"], ge(blk) - 1)
                    pool.tensor_copy(idx1[b], table_u[:, span(blk, 1)]).then_inc(s["e_idx"], 1)
                    pool.wait_ge(s["e_idx"], ge(blk) + 1)
                    pool.sem_inc(s["idx_seen"], 1)
                    pool.indirect_dma_start(out=xg[b], out_offset=None, in_=h2_d[l],
                                            in_offset=bass.IndirectOffsetOnAxis(ap=idx1[b], axis=0)).then_inc(e_x_in[l][b], 16)
                for b in range(2):
                    e_gather(b, b, l == 0)
                with pool.Fori(1, pairs) as i:
                    for b in range(2):
                        e_gather(2 * i + b, b, False)
                spare_pairs(pool, l, pairs, [("e_idx", 2)])
                pool.wait_ge(s["e_filled"], 16 * (nb + NBK[0] * l))
                for b in range(2):
                    pool.wait_ge(s[f"e_stored{b}"], 16 * ((nb + NBK[0] * l) // 2))

                def c_gather(t, b, first):
                    if not first:
                        pool.wait_ge(s["c_x3"], g(t) - 1)
                    pool.tensor_copy(idx2[b].unsqueeze(1), slots[:, span(t, 1), :]).then_inc(s["c_idx"], 1)
                    pool.wait_ge(s["c_idx"], g(t) + 1)
                    pool.sem_inc(s["idx_seen"], 1)
                    for j in range(TOPK):
                        pool.indirect_dma_start(out=y12[b][:, j, :], out_offset=None, in_=y_d[l],
                                                in_offset=bass.IndirectOffsetOnAxis(ap=idx2[b][:, j:j + 1], axis=0)).then_inc(s[f"c_y_in{b}"], 16)
                for b in range(2):
                    c_gather(b, b, l == 0)
                if l < DEPTH - 1:
                    with pool.Fori(1, nt // 2) as i:
                        for b in range(2):
                            c_gather(2 * i + b, b, False)
                else:
                    for t in range(TL):
                        pool.wait_ge(s["c_sq"], t + 1)
                        pool.tensor_tensor(h2s[:, 3:4], h2s[:, 2:3], eps8[:, 0:1], ALU.add).then_inc(s["c_mean"], 1)
                        pool.wait_ge(s["c_mean"], t + 1)
                        pool.tensor_tensor(h2s[:, 3:4], h2s[:, 3:4], halfs[:, 0:1], ALU.pow).then_inc(s["c_rs"], 1)
                        if t + 2 < TL:
                            c_gather(t + 2, t % 2, False)

        @block.vector
        def _(dve):
            dve.memset(cs[:, :, :], 0.0).then_inc(cs_ready, 1)
            dve.memset(relpad, 0.0).then_inc(relpad_set, 1)
            dve.memset(zeros_u, 0).then_inc(relpad_set, 1)
            R_START = [0]
            dve.wait_ge(exp_c, 1)
            ch = Count(dve, v_init, 0)
            ch.done(dve.tensor_scalar(ctmp[:, :, :], ctmp[:, :, :], 1.0, None, ALU.add)).sync()
            ch.done(dve.reciprocal(ctmp[:, :, :], ctmp[:, :, :])).sync()
            dve.wait_ge(cs_ready, 1)
            for r in range(2):
                dve.tensor_tensor(cs[:, :, r], csrc[:, r, :], ctmp[:, r, :], ALU.mult).then_inc(cs_ready, 1)
            dve.wait_ge(consts_in, 16)
            for l in range(1 if stop in ("P", "A") else DEPTH):
                g = lambda t: t + T * l
                row_ps = (S0[0:2, 0:512], S0[0:2, 512:1024])

                def mod_chunk(i):
                    for b in range(2):
                        n = 2 * i + b
                        dve.wait_ge(s["mod_mm"], n + 1 + NMCH * l)
                        dve.tensor_copy(part[b], (B6, B7)[b][:, :]).then_inc(s["mod_part"], 1)
                        dve.wait_ge(s["mod_sel"], n + 1 + NMCH * l)
                        cols = span(n * MCH, MCH)
                        dve.tensor_tensor(modrow[:, cols], row_ps[b], brow[:, cols], ALU.add).then_inc(s["mod_row"], 1)

                dve.wait_ge(s["mod_rows_in"], 16 * 6 * (l + 1))
                with dve.Fori(0, NMCH // 2) as i:
                    mod_chunk(i)
                dve.wait_ge(s["mod_row"], NMCH * (l + 1))
                for w, n in ((1, 0), (4, 1)):
                    a = modrow[:, w * D:(w + 1) * D]
                    dve.scalar_tensor_tensor(a, a, 1.0, nrow[:, n, :], ALU.add, ALU.mult).then_inc(s["mod_gain"], 1)

                def normalise(t):
                    dve.wait_ge(s["rstd_ready"], g(t) + 1)
                    dve.tensor_scalar(xt, xt, rstd[:, 0:1], None, ALU.mult).then_inc(s["xn_done"], 1)

                def rope(ch, x, t, rot, heads, outs):
                    q = rot // 4
                    ctab = cos[rot][:, span(t, 1), :]
                    stab = sin[rot][:, span(t, 1), :].rearrange("p o (a h c) -> p (o a) h c", a=2, h=2)
                    a3 = tmpA[:, 0:heads * rot].rearrange("p (h c) -> p h c", h=heads)
                    ch.done(dve.tensor_tensor(a3, x, ctab.to_broadcast([P, heads, rot]), ALU.mult))
                    x5 = x.rearrange("p h (a b c) -> p h a b c", a=2, b=2)
                    b5 = tmpB[:, 0:heads * rot].rearrange("p (h a b c) -> p h a b c", h=heads, a=2, b=2)
                    for half in range(2):
                        tab = stab[:, :, half, :].unsqueeze(1).to_broadcast([P, heads, 2, q])
                        ch.done(dve.tensor_tensor(b5[:, :, :, half, :], x5[:, :, :, 1 - half, :], tab, ALU.mult))
                    ch.sync()
                    b3 = tmpB[:, 0:heads * rot].rearrange("p (h c) -> p h c", h=heads)
                    for h0, h1, o in outs:
                        ai, bi = a3[:, h0:h1, :], b3[:, h0:h1, :]
                        if o.ndim == 4:
                            ai = ai.rearrange("p (a b) c -> p a b c", b=o.shape[2])
                            bi = bi.rearrange("p (a b) c -> p a b c", b=o.shape[2])
                        ch.done(dve.tensor_tensor(o, ai, bi, ALU.add))

                heads_of = lambda a, n: a.rearrange("p (h c) -> p h c", h=n)

                def evac_round(t, r, src, dst):
                    dve.wait_ge(s["round_tr"], ROUNDS * g(t) + r + 1)
                    dve.tensor_copy(dst, src).then_inc(s["round_evac"], 1)

                def to_qk(t, r, slot, n, rows=P):
                    evac_round(t, r, B7[0:rows, 0:n * P].rearrange("p (n c) -> p n c", n=n),
                               qk[0:rows, slot:slot + n, span(t * P, P)])

                N_PREP = 30

                def prep(t):
                    ch = Count(dve, s["v_prep"], N_PREP * g(t))
                    dve.wait_ge(s["u_evac"], NCH * g(t) + NCH)
                    ch.done(dve.tensor_tensor(tmpA[:, 0:384], U[:, AQ:AQ + 384], U[:, AQ:AQ + 384], ALU.mult))
                    ch.done(dve.tensor_tensor_reduce(tmpB[:, 0:192], U[:, CQ:CQ + 192], U[:, CQ:CQ + 192], 1.0 / 192, 0.0,
                                                     ALU.mult, ALU.add, s8[:, 6:7]))
                    ch.done(dve.tensor_tensor_reduce(tmpB[:, 192:320], U[:, CKV:CKV + 128], U[:, CKV:CKV + 128], 1.0 / 128, 0.0,
                                                     ALU.mult, ALU.add, s8[:, 7:8]))
                    ch.sync()
                    dve.tensor_reduce(s8[:, 0:6], heads_of(tmpA[:, 0:384], 6), AX.X, ALU.add).then_inc(s["stats"], 1)
                    dve.wait_ge(s["stats"], g(t) + 1)
                    rope(ch, heads_of(U[:, DQ:DQ + 512], 16), t, 32, 16,
                         [(0, 8, heads_of(st[:, ST_DQ:ST_DQ + 256], 8)), (8, 16, heads_of(st[:, ST_DK:ST_DK + 256], 8))])
                    to_qk(t, 0, SL_NK, 4)
                    dve.wait_ge(s["r8_ready"], g(t) + 1)
                    ch.done(dve.scalar_tensor_tensor(lor[:, 0:192], U[:, CQ:CQ + 192], r8[:, 6:7], lgain[:, 0:192], ALU.mult, ALU.mult))
                    ch.done(dve.scalar_tensor_tensor(lor[:, 192:320], U[:, CKV:CKV + 128], r8[:, 7:8], lgain[:, 192:320], ALU.mult, ALU.mult))
                    ch.sync()
                    dve.sem_inc(s["lor_ready"], 1)
                    rope(ch, heads_of(U[:, KPE:KPE + 32], 1), t, 32, 1, [(0, 1, heads_of(kper, 1))])
                    ch.sync()
                    dve.wait_ge(s["round_tr"], ROUNDS * g(t) + 2)
                    ch.done(dve.tensor_copy(lorT[0:96, 0:2, :], B7[0:96, 0:256].rearrange("p (n c) -> p n c", n=2)))
                    ch.sync()
                    dve.tensor_copy(lorT[:, 2, :], B7[:, 256:384]).then_inc(s["round_evac"], 1)
                    a3 = heads_of(tmpA[:, 0:384], 6)
                    g3 = heads_of(st[:, ST_MK:ST_MK + 384], 6)
                    ch.done(dve.tensor_tensor(a3, heads_of(U[:, AQ:AQ + 384], 6), r8[:, 0:6].unsqueeze(2).to_broadcast([P, 6, 64]), ALU.mult))
                    ch.sync()
                    ch.done(dve.tensor_tensor(g3, a3, gains[:, :, :], ALU.mult))
                    ch.sync()
                    dve.sem_inc(s["u_used"], 1)
                    rope(ch, g3, t, 64, 6,
                         [(0, 4, st[:, ST_AQ:ST_AQ + 256].rearrange("p (b a c) -> p a b c", b=2, a=2)),
                          (4, 6, heads_of(st[:, ST_AK:ST_AK + 128], 2))])
                    ch.sync()
                    dve.sem_inc(s["st_ready"], 1)
                    dve.wait_ge(s["round_tr"], ROUNDS * g(t) + 3)
                    q3, k3 = heads_of(B7[:, 0:384], 4), heads_of(B7[:, 0:512], 4)
                    mq, mk = heads_of(st[:, ST_MQ:ST_MQ + 384], 4), heads_of(st[:, ST_MK:ST_MK + 384], 4)
                    ch.done(dve.tensor_copy(mq[:, :, 0:64], q3[:, :, 0:64]))
                    rope(ch, q3[:, :, 64:96], t, 32, 4, [(0, 4, mq[:, :, 64:96])])
                    ch.sync()
                    dve.sem_inc(s["round_evac"], 1)
                    dve.wait_ge(s["round_tr"], ROUNDS * g(t) + 4)
                    ch.done(dve.tensor_copy(mk[:, :, 0:64], k3[:, :, 0:64]))
                    ch.done(dve.tensor_copy(mk[:, :, 64:96], kper.unsqueeze(1).to_broadcast([P, 4, 32])))
                    ch.done(dve.tensor_copy(vals[:, span(t, 1), V_M:V_M + 256].rearrange("p o (h c) -> p (o h) c", h=4), k3[:, :, 64:128]))
                    ch.sync()
                    dve.sem_inc(s["round_evac"], 1)
                    dve.sem_inc(s["st_m_ready"], 1)
                    to_qk(t, 4, SL_AK, 4)
                    to_qk(t, 5, SL_AQ + 1, 3)
                    to_qk(t, 6, SL_MK, 4, 96)
                    to_qk(t, 7, SL_MQ, 4, 96)
                    assert ch.n == N_PREP, ch.n

                normalise(0)
                normalise(1)
                with dve.Fori(0, T - 2) as t:
                    prep(t)
                    normalise(t + 2)
                prep(T - 2)
                prep(T - 1)

                if stop == "P":
                    continue
                nt = T if l == 0 else TL
                gend = T * l + nt
                lam_init = 0.8 - 0.6 * math.exp(-0.3 * l)
                dve.wait_ge(s["lam_in"], 16 * 5 * (l + 1))
                ch = Count(dve, s["v_lam"], 7 * l)
                ch.done(dve.tensor_tensor_reduce(dtmp[:, 0:32], lamb[:, 0, :], lamb[:, 1, :], 1.0, 0.0, ALU.mult, ALU.add, nlam[:, 2:3]))
                ch.done(dve.tensor_tensor_reduce(dtmp[:, 32:64], lamb[:, 2, :], lamb[:, 3, :], 1.0, 0.0, ALU.mult, ALU.add, nlam[:, 3:4]))
                ch.done(dve.tensor_scalar(subg[:, :], subg[:, :], 1.0 - lam_init, None, ALU.mult))
                ch.sync()
                dve.sem_inc(s["lam_sum"], 1)
                dve.wait_ge(s["lam_exp"], l + 1)
                ch.done(dve.tensor_tensor(nlam[:, 2:3], nlam[:, 1:2], nlam[:, 0:1], ALU.subtract)).sync()
                ch.done(dve.tensor_scalar(nlam[:, 2:3], nlam[:, 2:3], -lam_init, None, ALU.add)).sync()
                N_O = 48

                def queries(kind, t):
                    cols = span(t * P, P)
                    ins = []
                    if kind == "diff":
                        for m in range(4):
                            r = slice(32 * m, 32 * m + 32)
                            dst = Qs[r, 0:8, :].rearrange("p (a m) c -> p a m c", a=2)[:, :, m, :]
                            ins.append(dve.tensor_scalar(dst, qk[r, SL_DQ:SL_DQ + 2, cols], 32 ** -0.5, None, ALU.mult))
                    if kind == "gqa":
                        for m in range(2):
                            r = slice(64 * m, 64 * m + 64)
                            ins.append(dve.tensor_scalar(Qs[r, 8 + 2 * m:10 + 2 * m, :], qk[r, SL_AQ:SL_AQ + 2, cols], 64 ** -0.5, None, ALU.mult))
                    if kind == "mla":
                        ins.append(dve.tensor_scalar(Qs[0:96, 12:16, :], qk[0:96, SL_MQ:SL_MQ + 4, cols], 96 ** -0.5, None, ALU.mult))
                    if kind == "na":
                        for m in range(2):
                            r = slice(64 * m, 64 * m + 64)
                            dst = Qs[r, 16:20, :].rearrange("p (a m) c -> p a m c", a=2)[:, :, m, :]
                            ins.append(dve.tensor_scalar(dst, qk[r, SL_NQ:SL_NQ + 2, cols], 64 ** -0.5, None, ALU.mult))
                    ins[-1].then_inc(s["qs_ready"], 1)

                def att(t, nk, prev, last):
                    n0, p0 = HEADS * g(t), NP * g(t)
                    ch = Count(dve, s["v_o"], N_O * g(t)) if nk else Count(dve, s["v_lam"], 7 * l + 6)
                    for k in range(HEADS):
                        if nk:
                            Sk = (S0, S1)[k % 2]
                            dve.wait_ge(s["scored"], n0 + k + 1)
                            if nk == NTOK and k >= 16:
                                h = k - 16
                                bt = bias_t[:, h:h + 1, span((7 - 2 * t) * GRID_W, SEQ)]
                                ch.done(dve.tensor_tensor(Sk[:, 0:SEQ].unsqueeze(1), Sk[:, 0:SEQ].unsqueeze(1), bt, ALU.add)).sync()
                            dve.tensor_reduce(nmax[:, k:k + 1], Sk[:, 0:nk], AX.X, ALU.max, negate=True).then_inc(s["neg_max"], 1)
                        if (nk and k) or (prev and k == 0):
                            m = (k - 1) % HEADS
                            dve.wait_ge(s["exp_done"], n0 + k + 2)
                            ch.done(dve.reciprocal(rinv[:, m:m + 1], rsum[:, m:m + 1])).sync()
                            if m < 8 and m % 2:
                                ra = ratio[:, m // 2:m // 2 + 1]
                                ch.done(dve.scalar_tensor_tensor(ra, rinv[:, m:m + 1], nlam[:, 2:3], rsum[:, m - 1:m], ALU.mult, ALU.mult)).sync()
                                dve.scalar_tensor_tensor(Pb[m % 3][:, 0:nk], Pb[m % 3][:, 0:nk], ra, Pb[(m - 1) % 3][:, 0:nk],
                                                         ALU.mult, ALU.add).then_inc(s["comb_done"], 1)
                        at_T = product_at(k, 2, nk, prev)
                        if at_T:
                            j, _, n = at_T
                            h = 4 if n == NTOK else 1
                            dve.wait_ge(s["p_tr"], p0 + j + 3)
                            dve.wait_ge(s["pv_done"], p0 + j + 1)
                            dve.tensor_copy(PTs[j % 2][:, 0:h, :].rearrange("p a b -> p (a b)"), PT[:, 0:h * P]).then_inc(s["pt_v"], 1)
                        if k == 4 and prev:
                            dve.wait_ge(s["ot_tr"], g(t))
                            dve.tensor_copy(OT[:, 0:4, :].rearrange("p a b -> p (a b)"), PT[:, 0:512]).then_inc(s["ot_v"], 1)
                        at_V = product_at(k, 3, nk, prev)
                        if at_V:
                            j, m, n = at_V
                            dve.wait_ge(s["pv_done"], p0 + j + 3)
                            if 0 <= j < 4:
                                o = O[:, 512 + 64 * j:576 + 64 * j]
                                dve.tensor_scalar(o, B6[:, 0:64], rinv[:, m - 1:m], None, ALU.mult).then_inc(s["o_evac"], 1)
                                dve.wait_ge(s["o_evac"], p0 + j + 3)
                                ins = dve.tensor_tensor_reduce(dtmp[:, 64:128], o, o, 1.0 / 64, 0.0, ALU.mult, ALU.add, dstat[:, j:j + 1])
                                if j == 3:
                                    ins.then_inc(s["d_stat"], 1)
                                else:
                                    ch.done(ins)
                            else:
                                base = {2: 0, 3: 768, 4: 256}[m // 4]
                                dve.tensor_scalar(O[:, base + 64 * (m % 4):base + 64 * (m % 4) + 64], B6[:, 0:64], rinv[:, m:m + 1], None,
                                                  ALU.mult).then_inc(s["o_evac"], 1)
                        if k == 2 and prev:
                            dve.wait_ge(s["o_evac"], p0 + 2)
                            dve.sem_inc(s["o_all"], 1)
                        if k in (10, 15) and prev:
                            gp, c = g(t) - 1, int(k == 15)
                            if c == 0:
                                dve.wait_ge(s["x1_stored"], 16 * gp)
                                dve.wait_ge(s["h2_ready"], gp)
                            dve.wait_ge(s["op_mm"], 2 * gp + c + 1)
                            dve.tensor_tensor(xb[:, c * 512:(c + 1) * 512], B7[:, :], vec[:, 0 if prev == NTOK else 3, c * 512:(c + 1) * 512],
                                              ALU.mult).then_inc(s["res_mul"], 1)
                        if k == 14 and nk:
                            dve.wait_ge(s["d_rs"], g(t) + 1)
                            o4 = O[:, 512:768].rearrange("p (h c) -> p h c", h=4)
                            ch.done(dve.tensor_tensor(o4, o4, dstat[:, 4:8].unsqueeze(2).to_broadcast([P, 4, 64]), ALU.mult)).sync()
                            ch.done(dve.tensor_tensor(o4, o4, subg[:, :].unsqueeze(1).to_broadcast([P, 4, 64]), ALU.mult))
                        if k == 2 and nk:
                            queries("na", t)
                        if nk and not last and k in (9, 13, 17):
                            queries({9: "diff", 13: "gqa", 17: "mla"}[k], t + 1)
                    if nk:
                        ch.sync()
                        assert ch.n <= N_O, ch.n
                        if ch.n < N_O:
                            dve.sem_inc(s["v_o"], N_O - ch.n)
                    else:
                        assert ch.n == 1

                dve.wait_ge(s["vec_in"], 16 * 6 * (l + 1))
                dve.wait_ge(s["bias_ready"], l + 1)
                dve.wait_ge(s["round_evac"], ROUNDS * T * (l + 1))
                ch.done(dve.memset(Qs, 0.0)).sync()
                for kind in ("diff", "gqa", "mla"):
                    queries(kind, 0)
                over_tiles(dve, l, att)
                if stop == "A":
                    continue

                def x_half(m, b):
                    return (hT2, XT)[m == "e_"][b][:, 0:4, :].rearrange("p a b -> p (a b)")

                def first_T(m, gi, b):
                    dve.wait_ge(s[m + "tr"], gi + 1)
                    dve.tensor_copy(x_half(m, b), PT[:, 0:512]).then_inc(s[m + "t_v"], 1)

                def ffn(m, gi, b, more):
                    ch = Count(dve, s["v_" + m[0]], 3 * gi)
                    G = (S0, S1)[b]
                    dve.wait_ge(s[m + "ex"], gi + 1)
                    ch.done(dve.tensor_scalar(gex[b], gex[b], 1.0, None, ALU.add)).sync()
                    ch.done(dve.reciprocal(gex[b], gex[b])).sync()
                    ch.done(dve.tensor_tensor(gex[b], G[:, 0:DE], gex[b], ALU.mult)).sync()
                    dve.wait_ge(s[m + "u"], gi + 1)
                    dve.tensor_tensor(hid[b], G[:, 512:512 + DE], gex[b], ALU.mult).then_inc(s[m + "hid"], 1)
                    if more:
                        dve.wait_ge(s[m + "tr"], gi + 2)
                        dve.tensor_copy(x_half(m, 1 - b), PT[:, 0:512]).then_inc(s[m + "t_v"], 1)
                    dve.wait_ge(s[m + "ht"], gi + 1)
                    dve.tensor_copy(hidT[b].rearrange("p a b -> p (a b)"), B7[:, 0:256]).then_inc(s[m + "htv"], 1)
                    dve.wait_ge(s[m + "d"], gi + 1)

                def s_block(t, u, b, more, first, stream):
                    dve.wait_ge(s["s_rt"], g(t) + 1)
                    dve.tensor_copy(lg[:, span(t, 1), :], B6[:, 0:NE].unsqueeze(1)).then_inc(s["s_lg"], 1)
                    ffn("s_", g(t), b, more)
                    if not first:
                        dve.wait_ge(s[f"s_stored{b}"], 16 * (u + T // 2 * l))
                    dve.tensor_tensor(ob[b], (S0, S1)[b][:, :], g2[:, stream, :], ALU.mult).then_inc(s["s_ob"], 1)

                first_T("s_", g(0), 0)
                for b in range(2):
                    s_block(b, 0, b, True, l == 0, 0)
                if l == 0:
                    for b in range(2):
                        s_block(2 + b, 1, b, True, False, 0)
                    for b in range(2):
                        s_block(4 + b, 2, b, b == 0, False, 1)
                else:
                    for b in range(2):
                        s_block(2 + b, 1, b, b == 0, False, 0)

                ch = Count(dve, s["v_r"], R_START[0])
                row = lambda a: a.rearrange("p a b -> p (a b)")
                sc_, sel_ = score[:, 0:nt, :], selb[:, 0:nt, :]
                step = lambda ins: ch.done(ins).sync()
                dve.wait_ge(s["r_exp"], l + 1)
                step(dve.tensor_scalar(sc_, sc_, 1.0, None, ALU.add))
                step(dve.reciprocal(sc_, sc_))
                step(dve.tensor_tensor(sel_, sc_, rb.unsqueeze(1).to_broadcast([P, nt, NE]), ALU.add))
                q = row(sel_).rearrange("p (a b) -> p a b", b=4)
                ng = nt * NG
                pr = lambda n: pair[:, n, 0:ng]
                ch.done(dve.tensor_tensor(pr(0), q[:, :, 0], q[:, :, 1], ALU.max))
                ch.done(dve.tensor_tensor(pr(1), q[:, :, 2], q[:, :, 3], ALU.max))
                ch.done(dve.tensor_tensor(pr(2), q[:, :, 0], q[:, :, 1], ALU.min))
                ch.done(dve.tensor_tensor(pr(3), q[:, :, 2], q[:, :, 3], ALU.min)).sync()
                step(dve.tensor_tensor(pr(3), pr(2), pr(3), ALU.max))
                step(dve.tensor_tensor(pr(4), pr(0), pr(1), ALU.min))
                step(dve.tensor_tensor(pr(3), pr(3), pr(4), ALU.max))
                step(dve.tensor_tensor(pr(0), pr(0), pr(1), ALU.max))
                ch.done(dve.memset(gs8[:, 0:nt, 4:8], -BIG))
                step(dve.tensor_tensor(gs8[:, 0:nt, 0:4], pr(0).rearrange("p (a b) -> p a b", b=4), pr(3).rearrange("p (a b) -> p a b", b=4), ALU.add))

                def best(src):
                    for t in range(nt):
                        ch.done(dve.max(mx8[:, t, :], src[:, t, :]))
                    ch.sync()
                    for t in range(nt):
                        ch.done(dve.max_index(ix8[:, t, :], mx8[:, t, :], src[:, t, :]))
                    ch.sync()
                best(gs8)
                step(dve.tensor_copy(gidx[:, 0:nt].unsqueeze(2), ix8[:, 0:nt, 0:1]))
                grp = C("group_of").unsqueeze(1).to_broadcast([P, nt, NE])
                step(dve.tensor_tensor(tmp16[:, 0:nt, :], grp, gidx[:, 0:nt].unsqueeze(2).to_broadcast([P, nt, NE]), ALU.is_equal))
                step(dve.tensor_scalar(tmp16[:, 0:nt, :], tmp16[:, 0:nt, :], 1.0, BIG, ALU.subtract, ALU.mult))
                step(dve.tensor_tensor(sel_, sel_, tmp16[:, 0:nt, :], ALU.add))
                best(selb)
                step(dve.tensor_copy(eidx[:, 0:nt, :], ix8[:, 0:nt, 0:TOPK]))
                exi = C("expert").unsqueeze(1).to_broadcast([P, nt, NE])
                ohs = (oh0, oh1)
                for j in range(TOPK):
                    ch.done(dve.tensor_tensor(ohs[j][:, 0:nt, :], exi, eidx[:, 0:nt, j:j + 1].to_broadcast([P, nt, NE]), ALU.is_equal))
                ch.sync()
                dve.tensor_tensor(both[:, 0:nt, :], oh0[:, 0:nt, :], oh1[:, 0:nt, :], ALU.add).then_inc(s["r_mat"], 1)
                for j in range(TOPK):
                    step(dve.tensor_tensor(tmp16[:, 0:nt, :], sc_, ohs[j][:, 0:nt, :], ALU.mult))
                    step(dve.tensor_reduce(wts[:, 0:nt, j], tmp16[:, 0:nt, :], AX.X, ALU.add))
                step(dve.tensor_reduce(wsum[:, 0:nt], wts[:, 0:nt, :], AX.X, ALU.add))
                step(dve.reciprocal(wsum[:, 0:nt], wsum[:, 0:nt]))
                step(dve.tensor_tensor(wts[:, 0:nt, :], wts[:, 0:nt, :], wsum[:, 0:nt].unsqueeze(2).to_broadcast([P, nt, TOPK]), ALU.mult))
                dve.wait_ge(s["r_cum"], l + 1)
                ch.done(dve.memset(offs[:, 0, :], 0.0))
                step(dve.tensor_copy(row(tots[:, 0:nt, :]), B7[:, 0:nt * NE]))
                for t in range(1, nt):
                    step(dve.tensor_tensor(offs[:, t, :], offs[:, t - 1, :], tots[:, t - 1, :], ALU.add))
                step(dve.tensor_tensor(count_e, offs[:, nt - 1, :], tots[:, nt - 1, :], ALU.add))
                step(dve.tensor_tensor(cmp6[:, :, 0:nt], count_e.unsqueeze(2).to_broadcast([P, NE, nt]),
                                       C("tile_start")[:, 0:nt].unsqueeze(1).to_broadcast([P, NE, nt]), ALU.is_gt))
                step(dve.tensor_reduce(nblk, cmp6[:, :, 0:nt], AX.X, ALU.add))
                step(dve.tensor_tensor_scan(bend, ones[:, 0:NE], nblk, 0.0, ALU.mult, ALU.add))
                step(dve.tensor_tensor(bbase, bend, nblk, ALU.subtract))
                step(dve.tensor_scalar(bbase, bbase, float(P), None, ALU.mult))
                step(dve.tensor_tensor(row(posn[:, 0:nt, :]), B6[:, 0:nt * NE], row(offs[:, 0:nt, :]), ALU.add))
                step(dve.tensor_tensor(posn[:, 0:nt, :], posn[:, 0:nt, :], bbase.unsqueeze(1).to_broadcast([P, nt, NE]), ALU.add))
                for j in range(TOPK):
                    step(dve.tensor_tensor(tmp16[:, 0:nt, :], posn[:, 0:nt, :], ohs[j][:, 0:nt, :], ALU.mult))
                    step(dve.tensor_reduce(slotf[:, 0:nt, j], tmp16[:, 0:nt, :], AX.X, ALU.add))
                ch.done(dve.tensor_copy(tok_u, C("token")))
                step(dve.tensor_copy(slots[:, 0:nt, :], slotf[:, 0:nt, :]))
                dve.sem_inc(s["r_slots"], 1)
                nb = NBK[l]
                step(dve.tensor_tensor(cmpb[:, 0:nb, :], bend.unsqueeze(1).to_broadcast([P, nb, NE]),
                                       C("block")[:, 0:nb].unsqueeze(2).to_broadcast([P, nb, NE]), ALU.is_le))
                step(dve.tensor_reduce(bexp[:, 0:nb], cmpb[:, 0:nb, :], AX.X, ALU.add))
                step(dve.tensor_scalar(bexp[:, 0:nb], bexp[:, 0:nb], float(NE - 1), None, ALU.min))
                step(dve.tensor_copy(bexp_i[:, 0:nb], bexp[:, 0:nb]))
                even = cmpb[:, 0:nb // 2, 0]
                step(dve.tensor_tensor(even, C("block")[:, 0:nb:2], bend[:, NE - 1:NE].to_broadcast([P, nb // 2]), ALU.is_lt))
                step(dve.tensor_reduce(npair_f[:, 0:1], even, AX.X, ALU.add))
                for n in (1, 2):
                    ch.done(dve.tensor_scalar(npair_f[:, n:n + 1], npair_f[:, 0:1], float(n), None, ALU.subtract))
                ch.sync()
                step(dve.tensor_copy(npair_i, npair_f))
                dve.sem_inc(s["r_ready"], 1)
                R_START[0] += ch.n
                pairs, pairs_1, pairs_2 = pair_counts(dve, l)
                ge = lambda b: b + NBK[0] * l
                first_T("e_", ge(0), 0)

                def e_block(blk, u, b, more, first):
                    ffn("e_", ge(blk), b, more)
                    if not first:
                        dve.wait_ge(s[f"e_stored{b}"], 16 * (u + NBK[0] // 2 * l))
                    dve.tensor_copy(yb[b][:, 0:512], (S0, S1)[b][:, 0:512]).then_inc(s["e_y_v"], 1)

                for b in range(2):
                    e_block(b, 0, b, True, l == 0)
                with dve.Fori(1, pairs_1) as i:
                    for b in range(2):
                        e_block(2 * i + b, i, b, True, False)
                for b in range(2):
                    e_block(2 * pairs_2 + 2 + b, pairs_2 + 1, b, b == 0, False)
                dve.wait_ge(s["e_y_v"], 2 * pairs_1 + 2 + NBK[0] * l)
                spare_pairs(dve, l, pairs, [("e_t_v", 2), ("v_e", 6), ("e_hid", 2), ("e_htv", 2), ("e_y_v", 2)])
                def c_tile(t, u, b, stream, first):
                    ch = Count(dve, s["v_c"], 3 * g(t))
                    dve.wait_ge(s[f"c_y_in{b}"], 16 * TOPK * (u + 1 + T // 2 * l))
                    w = lambda j: wts[:, span(t, 1), j]
                    y1, y2 = y12[b][:, 0, :], y12[b][:, 1, :]
                    ch.done(dve.tensor_scalar(y1, y1, w(0), None, ALU.mult)).sync()
                    ch.done(dve.scalar_tensor_tensor(y1, y2, w(1), y1, ALU.mult, ALU.add)).sync()
                    ch.done(dve.tensor_tensor(y1, y1, g2[:, stream, :], ALU.mult)).sync()
                    assert ch.n == 3
                    dve.wait_ge(s[f"c_x_in{b}"], 16 * (u + 1 + T // 2 * l))
                    if not first:
                        dve.wait_ge(s[f"c_stored{b}"], 16 * (u + T // 2 * l))
                    if l < DEPTH - 1:
                        dve.tensor_tensor(x3b[b], y1, x2b[b], ALU.add).then_inc(s["c_x3"], 1)
                    else:
                        dve.tensor_tensor(x3b[b], y1, x2b[b], ALU.add).then_inc(c_sum, 1)
                        dve.wait_ge(s["c_rs"], t + 1)
                        dve.scalar_tensor_tensor(x3b[b], x3b[b], h2s[:, 3:4], fgain, ALU.mult, ALU.mult).then_inc(s["c_x3"], 1)
                if l < DEPTH - 1:
                    for b in range(2):
                        c_tile(b, 0, b, 0, True)
                    for t in range(2, nt):
                        c_tile(t, t // 2, t % 2, int(t >= TL), False)
                else:
                    dve.wait_ge(fgain_in, 16)
                    for t in range(nt):
                        c_tile(t, t // 2, t % 2, 0, False)


_INS = ["x", "c", "ctx", "c_ctx", "w_mod", "b_mod", "norm_mix", "norm_ffn", "w_in", "w_out",
        "gqa_q_norm", "gqa_k_norm", "na_rel_bias", "diff_lq1", "diff_lk1", "diff_lq2", "diff_lk2", "diff_subln",
        "mla_q_norm", "mla_w_q_up", "mla_kv_norm", "mla_w_kv_up", "router_w", "router_b",
        "moe_w_gate", "moe_w_up", "moe_w_down", "shared_w_gate", "shared_w_up", "shared_w_down", "final_norm"]


def kernel(**inputs):
    import concourse.bacc as bacc
    from concourse.bass_utils import run_bass_kernel_spmd

    nc = bacc.Bacc("TRN2", target_bir_lowering=False, num_devices=1)
    arrays, A = {}, {}
    for name in _INS:
        a = np.ascontiguousarray(inputs[name])
        arrays[f"in_{name}"] = a
        A[name] = nc.dram_tensor(f"in_{name}", a.shape, mybir.dt.from_np(a.dtype), kind="ExternalInput").ap()
    out = nc.dram_tensor("out", (1, SEQ, D), F32, kind="ExternalOutput").ap()
    program(nc, A, out)
    return run_bass_kernel_spmd(nc, [arrays], core_ids=[0]).results[0]["out"]
```

```python
import math
from contextlib import ExitStack

import numpy as np
import concourse.bass as bass
from concourse import mybir

ALU = mybir.AluOpType
ACT = mybir.ActivationFunctionType
AX = mybir.AxisListType
F32 = mybir.dt.float32
BF16 = mybir.dt.bfloat16
I32 = mybir.dt.int32
U32 = mybir.dt.uint32

P = 128
D = 1024
DEPTH = 2
SEQ = 512
CTX = 256
NTOK = SEQ + CTX
T = NTOK // P
TL = SEQ // P
TC = CTX // P
KT = D // P
GRID_W = 64
GRID_H = SEQ // GRID_W
EPS = 1e-6
IN_COLS = 2400
UCH = 480
NCH = IN_COLS // UCH
MCH = 512
NMCH = 6 * D // MCH
NE = 16
NG = 4
DE = 256
BIG = 1e30
TOPK = 2
NBK = [-(-((TOPK * n + NE * (P - 1)) // P) // 2) * 2 for n in (NTOK, SEQ)]
HEADS = 20

W_RUNS = [(512, 256), (2048, 192), (1280, 256), (0, 256),
          (256, 256), (768, 512), (1536, 512), (2240, 160)]
NQ, CQ, DQ, AQ, AK, AV, NK_, NV, DK, DV, CKV, KPE = (
    0, 256, 448, 704, 960, 1088, 1216, 1472, 1728, 1984, 2240, 2368)
Q_CH = 2
ST_AK, ST_DK, ST_AQ, ST_DQ, ST_MK, ST_MQ, ST_W = 0, 128, 384, 640, 896, 1280, 1664
SL_NK, SL_NQ, SL_AK, SL_DK, SL_AQ, SL_DQ, SL_MK, SL_MQ, NSL = 0, 2, 4, 5, 7, 9, 11, 15, 19
V_A, V_N, V_D, V_M, V_W = 0, 128, 384, 640, 896
PROD = {1: 0, 3: 1, 5: 2, 7: 3, **{m: m - 4 for m in range(8, HEADS)}}
NP = len(PROD)
ROUNDS = 8


def constants():
    parts, at = [], {}
    width = 0

    def add(name, a):
        nonlocal width
        a = np.asarray(a, np.float32).reshape(P, -1)
        at[name] = (width, width + a.shape[1])
        parts.append(a)
        width += a.shape[1]

    p = np.arange(P)
    add("ident", np.eye(P))
    add("ones", np.ones((P, P)))
    add("before", p[:, None] < p[None, :])
    for rot, heads in ((64, "64"), (32, "32")):
        half = rot // 2
        freqs = (np.float32(10000.0) ** (-np.arange(0, half, 2, dtype=np.float32) / np.float32(half))).astype(np.float32)
        cos = np.ones((NTOK, rot), np.float32)
        sin = np.zeros((NTOK, rot), np.float32)
        tok = np.arange(SEQ)
        for a, place in enumerate((tok // GRID_W, tok % GRID_W)):
            ang = place.astype(np.float32)[:, None] * freqs
            n = freqs.size
            o = a * half
            cos[:SEQ, o:o + n] = cos[:SEQ, o + n:o + 2 * n] = np.cos(ang)
            sin[:SEQ, o:o + n] = -np.sin(ang)
            sin[:SEQ, o + n:o + 2 * n] = np.sin(ang)
        add("cos" + heads, cos.reshape(T, P, rot).transpose(1, 0, 2))
        add("sin" + heads, sin.reshape(T, P, rot).transpose(1, 0, 2))
    col = p % GRID_W
    lo = np.clip(col - 8, 0, GRID_W - 16)[:, None]
    keys = np.arange(GRID_W)[None, :]
    add("window", np.where((keys >= lo) & (keys < lo + 16), 0.0, -BIG))
    add("pick", (p[:, None] % 32) == np.arange(2)[None, :])
    add("expert", np.broadcast_to(np.arange(NE), (P, NE)))
    add("group_of", np.broadcast_to(np.arange(NE) // (NE // NG), (P, NE)))
    add("block", np.broadcast_to(np.arange(NBK[0] + 1), (P, NBK[0] + 1)))
    add("place", np.broadcast_to(p, (P, P)))
    add("tile_start", np.broadcast_to(P * np.arange(T), (P, T)))
    add("token", np.arange(T)[None, :] * P + p[:, None])
    return np.concatenate(parts, 1), at


def span(start, size):
    return slice(start, start + size) if isinstance(start, int) else bass.ds(start, size)


class Count:

    def __init__(self, eng, sem, start):
        self.eng, self.sem, self.start, self.n = eng, sem, start, 0

    def done(self, ins):
        ins.then_inc(self.sem, 1)
        self.n += 1
        return self

    def sync(self):
        self.eng.wait_ge(self.sem, self.start + self.n)


def program(nc, A, out):
    table, at = constants()
    cst_d = nc.inline_tensor(table, name="shape_constants").ap()
    dram = lambda n, s, d=F32: nc.dram_tensor(n, s, d, kind="Internal").ap()
    x_in = [A["tokens"]] + [dram(f"x_in{l}", (NTOK, D)) for l in range(1, DEPTH)]
    x_mix = [dram(f"x_mix{l}", ((NTOK, SEQ)[l], D)) for l in range(DEPTH)]
    h2_d = [dram(f"h2_{l}", ((NTOK, SEQ)[l], D)) for l in range(DEPTH)]
    x_ffn = [dram(f"x_ffn{l}", ((NTOK, SEQ)[l], D)) for l in range(DEPTH)]
    y_d = [dram(f"y{l}", (NBK[l] * P, D)) for l in range(DEPTH)]
    REL_ROW = DEPTH * P
    REL_COPY = (4 * 15 + 2) * REL_ROW
    rel_d = dram("rel_padded", (1, REL_COPY))
    rel_copies = dram("rel_copies", (GRID_W, REL_COPY))
    mod_d = [dram(f"mod{l}", (2, 6 * D)) for l in range(DEPTH)]

    with ExitStack() as ctx:
        sb = lambda n, s, d=F32: ctx.enter_context(nc.sbuf_tensor(n, s, d))
        pb = lambda n, s: ctx.enter_context(nc.psum_tensor(n, s, F32))
        sem = lambda n: ctx.enter_context(nc.semaphore(n))

        cst = sb("cst", [P, table.shape[1]])
        C = lambda n: cst[:, at[n][0]:at[n][1]]
        ident, ones = C("ident"), C("ones")
        cos = {64: C("cos64").rearrange("p (t c) -> p t c", t=T), 32: C("cos32").rearrange("p (t c) -> p t c", t=T)}
        sin = {64: C("sin64").rearrange("p (t c) -> p t c", t=T), 32: C("sin32").rearrange("p (t c) -> p t c", t=T)}
        csrc = sb("csrc", [P, 2, KT])
        ctmp = sb("ctmp", [P, 2, KT])
        cs = sb("cs", [P, KT, 32])
        modcol = sb("modcol", [P, T, 2, KT])
        gains = sb("gains", [P, 6, 64])
        lgain = sb("lgain", [P, 320])
        sumsq = sb("sumsq", [P, 2])
        meansq = sb("meansq", [P, 2])
        rstd = sb("rstd", [P, 2])
        s8 = sb("s8", [P, 8])
        m8 = sb("m8", [P, 8])
        r8 = sb("r8", [P, 8])
        halfs = sb("halfs", [P, 24])
        inv8, eps8 = halfs[:, 8:16], halfs[:, 16:24]
        nmax = sb("nmax", [P, HEADS])
        rsum = sb("rsum", [P, HEADS])
        rinv = sb("rinv", [P, HEADS])
        nlam = sb("nlam", [P, 4])
        dtmp = sb("dtmp", [P, 128])
        dstat = sb("dstat", [P, 8])
        ratio = sb("ratio", [P, 4])
        subg = sb("subg", [P, 64])
        lamb = dtmp[:, :].rearrange("p (a b) -> p a b", a=4)
        h2s = sb("h2s", [P, 4])

        ARENA = 49928
        arena = sb("arena", [P, ARENA])

        def region(start):
            at_ = [start]

            def take(*shape, parts=P):
                n = int(np.prod(shape))
                a = arena[0:parts, at_[0]:at_[0] + n]
                at_[0] += n
                assert at_[0] <= ARENA, (shape, at_[0])
                if len(shape) == 2:
                    a = a.rearrange("p (a b) -> p a b", a=shape[0])
                return a
            take.at = at_
            return take

        take = region(0)
        win = take(KT, IN_COLS)
        WIN_END = take.at[0]
        qk = take(NSL, NTOK)
        vals = take(T, V_W)
        QKV_END = take.at[0]
        U = take(IN_COLS)
        st = take(ST_W)
        xt = take(D)
        junk = take(D // 2).bitcast(BF16)
        hT = [take(KT, P) for _ in range(2)]
        tmpA, tmpB = take(512), take(512)
        wqu = take(2, 384)
        wkvu = take(512)
        MIX_END = take.at[0]
        lor = take(320)
        lorT = take(3, P)
        kper = take(32)
        mod_bufs = []
        for l in range(DEPTH):
            take = region(0 if l else WIN_END)
            mod_bufs.append(([take(KT, MCH) for _ in range(2)], [take(MCH) for _ in range(2)],
                             take(6 * D, parts=2), take(2, D, parts=2)))
            if l == 0:
                relpad = take(DEPTH * P, parts=62)
                assert take.at[0] <= QKV_END
        MOD_END = take.at[0]

        take = region(0)
        wout = take(KT, D)
        vec = take(6, D)
        bias_t = take(4, 16 * GRID_W)
        Pb = [take(NTOK)]
        assert take.at[0] <= WIN_END
        take = region(QKV_END)
        Qs = take(HEADS, P)
        Pb += [take(NTOK) for _ in range(2)]
        PTs = [take(T, P) for _ in range(2)]
        O = take(D)
        OT = take(KT, P)
        xa, xb, h2b = take(D), take(D), take(D)
        take = region(WIN_END)
        swgu = take(KT, 512)
        swd = take(2, D)
        hs = [take(D) for _ in range(2)]
        hT2_all, gex_all, hid_all = take(2 * D), take(2 * DE), take(2 * DE)
        hT2 = [hT2_all[:, b * D:(b + 1) * D].rearrange("p (a b) -> p a b", a=KT) for b in range(2)]
        gex = [gex_all[:, b * DE:(b + 1) * DE] for b in range(2)]
        hid = [hid_all[:, b * DE:(b + 1) * DE] for b in range(2)]
        hidT = [take(2, P) for _ in range(2)]
        x1b = [take(D) for _ in range(2)]
        ob = [take(D) for _ in range(2)]
        G2_START = take.at[0]
        g2 = take(2, D)
        rw = take(KT, NE)
        rb = take(NE)
        wgu = [take(2, KT * DE) for _ in range(2)]
        wdn = [take(2, D) for _ in range(2)]
        xg, XT, yb = hs, hT2, x1b
        assert take.at[0] >= MIX_END
        wts = take(T, 2)
        slots = take(T, 2).bitcast(U32)
        slotf = take(T, 2)
        block_of = take(T, 2)
        gidx = take(T)
        eidx = take(T, 2)
        wsum = take(T)
        nblk, bend, bbase, count_e = take(NE), take(NE), take(NE), take(NE)
        bexp = take(NBK[0] + 1)
        bexp_i = take(NBK[0] + 1).bitcast(I32)
        npair_f = take(3)
        npair_i = take(3).bitcast(I32)
        table_u = take(NBK[0] + 1).bitcast(U32)
        idx1 = [take(1).bitcast(U32) for _ in range(2)]
        idx2 = [take(2).bitcast(U32) for _ in range(2)]
        from_block = gex_all[:, 0:TOPK * T * (NBK[0] + 1)].rearrange("p (a b) -> p a b", a=TOPK * T)
        in_block = hid_all[:, 0:TOPK * T * NBK[0]].rearrange("p (a b) -> p a b", a=TOPK * T)
        in_place = hT2_all[:, 0:TOPK * T * P].rearrange("p (a b) -> p a b", a=TOPK * T)
        take = region(MOD_END)
        lg = take(T, NE)
        score, selb, oh0, oh1, both, tmp16, tots, offs, posn = [take(T, NE) for _ in range(9)]
        gs8, mx8 = take(T, 8), take(T, 8)
        ix8 = take(T, 8).bitcast(U32)
        pair = take(5, T * NG)
        cmp6 = take(NE, T)
        cmpb = take(NBK[0] + 1, NE)
        assert take.at[0] <= WIN_END, take.at[0]
        take = region(WIN_END)
        y12 = [take(2, D) for _ in range(2)]
        x2b = [take(D) for _ in range(2)]
        x3b = [take(D) for _ in range(2)]
        fgain = ob[0]
        c_junk = [ob[1], hT2_all[:, D:2 * D]]
        assert take.at[0] <= min(G2_START, QKV_END)

        S0, S1, PT = pb("S0", [P, 1024]), pb("S1", [P, 1024]), pb("PT", [P, 1024])
        B6, B7 = pb("B6", [P, 512]), pb("B7", [P, 512])
        ubank = [S0[:, 0:512], S0[:, 512:1024], S1[:, 0:512], S1[:, 512:1024], B6[:, :]]

        consts_in, cond_in = sem("consts_in"), sem("cond_in")
        exp_c, cs_ready = sem("exp_c"), sem("cs_ready")
        halfs_set = sem("halfs_set")
        relpad_set, relpad_in, rel_stored, fgain_in = sem("relpad_set"), sem("relpad_in"), sem("rel_stored"), sem("fgain_in")
        c_sum = sem("c_sum")
        UNITS = ["exp_done", "p_tr", "pt_v", "pt_s", "pv_done", "o_evac"]
        v_init = sem("v_init")
        NAMES = ["mod_w_in0", "mod_w_in1", "mod_rows_in", "mod_mm", "mod_part", "mod_sel", "mod_row", "mod_gain", "mod_stored",
                 "modcol_in", "wsmall_in", "x_in", "ssq", "rstd_ready", "xn_done", "hT_tr", "hT_evac", "u_mm", "u_evac",
                 "v_copied", "u_used", "stats", "r8_ready", "lor_ready", "st_ready", "st_m_ready", "round_tr", "round_evac",
                 "v_prep", "g_prep", "mean_x",
                 "bias_in", "lam_in", "bias_ready", "wout_in", "vec_in", "lam_sum", "lam_exp", "v_lam",
                 "xa_in", "qs_ready", "scored", "neg_max", "exp_done", "p_tr", "pt_v", "pt_s", "pv_done", "o_evac",
                 "v_o", "d_stat", "d_rs", "g_att", "o_all", "ot_tr", "ot_v", "ot_s", "op_mm", "res_mul", "x1_ready", "x1_sq",
                 "h2_ready", "x1_stored", "h2_stored",
                 "s_w_in", "hs_in0", "hs_in1", "x1_in0", "x1_in1", "s_tr", "s_t_v", "s_t_s", "s_rt", "s_lg", "s_g", "s_u", "s_ex",
                 "v_s", "s_hid", "s_ht", "s_htv", "s_d", "s_ob", "s_x2", "s_stored0", "s_stored1",
                 "r_exp", "v_r", "r_mat", "r_cum", "r_slots", "r_hot", "comb_done", "g_x", "r_tab", "r_ready",
                 "e_w_in0", "e_w_in1", "e_idx", "spare_seen", "e_filled", "e_tr", "e_t_v", "e_t_s", "e_g", "e_u", "e_ex", "v_e",
                 "e_hid", "e_ht", "e_htv", "e_d", "e_y_v", "e_y_s", "e_stored0", "e_stored1",
                 "c_idx", "idx_seen", "c_y_in0", "c_y_in1", "c_x_in0", "c_x_in1", "v_c", "c_x3", "c_stored0", "c_stored1", "c_sq", "c_mean",
                 "c_rs"]
        s = {n: sem(n) for n in NAMES}
        e_x_in = [[sem(f"e_x_in{b}_{l}") for b in range(2)] for l in range(DEPTH)]
        s["win_in"] = [sem(f"win_in{c}") for c in range(NCH)]

        FIRST_STEPS = [("mod", 4), ("mod", 5), ("proj", 0), ("mod", 6), ("proj", 1), ("mod", 7), ("mod", 8), ("proj", 2),
                       ("mod", 9), ("mod", 10), ("mod", 11), ("proj", 3), ("proj", 4)]

        def mod_banks(n):
            if n == 4:
                return B6[:, :], S1[:, 0:512]
            if n == 5:
                return B7[:, :], S1[:, 512:1024]
            return (B7[:, :] if n % 2 else PT[:, 0:512]), PT[:, 512:1024]

        def win_parts(c):
            ends = np.cumsum([width for _, width in W_RUNS])
            return sum(int(e - w < (c + 1) * UCH and e > c * UCH) for e, (_, w) in zip(ends, W_RUNS))

        def over_tiles(eng, l, att):
            att(0, NTOK, None, False)
            with eng.Fori(1, TL if l == 0 else TL - 1) as t:
                att(t, NTOK, NTOK, False)
            if l == 0:
                att(TL, CTX, NTOK, False)
                for t in range(TL + 1, T):
                    att(t, CTX, CTX, t == T - 1)
                att(T, None, CTX, False)
            else:
                att(TL - 1, NTOK, NTOK, True)
                att(TL, None, NTOK, False)

        def pair_counts(eng, l):
            eng.wait_ge(s["r_ready"], l + 1)
            least = TOPK * (NTOK, SEQ)[l] // P // 2
            return [eng.value_load(npair_i[0:1, n:n + 1], min_val=least - n, max_val=NBK[l] // 2 - n) for n in range(3)]

        def spare_pairs(eng, l, pairs, counts):
            eng.sem_inc(s["spare_seen"], 1)
            with eng.Fori(pairs, NBK[l] // 2):
                for name, n in counts:
                    eng.sem_inc(s[name], n)

        def product_at(k, lag, nk, prev):
            m = k - lag
            moved = {(2, 5): None, (2, 6): 3, (3, 4): None, (3, 5): 1, (3, 6): None, (3, 7): 3}
            if (lag, k) in moved:
                m = moved[lag, k]
                return (PROD[m], m, nk) if nk and m else None
            if m < 0 and prev:
                return PROD[HEADS + m] - NP, HEADS + m, prev
            if m >= 0 and nk and m in PROD:
                return PROD[m], m, nk
            return None

        block = ctx.enter_context(nc.Block())

        @block.sync
        def _(sp):
            sp.dma_start(cst[:, :], cst_d).then_inc(consts_in, 16)
            sp.dma_start(csrc[:, 0, :], A["c"].rearrange("a (p k) -> (a p) k", k=KT)).then_inc(cond_in, 16)
            sp.dma_start(csrc[:, 1, :], A["c_ctx"].rearrange("(p k) -> p k", k=KT)).then_inc(cond_in, 16)
            for u in range(2):
                for n in UNITS:
                    sp.sem_inc(s[n], 1)
            for l in range(DEPTH):
                g = lambda t: t + T * l

                def mod_rows(l):
                    _, _, modrow, nrow = mod_bufs[l]
                    for q in range(2):
                        sp.dma_start(modrow[q:q + 1, :], A["b_mod"][l:l + 1, :]).then_inc(s["mod_rows_in"], 16)
                        sp.dma_start(nrow[q:q + 1, 0, :], A["norm_mix"][l:l + 1, :]).then_inc(s["mod_rows_in"], 16)
                        sp.dma_start(nrow[q:q + 1, 1, :], A["norm_ffn"][l:l + 1, :]).then_inc(s["mod_rows_in"], 16)

                def mod_load(l, n, b, first):
                    if not first:
                        sp.wait_ge(s["mod_mm"], n - 1 + NMCH * l)
                    src = A["w_mod"][l].rearrange("(p k) n -> p k n", k=KT)[:, :, span(n * MCH, MCH)]
                    sp.dma_start(mod_bufs[l][0][b], src).then_inc(s[f"mod_w_in{b}"], 16)

                def mod_store(l, half, meanwhile=None):
                    cols = (slice(0, 2 * D), slice(2 * D, 6 * D))[half]
                    sp.wait_ge(s["mod_gain"], 2 * l + half + 1)
                    sp.dma_start(mod_d[l][:, cols], mod_bufs[l][2][:, cols]).then_inc(s["mod_stored"], 16)
                    if meanwhile:
                        meanwhile()
                    sp.wait_ge(s["mod_stored"], 16 * (2 * l + half + 1))

                def win_load(l, c):
                    w_in = A["w_in"][l].rearrange("(p k) n -> p k n", k=KT)
                    at_ = 0
                    for first, width in W_RUNS:
                        lo, hi = max(at_, c * UCH), min(at_ + width, (c + 1) * UCH)
                        if lo < hi:
                            src = w_in[:, :, first + lo - at_:first + hi - at_]
                            sp.dma_start(win[:, :, lo:hi], src).then_inc(s["win_in"][c], 16)
                        at_ += width

                def modcol_load(l):
                    for t in range(T):
                        src = mod_d[l][int(t >= TL), 0:2 * D].rearrange("(w p k) -> p w k", w=2, k=KT)
                        sp.dma_start(modcol[:, t], src).then_inc(s["modcol_in"], 16)

                def x_load(l, t, first):
                    if not first:
                        sp.wait_ge(s["hT_tr"], t + T * l)
                    sp.dma_start(xt, x_in[l][span(t * P, P), :]).then_inc(s["x_in"], 16)

                def gain_load(l):
                    for n, w in enumerate(("diff_lq1", "diff_lk1", "diff_lq2", "diff_lk2")):
                        sp.dma_start(lamb[:, n, :], A[w][l].partition_broadcast(P)).then_inc(s["lam_in"], 16)
                    sp.dma_start(subg[:, :], A["diff_subln"][l].partition_broadcast(P)).then_inc(s["lam_in"], 16)
                    for h in range(6):
                        gain = A["gqa_q_norm"] if h < 4 else A["gqa_k_norm"]
                        sp.dma_start(gains[:, h, :], gain[l].partition_broadcast(P)).then_inc(s["wsmall_in"], 16)
                    sp.dma_start(lgain[:, 0:192], A["mla_q_norm"][l].partition_broadcast(P)).then_inc(s["wsmall_in"], 16)
                    sp.dma_start(lgain[:, 192:320], A["mla_kv_norm"][l].partition_broadcast(P)).then_inc(s["wsmall_in"], 16)

                def small_load(l):
                    sp.dma_start(wqu[0:96], A["mla_w_q_up"][l].rearrange("(k p) n -> p k n", p=96)).then_inc(s["wsmall_in"], 16)
                    sp.dma_start(wkvu, A["mla_w_kv_up"][l]).then_inc(s["wsmall_in"], 16)

                if l == 0:
                    mod_load(0, 0, 0, True)
                    mod_load(0, 1, 1, True)
                    mod_rows(0)
                    gain_load(0)
                    small_load(0)
                    sp.wait_ge(relpad_set, 1)
                    for layer in range(DEPTH):
                        sp.dma_start(relpad[1:61, layer * P + 48:layer * P + 79], A["na_rel_bias"][layer].rearrange("h a b -> (h a) b")).then_inc(relpad_in, 16)
                    sp.wait_ge(relpad_in, 16 * DEPTH)
                    sp.dma_start(rel_d.rearrange("o (a c) -> (o a) c", c=REL_ROW), relpad).then_inc(rel_stored, 16)
                    x_load(0, 0, True)
                    for n in range(2, 5):
                        mod_load(0, n, n % 2, False)
                    sp.wait_ge(rel_stored, 16)
                    mod_store(0, 0, lambda: mod_load(0, 5, 1, False))
                    modcol_load(0)
                    for kind, n in FIRST_STEPS[2:]:
                        if kind == "mod":
                            mod_load(0, n, n % 2, False)
                        else:
                            win_load(0, n)
                        if (kind, n) == ("proj", 0):
                            x_load(0, 1, False)

                if l == 0:
                    mod_store(0, 1)
                with sp.Fori(2, T) as t:
                    x_load(l, t, False)
                if l == 0:
                    sp.dma_start(rel_copies, rel_d[0].partition_broadcast(GRID_W)).then_inc(rel_stored, 16)

                sp.wait_ge(s["u_mm"], NCH * T * (l + 1))
                if l == 0:
                    sp.wait_ge(rel_stored, 32)
                for h in range(4):
                    for r2 in range(2):
                        src = bass.AP(rel_copies.tensor, (1 + h * 15 - r2) * REL_ROW + l * P + GRID_W - 1,
                                      [[REL_COPY - 1, GRID_W], [REL_ROW, 16], [1, GRID_W]])
                        dst = bias_t[r2 * GRID_W:(r2 + 1) * GRID_W, h, :]
                        sp.dma_start(dst.rearrange("p (j c) -> p j c", c=GRID_W), src).then_inc(s["bias_in"], 16)
                sp.dma_start(wout, A["w_out"][l].rearrange("(p k) n -> p k n", k=KT)).then_inc(s["wout_in"], 16)
                for stream in range(2):
                    for n, w in enumerate((2, 4, 3)):
                        sp.dma_start(vec[:, 3 * stream + n, :], mod_d[l][stream, w * D:(w + 1) * D].partition_broadcast(P)).then_inc(s["vec_in"], 16)
                with sp.Fori(TOPK * (NTOK, SEQ)[l] // P, NBK[l]) as blk:
                    sp.dma_start(y_d[l][span(blk * P, P), :].rearrange("p (a c) -> p a c", c=P),
                                 ones.unsqueeze(1).to_broadcast([P, KT, P])).then_inc(s["e_filled"], 16)
                sp.wait_ge(s["round_evac"], ROUNDS * T * (l + 1))

                nt = T if l == 0 else TL
                gend = T * l + nt

                def att_rows(t, first, meanwhile=None):
                    rows = span(t * P, P)
                    if not first:
                        sp.wait_ge(s["x1_ready"], g(t))
                    sp.dma_start(xa, x_in[l][rows, :]).then_inc(s["xa_in"], 16)
                    if meanwhile:
                        meanwhile()
                    sp.wait_ge(s["x1_ready"], g(t) + 1)
                    sp.dma_start(x_mix[l][rows, :], xb).then_inc(s["x1_stored"], 16)
                    sp.wait_ge(s["h2_ready"], g(t) + 1)
                    sp.dma_start(h2_d[l][rows, :], h2b).then_inc(s["h2_stored"], 16)

                def s_load(t, b, first):
                    if not first:
                        sp.wait_ge(s["s_tr"], g(t) - 1)
                    sp.dma_start(hs[b], h2_d[l][span(t * P, P), :]).then_inc(s[f"hs_in{b}"], 16)
                    if not first:
                        sp.wait_ge(s["s_x2"], g(t) - 1)
                    sp.dma_start(x1b[b], x_mix[l][span(t * P, P), :]).then_inc(s[f"x1_in{b}"], 16)

                def s_first_loads():
                    sp.wait_ge(s["pv_done"], NP * gend + 2)
                    for b in range(2):
                        s_load(b, b, True)
                    sp.dma_start(rw, A["router_w"].rearrange("(p k) n -> p k n", k=KT)).then_inc(s["s_w_in"], 16)
                    for name, e0 in (("shared_w_gate", 0), ("shared_w_up", DE)):
                        sp.dma_start(swgu[:, :, e0:e0 + DE], A[name][l].rearrange("(p k) n -> p k n", k=KT)).then_inc(s["s_w_in"], 16)
                    sp.dma_start(swd, A["shared_w_down"][l].rearrange("(p k) n -> p k n", k=2)).then_inc(s["s_w_in"], 16)
                    sp.dma_start(rb, A["router_b"].partition_broadcast(P)).then_inc(s["s_w_in"], 16)
                    for stream in range(2):
                        sp.dma_start(g2[:, stream, :], mod_d[l][stream, 5 * D:6 * D].partition_broadcast(P)).then_inc(s["s_w_in"], 16)

                att_rows(0, l == 0)
                with sp.Fori(1, nt - 1) as t:
                    att_rows(t, False)
                att_rows(nt - 1, False, s_first_loads)
                sp.wait_ge(s["h2_stored"], 16 * gend)
                sp.wait_ge(s["x1_stored"], 16 * gend)

                def s_store(t, b):
                    sp.wait_ge(s["s_x2"], g(t) + 1)
                    sp.dma_start(x_ffn[l][span(t * P, P), :], ob[b]).then_inc(s[f"s_stored{b}"], 16)

                if l == 0:
                    sp.wait_ge(s["res_mul"], 2 * gend)
                    sp.wait_ge(s["h2_ready"], gend)
                    mod_rows(1)
                    mod_load(1, 0, 0, True)
                    mod_load(1, 1, 1, True)
                    for t in range(nt):
                        mod_load(1, t + 2, t % 2, False)
                        s_store(t, t % 2)
                        if t + 2 < nt:
                            s_load(t + 2, t % 2, False)
                    for n in range(nt + 2, NMCH):
                        mod_load(1, n, n % 2, False)
                else:
                    with sp.Fori(0, nt // 2 - 1) as i:
                        for b in range(2):
                            s_store(2 * i + b, b)
                            s_load(2 * i + 2 + b, b, False)
                    for b in range(2):
                        s_store(nt - 2 + b, b)
                pairs, pairs_1, pairs_2 = pair_counts(sp, l)
                nb = NBK[l]
                ge = lambda b: b + NBK[0] * l

                def w_load(blk, b, first):
                    if not first:
                        sp.wait_ge(s["e_d"], ge(blk) - 1)
                    e = sp.value_load(bexp_i[0:1, span(blk, 1)], min_val=0, max_val=NE - 1)
                    for n, name in enumerate(("moe_w_gate", "moe_w_up")):
                        src = A[name][l].rearrange("e (p k) n -> e p (k n)", k=KT)[bass.ds(e, 1)].rearrange("o p n -> (o p) n")
                        sp.dma_start(wgu[b][:, n, :], src).then_inc(s[f"e_w_in{b}"], 16)
                    src = A["moe_w_down"][l].rearrange("e (p k) n -> e p (k n)", k=2)[bass.ds(e, 1)].rearrange("o p n -> (o p) n")
                    sp.dma_start(wdn[b].rearrange("p a b -> p (a b)"), src).then_inc(s[f"e_w_in{b}"], 16)

                def y_store(blk, b):
                    sp.wait_ge(s["e_y_v"], ge(blk) + 1)
                    sp.wait_ge(s["e_y_s"], ge(blk) + 1)
                    sp.dma_start(y_d[l][span(blk * P, P), :], yb[b]).then_inc(s[f"e_stored{b}"], 16)

                w_load(0, 0, l == 0)
                sp.wait_ge(s["e_idx"], 2 + NBK[0] * l)
                w_load(1, 1, l == 0)
                sp.wait_ge(s["e_filled"], 16 * sum(NBK[i] - TOPK * (NTOK, SEQ)[i] // P for i in range(l + 1)))
                if l == 0:
                    gain_load(1)
                    mod_store(1, 0)
                    modcol_load(1)
                    mod_store(1, 1)
                with sp.Fori(0, pairs_1) as i:
                    for b in range(2):
                        w_load(2 * i + 2 + b, b, False)
                        y_store(2 * i + b, b)
                if l == 0:
                    win_load(1, 0)
                for b in range(2):
                    sp.wait_ge(s[f"s_stored{b}"], 8 * gend if l == 0 else 16 * (T // 2 + TL // 2))
                for b in range(2):
                    sp.dma_start(x2b[b], x_ffn[l][b * P:(b + 1) * P, :]).then_inc(s[f"c_x_in{b}"], 16)
                if l == DEPTH - 1:
                    sp.dma_start(fgain, A["final_norm"].partition_broadcast(P)).then_inc(fgain_in, 16)
                for b in range(2):
                    y_store(2 * pairs_2 + 2 + b, b)
                for b in range(2):
                    sp.wait_ge(s[f"e_stored{b}"], 16 * (pairs_1 + 1 + NBK[0] // 2 * l))
                    sp.sem_inc(s["spare_seen"], 1)
                spare_pairs(sp, l, pairs, [("e_w_in0", 48), ("e_w_in1", 48), ("e_stored0", 16), ("e_stored1", 16)])

                gc = lambda t: t + T * l
                dst = (lambda rows: x_in[l + 1][rows, :]) if l < DEPTH - 1 else (lambda rows: out[0, rows, :])

                def c_store(t, b):
                    sp.wait_ge(s["c_x3"], gc(t) + 1)
                    src = xt if l == 0 and isinstance(t, int) and t == 0 else x3b[b]
                    sp.dma_start(dst(span(t * P, P)), src).then_inc(s[f"c_stored{b}"], 16)

                def c_next(t, b):
                    c_store(t, b)
                    sp.dma_start(x2b[b], x_ffn[l][span((t + 2) * P, P), :]).then_inc(s[f"c_x_in{b}"], 16)

                if l == 0:
                    small_load(1)
                    c_next(0, 0)
                    c_next(1, 1)
                    win_load(1, 1)
                    c_next(2, 0)
                    win_load(1, 2)
                    c_next(3, 1)
                    sp.wait_ge(s["c_stored1"], 16)
                    x_load(1, 1, False)
                    win_load(1, 3)
                    win_load(1, 4)
                else:
                    for t in range(nt - 2):
                        sp.wait_ge(c_sum, t + 1)
                        sp.dma_start(x2b[t % 2], x_ffn[l][(t + 2) * P:(t + 3) * P, :]).then_inc(s[f"c_x_in{t % 2}"], 16)
                        c_store(t, t % 2)
                for b in range(2):
                    c_store(nt - 2 + b, b)
                for b in range(2):
                    sp.wait_ge(s[f"c_stored{b}"], 16 * (gend // 2))

        @block.scalar
        def _(act):
            act.wait_ge(cond_in, 32)
            act.activation(ctmp[:, :, :], csrc[:, :, :], ACT.Exp, scale=-1.0).then_inc(exp_c, 1)
            for l in range(DEPTH):
                g = lambda t: t + T * l

                def square(t, first):
                    if l and first:
                        act.wait_ge(s["c_x3"], 1)
                    else:
                        act.wait_ge(s["x_in"], 16 * (g(t) + 1 - l))
                    if l or not first:
                        act.wait_ge(s["rstd_ready"], g(t))
                    act.activation(junk, xt, ACT.Square, scale=D ** -0.5, accum_out=sumsq[:, 0:1]).then_inc(s["ssq"], 1)

                def evac_hT(t, b):
                    act.wait_ge(s["hT_tr"], g(t) + 1)
                    for j in range(KT):
                        ins = act.activation(hT[b][:, j, :], PT[:, j * P:(j + 1) * P], ACT.Identity,
                                             bias=modcol[:, span(t, 1), 0, j], scale=modcol[:, span(t, 1), 1, j])
                    ins.then_inc(s["hT_evac"], 1)

                def evac_u(t, c, c0, first):
                    act.wait_ge(s["u_mm"], NCH * g(t) + c + 1)
                    if c == c0 and not first:
                        act.wait_ge(s["u_used"], g(t))
                        act.wait_ge(s["v_copied"], g(t))
                        act.wait_ge(s["round_tr"], ROUNDS * (g(t) - 1) + 1)
                    act.activation(U[:, c * UCH:(c + 1) * UCH], ubank[c][:, 0:UCH], ACT.Copy).then_inc(s["u_evac"], 1 + c if c == c0 else 1)

                def tile(t, b, first, last, c0=0):
                    if not last:
                        square(t + 1, False)
                    for c in range(c0, NCH - 1):
                        evac_u(t, c, c0, first)
                    if not last:
                        evac_hT(t + 1, 1 - b)
                    evac_u(t, NCH - 1, c0, first)

                square(0, True)
                act.wait_ge(s["modcol_in"], 16 * T * (l + 1))
                evac_hT(0, 0)
                tile(0, 0, True, False)
                if l == 0:
                    with act.Fori(0, (T - 2) // 2) as i:
                        tile(2 * i + 1, 1, False, False)
                        tile(2 * i + 2, 0, False, False)
                    tile(T - 1, 1, False, True)
                else:
                    for t in range(1, T):
                        tile(t, t % 2, False, t == T - 1, Q_CH if t >= TL else 0)

                act.wait_ge(s["lam_sum"], l + 1)
                act.activation(nlam[:, 0:2], nlam[:, 2:4], ACT.Exp).then_inc(s["lam_exp"], 1)

                def att(t, nk, prev, last):
                    for k in range(HEADS):
                        if nk:
                            act.wait_ge(s["neg_max"], HEADS * g(t) + k + 1)
                            if k >= 3 and k - 3 in PROD:
                                act.wait_ge(s["p_tr"], NP * g(t) + PROD[k - 3] + 3)
                            elif k >= 3:
                                act.wait_ge(s["comb_done"], 4 * g(t) + (k - 3) // 2 + 1)
                            elif prev:
                                act.wait_ge(s["p_tr"], NP * g(t) - NP + PROD[(18, 19, 17)[k]] + 3)
                            act.activation(Pb[k % 3][:, 0:nk], (S0, S1)[k % 2][:, 0:nk], ACT.Exp, bias=nmax[:, k:k + 1],
                                           accum_out=rsum[:, k:k + 1]).then_inc(s["exp_done"], 1)
                        if k == 5 and prev:
                            act.wait_ge(s["ot_tr"], g(t))
                            act.activation(OT[:, 4:8, :].rearrange("p a b -> p (a b)"), PT[:, 512:1024], ACT.Copy).then_inc(s["ot_s"], 1)
                        at_T = product_at(k, 2, nk, prev)
                        if at_T:
                            j, _, n = at_T
                            h = 4 if n == NTOK else 1
                            act.wait_ge(s["p_tr"], NP * g(t) + j + 3)
                            act.wait_ge(s["pv_done"], NP * g(t) + j + 1)
                            act.activation(PTs[j % 2][:, h:n // P, :].rearrange("p a b -> p (a b)"), PT[:, 512:512 + n - h * P],
                                           ACT.Copy).then_inc(s["pt_s"], 1)
                        if k == 18 and prev:
                            act.wait_ge(s["x1_ready"], g(t))
                            act.wait_ge(s["h2_stored"], 16 * (g(t) - 1))
                            act.activation(h2b, xb, ACT.Square, scale=D ** -0.5, accum_out=h2s[:, 0:1]).then_inc(s["x1_sq"], 1)

                over_tiles(act, l, att)
                nt = T if l == 0 else TL
                gend = T * l + nt

                def ffn(m, gi, b, more):
                    act.wait_ge(s[m + "g"], gi + 1)
                    act.activation(gex[b], (S0, S1)[b][:, 0:DE], ACT.Exp, scale=-1.0).then_inc(s[m + "ex"], 1)
                    if more:
                        act.wait_ge(s[m + ("tr")], gi + 2)
                        act.activation((hT2, XT)[m == "e_"][1 - b][:, 4:8, :].rearrange("p a b -> p (a b)"), PT[:, 512:1024], ACT.Copy).then_inc(s[m + "t_s"], 1)

                def first_T(m, gi, b):
                    act.wait_ge(s[m + "tr"], gi + 1)
                    act.activation((hT2, XT)[m == "e_"][b][:, 4:8, :].rearrange("p a b -> p (a b)"), PT[:, 512:1024], ACT.Copy).then_inc(s[m + "t_s"], 1)

                first_T("s_", g(0), 0)
                with act.Fori(0, nt // 2 - 1) as i:
                    for b in range(2):
                        ffn("s_", g(2 * i + b), b, True)
                ffn("s_", g(nt - 2), 0, True)
                ffn("s_", g(nt - 1), 1, False)
                act.wait_ge(s["s_lg"], gend)
                act.activation(score[:, 0:nt, :], lg[:, 0:nt, :], ACT.Exp, scale=-1.0).then_inc(s["r_exp"], 1)
                act.wait_ge(s["s_x2"], gend)
                pairs, pairs_1, pairs_2 = pair_counts(act, l)
                ge = lambda b: b + NBK[0] * l
                first_T("e_", ge(0), 0)

                def e_out(blk, b):
                    act.wait_ge(s["e_d"], ge(blk) + 1)
                    act.activation(yb[b][:, 512:1024], (S0, S1)[b][:, 512:1024], ACT.Copy).then_inc(s["e_y_s"], 1)

                def e_block(blk, u, b, more, first):
                    ffn("e_", ge(blk), b, more)
                    if not first:
                        act.wait_ge(s[f"e_stored{b}"], 16 * (u + NBK[0] // 2 * l))
                    e_out(blk, b)

                for b in range(2):
                    e_block(b, 0, b, True, l == 0)
                with act.Fori(1, pairs_1) as i:
                    for b in range(2):
                        e_block(2 * i + b, i, b, True, False)
                for b in range(2):
                    e_block(2 * pairs_2 + 2 + b, pairs_2 + 1, b, b == 0, False)
                act.wait_ge(s["e_y_s"], 2 * pairs_1 + 2 + NBK[0] * l)
                spare_pairs(act, l, pairs, [("e_ex", 2), ("e_t_s", 2), ("e_y_s", 2)])
                if l == DEPTH - 1:
                    for t in range(TL):
                        act.wait_ge(c_sum, t + 1)
                        if t >= 2:
                            act.wait_ge(s["c_mean"], t - 1)
                        act.activation(c_junk[t % 2], x3b[t % 2], ACT.Square, scale=D ** -0.5, accum_out=h2s[:, t % 2:t % 2 + 1]).then_inc(s["c_sq"], 1)

        @block.tensor
        def _(pe):
            pe.wait_ge(consts_in, 16)
            pe.wait_ge(cs_ready, 3)
            for l in range(DEPTH):
                g = lambda t: t + T * l
                def mod_product(l, n, b, bank):
                    pe.wait_ge(s[f"mod_w_in{b}"], mod_in_count(l, n, b))
                    for k in range(KT):
                        q = k % 4
                        mm = pe.matmul(bank[32 * q:32 * q + 32, :], cs[:, k, :], mod_bufs[l][0][b][:, k, :], start=k < 4, stop=k >= 4)
                    mm.then_inc(s["mod_mm"], 1)

                def mod_pick(l, n, b, bank):
                    pe.wait_ge(s["mod_part"], n + 1 + NMCH * l)
                    pe.matmul(bank[0:2, :], C("pick"), mod_bufs[l][1][b], start=True, stop=True).then_inc(s["mod_sel"], 1)

                def mod_in_count(l, n, b):
                    return 8 * (n - b) + 16 + 8 * NMCH * l

                def mod_chunk(l, n, b, banks, rows, first):
                    if not first:
                        pe.wait_ge(s["mod_part"], n - 1 + NMCH * l)
                    mod_product(l, n, b, banks[b])
                    if not first:
                        pe.wait_ge(s["mod_row"], n - 1 + NMCH * l)
                    mod_pick(l, n, b, rows[b])

                def transpose_x(t, first):
                    pe.wait_ge(s["xn_done"], g(t) + 1)
                    if not first:
                        pe.wait_ge(s["hT_evac"], g(t))
                    xs = xt.rearrange("p (n k) -> p k n", k=KT)
                    for j in range(KT):
                        tr = pe.transpose(PT[:, j * P:(j + 1) * P], xs[:, j, :], ident)
                    tr.then_inc(s["hT_tr"], 1)

                if l == 0:
                    for n in range(4):
                        mod_chunk(0, n, n % 2, (B6, B7), (S0[:, 0:512], S0[:, 512:1024]), n < 2)
                    transpose_x(0, True)
                    for kind, n in FIRST_STEPS:
                        if kind == "mod":
                            bank, rows = mod_banks(n)
                            pe.wait_ge(s["mod_part"], n)
                            if n == 6:
                                pe.wait_ge(s["hT_evac"], 1)
                            mod_product(0, n, n % 2, bank)
                            pe.wait_ge(s["mod_row"], n)
                            mod_pick(0, n, n % 2, rows)
                        else:
                            if n == 0:
                                pe.wait_ge(s["hT_evac"], 1)
                                pe.wait_ge(s["mod_row"], 4)
                            if n == 4:
                                transpose_x(1, False)
                            pe.wait_ge(s["win_in"][n], 16 * win_parts(n))
                            for k in range(KT):
                                mm = pe.matmul(ubank[n][:, 0:UCH], hT[0][:, k, :], win[:, k, n * UCH:(n + 1) * UCH], start=k == 0, stop=k == KT - 1)
                            mm.then_inc(s["u_mm"], 1)
                            if n == 3:
                                pe.wait_ge(s["mod_row"], NMCH)

                def prep_round(t, r):
                    def copies(srcs, width):
                        for n, a in enumerate(srcs):
                            tr = pe.transpose(B7[0:width, n * P:(n + 1) * P], a, ident)
                        tr.then_inc(s["round_tr"], 1)
                    if r == 0:
                        pe.wait_ge(s["u_evac"], NCH * g(t) + NCH)
                    if not (l == 0 and r == 0 and isinstance(t, int) and t == 0):
                        pe.wait_ge(s["round_evac"], ROUNDS * g(t) + r)
                    if r == 0:
                        copies([U[:, a:a + P] for a in (NK_, NK_ + P, NQ, NQ + P)], P)
                    if r == 1:
                        pe.wait_ge(s["lor_ready"], g(t) + 1)
                        pe.transpose(B7[0:96, 0:P], lor[:, 0:96], ident)
                        pe.transpose(B7[0:96, P:2 * P], lor[:, 96:192], ident)
                        pe.transpose(B7[:, 2 * P:3 * P], lor[:, 192:320], ident).then_inc(s["round_tr"], 1)
                    if r == 2:
                        for k in range(2):
                            mm = pe.matmul(B7[:, 0:384], lorT[0:96, k, :], wqu[0:96, k, :], start=k == 0, stop=k == 1)
                        mm.then_inc(s["round_tr"], 1)
                    if r == 3:
                        pe.matmul(B7[:, :], lorT[:, 2, :], wkvu, start=True, stop=True).then_inc(s["round_tr"], 1)
                    if r == 4:
                        pe.wait_ge(s["st_ready"], g(t) + 1)
                        copies([st[:, P * n:P * n + P] for n in range(4)], P)
                    if r == 5:
                        copies([st[:, P * n:P * n + P] for n in range(4, 7)], P)
                    if r == 6:
                        pe.wait_ge(s["st_m_ready"], g(t) + 1)
                        copies([st[:, ST_MK + 96 * n:ST_MK + 96 * n + 96] for n in range(4)], 96)
                    if r == 7:
                        copies([st[:, ST_MQ + 96 * n:ST_MQ + 96 * n + 96] for n in range(4)], 96)

                def tile(t, b, first, last, first_c=0):
                    pe.wait_ge(s["hT_evac"], g(t) + 1)
                    rounds = 0
                    for half in range(2 * first_c, 2 * NCH):
                        c, k0 = half // 2, (half % 2) * (KT // 2)
                        if k0 == 0:
                            pe.wait_ge(s["win_in"][c], 16 * win_parts(c) * (l + 1))
                            if not first:
                                pe.wait_ge(s["u_evac"], NCH * (g(t) - 1) + c + 1)
                        for k in range(k0, k0 + KT // 2):
                            mm = pe.matmul(ubank[c][:, 0:UCH], hT[b][:, k, :], win[:, k, c * UCH:(c + 1) * UCH],
                                           start=k == 0, stop=k == KT - 1)
                        if k0:
                            mm.then_inc(s["u_mm"], 1 + c if c == first_c else 1)
                        while not first and rounds < min(ROUNDS, (half - 2 * first_c + 1) * ROUNDS // (2 * NCH - 2 - 2 * first_c)):
                            prep_round(t - 1, rounds)
                            rounds += 1
                        if half == 8 and not last:
                            transpose_x(t + 1, False)

                if l:
                    transpose_x(0, True)
                pe.wait_ge(s["wsmall_in"], 16 * 10 * (l + 1))
                pe.wait_ge(s["mod_row"], NMCH * (l + 1))
                if l:
                    tile(0, 0, True, False)
                if l == 0:
                    with pe.Fori(0, (T - 2) // 2) as i:
                        tile(2 * i + 1, 1, False, False)
                        tile(2 * i + 2, 0, False, False)
                    tile(T - 1, 1, False, True)
                else:
                    for t in range(1, T):
                        tile(t, t % 2, False, t == T - 1, Q_CH if t >= TL else 0)
                for r in range(ROUNDS):
                    prep_round(T - 1, r)

                units = [(P, SL_DK + m // 4, V_D + 64 * (m // 2)) for m in range(8)]
                units += [(P, SL_AK, V_A + 64 * (h // 2)) for h in range(4)]
                units += [(96, SL_MK + h, V_M + 64 * h) for h in range(4)]
                units += [(P, SL_NK + h // 2, V_N + 64 * h) for h in range(4)]

                def att(t, nk, prev, last):
                    n0, p0 = HEADS * g(t), NP * g(t)
                    o8 = O.rearrange("p (n k) -> p k n", k=KT)
                    for k in range(HEADS):
                        if nk:
                            if k in (0, 8, 12, 16):
                                pe.wait_ge(s["qs_ready"], 4 * g(t) + (0, 8, 12, 16).index(k) + 1)
                            nr, ks, _ = units[k]
                            pe.wait_ge(s["exp_done"], n0 + k + 1)
                            for c0 in range(0, nk, 512):
                                c1 = min(c0 + 512, nk)
                                mm = pe.matmul((S0, S1)[k % 2][:, c0:c1], Qs[0:nr, k, :], qk[0:nr, ks, NTOK - nk + c0:NTOK - nk + c1],
                                               start=True, stop=True)
                            mm.then_inc(s["scored"], 1)
                        if k == HEADS - 1 and not prev:
                            pe.wait_ge(s["wout_in"], 16 * (l + 1))
                        if k == 5 and prev:
                            pe.wait_ge(s["o_all"], g(t))
                            pe.wait_ge(s["pt_v"], p0 + (3 if nk else 2))
                            pe.wait_ge(s["pt_s"], p0 + (3 if nk else 2))
                            for j in range(KT):
                                tr = pe.transpose(PT[:, j * P:(j + 1) * P], o8[:, j, :], ident)
                            tr.then_inc(s["ot_tr"], 1)
                        at_T = product_at(k, 2, nk, prev)
                        if at_T:
                            j, m, n = at_T
                            if 0 <= j < 4:
                                pe.wait_ge(s["comb_done"], 4 * g(t) + j + 1)
                            else:
                                pe.wait_ge(s["exp_done"], n0 + m + 3 - (HEADS if j < 0 else 0))
                            pe.wait_ge(s["pt_v"], p0 + j + 2)
                            pe.wait_ge(s["pt_s"], p0 + j + 2)
                            if k == 6 and prev:
                                pe.wait_ge(s["ot_v"], g(t))
                                pe.wait_ge(s["ot_s"], g(t))
                            for i in range(n // P):
                                c0 = i * P if n == NTOK else i * 512
                                tr = pe.transpose(PT[:, c0:c0 + P], Pb[m % 3][:, i * P:(i + 1) * P], ident)
                            tr.then_inc(s["p_tr"], 1)
                        at_V = product_at(k, 3, nk, prev)
                        if at_V:
                            j, m, n = at_V
                            pe.wait_ge(s["pt_v"], p0 + j + 3)
                            pe.wait_ge(s["pt_s"], p0 + j + 3)
                            pe.wait_ge(s["o_evac"], p0 + j + 2)
                            v0 = units[m][2]
                            for i in range(n // P):
                                mm = pe.matmul(B6[:, 0:64], PTs[j % 2][:, i, :], vals[:, (NTOK - n) // P + i, v0:v0 + 64],
                                               start=i == 0, stop=i == n // P - 1)
                            mm.then_inc(s["pv_done"], 1)
                        if prev and (6 <= k < 10 or 11 <= k < 15):
                            c, i = int(k > 10), (k - 6) % 5
                            if k == 6:
                                pe.wait_ge(s["ot_v"], g(t))
                                pe.wait_ge(s["ot_s"], g(t))
                            if i == 0:
                                pe.wait_ge(s["res_mul"], 2 * (g(t) - 1) + c)
                            for q in (2 * i, 2 * i + 1):
                                mm = pe.matmul(B7[:, :], OT[:, q, :], wout[:, q, c * 512:(c + 1) * 512], start=q == 0, stop=q == KT - 1)
                            if i == 3:
                                mm.then_inc(s["op_mm"], 1)

                pe.wait_ge(s["u_evac"], NCH * T * (l + 1))
                pe.wait_ge(s["round_evac"], ROUNDS * T * (l + 1))
                over_tiles(pe, l, att)
                nt = T if l == 0 else TL
                gend = T * l + nt

                def transposes(m, b, half):
                    x8 = (hs, xg)[m == "e_"][b].rearrange("p (n k) -> p k n", k=KT)
                    for j in range(half * KT // 2, (half + 1) * KT // 2):
                        tr = pe.transpose(PT[:, j * P:(j + 1) * P], x8[:, j, :], ident)
                    if half:
                        tr.then_inc(s[m + "tr"], 1)

                def ffn(m, gi, b, nxt, product=None, pick=None):
                    e = m == "e_"
                    X = (hT2, XT)[e][b]
                    G = (S0, S1)[b]
                    pe.wait_ge(s[m + "t_v"], gi + 1)
                    pe.wait_ge(s[m + "t_s"], gi + 1)
                    if not e:
                        pe.wait_ge(s["s_lg"], gi)
                        if l == 0 and gi:
                            pe.wait_ge(s["mod_row"], NMCH + gi)
                        for k in range(KT):
                            mm = pe.matmul(B6[:, 0:NE], X[:, k, :], rw[:, k, :], start=k == 0, stop=k == KT - 1)
                        mm.then_inc(s["s_rt"], 1)
                    for w, name in enumerate(("g", "u")):
                        for k in range(KT):
                            wk = wgu[b][:, w, k * DE:(k + 1) * DE] if e else swgu[:, k, w * DE:(w + 1) * DE]
                            mm = pe.matmul(G[:, 512 * w:512 * w + DE], X[:, k, :], wk, start=k == 0, stop=k == KT - 1)
                        mm.then_inc(s[m + name], 1)
                    nxt(0)
                    if product:
                        product()
                    pe.wait_ge(s[m + "hid"], gi + 1)
                    hd = hid[b].rearrange("p (n k) -> p k n", k=2)
                    for j in range(2):
                        tr = pe.transpose(B7[:, j * P:(j + 1) * P], hd[:, j, :], ident)
                    tr.then_inc(s[m + "ht"], 1)
                    nxt(1)
                    pe.wait_ge(s[m + "htv"], gi + 1)
                    for c in range(2):
                        if c and pick:
                            pick()
                        for k in range(2):
                            wk = wdn[b][:, k, c * 512:(c + 1) * 512] if e else swd[:, k, c * 512:(c + 1) * 512]
                            mm = pe.matmul(G[:, c * 512:(c + 1) * 512], hidT[b][:, k, :], wk, start=k == 0, stop=k == 1)
                    mm.then_inc(s[m + "d"], 1)

                pe.wait_ge(s["res_mul"], 2 * gend)
                pe.wait_ge(s["s_w_in"], 16 * 7 * (l + 1))
                def s_next(t, b, first, half):
                    if half == 0:
                        pe.wait_ge(s[f"hs_in{b}"], hs_count(t, b))
                        if not first:
                            pe.wait_ge(s["s_t_v"], g(t))
                            pe.wait_ge(s["s_t_s"], g(t))
                    transposes("s_", b, half)

                def hs_count(t, b):
                    return 8 * (t - b) + 16 + 8 * T * l

                for half in range(2):
                    s_next(0, 0, l == 0, half)
                def s_block(t, b, more, first):
                    if not first:
                        pe.wait_ge(s["s_ob"], g(t) - 1)
                    nxt = (lambda half: s_next(t + 1, 1 - b, False, half)) if more else (lambda half: None)
                    if l == 0:
                        def product():
                            pe.wait_ge(s["s_lg"], g(t) + 1)
                            mod_product(1, t, b, B6)
                        ffn("s_", g(t), b, nxt, product, lambda: mod_pick(1, t, b, B6))
                    else:
                        ffn("s_", g(t), b, nxt)
                for b in range(2):
                    s_block(b, b, True, l == 0)
                for i in range(1, nt // 2 - 1):
                    for b in range(2):
                        s_block(2 * i + b, b, True, False)
                for b in range(2):
                    s_block(nt - 2 + b, b, b == 0, False)
                pe.wait_ge(s["r_mat"], l + 1)
                if l == 0:
                    pe.wait_ge(s["mod_row"], NMCH + nt)
                pe.matmul(B6[:, 0:nt * NE], C("before"), both[:, 0:nt, :].rearrange("p a b -> p (a b)"), start=True, stop=True)
                pe.matmul(B7[:, 0:nt * NE], ones, both[:, 0:nt, :].rearrange("p a b -> p (a b)"), start=True, stop=True).then_inc(s["r_cum"], 1)
                pe.wait_ge(s["r_hot"], l + 1)
                for n in range(TOPK * nt):
                    mm = pe.matmul(B6[:, 0:NBK[l]], in_place[:, n, :], in_block[:, n, 0:NBK[l]], start=n == 0, stop=n == TOPK * nt - 1)
                mm.then_inc(s["r_tab"], 1)
                pe.wait_ge(s["s_ob"], gend)
                if l == 0:
                    for n in range(nt, NMCH):
                        mod_chunk(1, n, n % 2, (S1[:, 0:512], S1[:, 512:1024]), (S0[:, 0:512], S0[:, 512:1024]), n < nt + 2)
                    pe.wait_ge(s["mod_row"], 2 * NMCH)
                pairs, pairs_1, pairs_2 = pair_counts(pe, l)
                ge = lambda b: b + NBK[0] * l

                def e_next(blk, u, b, first, half):
                    if half == 0:
                        pe.wait_ge(e_x_in[l][b], 16 * (u + 1))
                        if not first:
                            pe.wait_ge(s["e_t_v"], ge(blk))
                            pe.wait_ge(s["e_t_s"], ge(blk))
                    transposes("e_", b, half)

                def e_block(blk, u, b, more, first):
                    pe.wait_ge(s[f"e_w_in{b}"], 48 * (u + 1 + NBK[0] // 2 * l))
                    if not first:
                        pe.wait_ge(s["e_y_v"], ge(blk) - 1)
                        pe.wait_ge(s["e_y_s"], ge(blk) - 1)
                    ffn("e_", ge(blk), b, (lambda half: e_next(blk + 1, u + b, 1 - b, False, half)) if more else (lambda half: None))

                for half in range(2):
                    e_next(0, 0, 0, l == 0, half)
                for b in range(2):
                    e_block(b, 0, b, True, l == 0)
                with pe.Fori(1, pairs_1) as i:
                    for b in range(2):
                        e_block(2 * i + b, i, b, True, False)
                for b in range(2):
                    e_block(2 * pairs_2 + 2 + b, pairs_2 + 1, b, b == 0, False)
                pe.wait_ge(s["e_d"], 2 * pairs_1 + 2 + NBK[0] * l)
                spare_pairs(pe, l, pairs, [("e_tr", 2), ("e_g", 2), ("e_u", 2), ("e_ht", 2), ("e_d", 2)])

        @block.gpsimd
        def _(pool):
            pool.memset(halfs[:, 0:8], -0.5).then_inc(halfs_set, 1)
            pool.memset(halfs[:, 8:14], 1.0 / 64).then_inc(halfs_set, 1)
            pool.memset(halfs[:, 14:16], 1.0).then_inc(halfs_set, 1)
            pool.memset(halfs[:, 16:24], EPS).then_inc(halfs_set, 1)
            pool.wait_ge(halfs_set, 4)
            for l in range(DEPTH):
                g = lambda t: t + T * l

                def rstd_of(l, t):
                    g = lambda t: t + T * l
                    pool.wait_ge(s["ssq"], g(t) + 1)
                    pool.tensor_tensor(meansq[:, 0:1], sumsq[:, 0:1], eps8[:, 0:1], ALU.add).then_inc(s["mean_x"], 1)
                    pool.wait_ge(s["mean_x"], g(t) + 1)
                    pool.tensor_tensor(rstd[:, 0:1], meansq[:, 0:1], halfs[:, 0:1], ALU.pow).then_inc(s["rstd_ready"], 1)

                def prep(t):
                    pool.wait_ge(s["u_evac"], NCH * g(t) + NCH)
                    vt = vals[:, span(t, 1), :]
                    pool.tensor_copy(vt[:, :, V_A:V_A + 128], U[:, AV:AV + 128].unsqueeze(1))
                    pool.tensor_copy(vt[:, :, V_N:V_N + 256], U[:, NV:NV + 256].unsqueeze(1))
                    pool.tensor_copy(vt[:, :, V_D:V_D + 256], U[:, DV:DV + 256].unsqueeze(1)).then_inc(s["v_copied"], 1)
                    pool.wait_ge(s["stats"], g(t) + 1)
                    ch = Count(pool, s["g_prep"], 2 * g(t))
                    ch.done(pool.tensor_tensor(m8[:, :], s8[:, :], inv8, ALU.mult)).sync()
                    ch.done(pool.tensor_tensor(m8[:, :], m8[:, :], eps8, ALU.add)).sync()
                    assert ch.n == 2
                    pool.tensor_tensor(r8[:, :], m8[:, :], halfs[:, 0:8], ALU.pow).then_inc(s["r8_ready"], 1)

                if l == 0:
                    rstd_of(0, 0)
                rstd_of(l, 1)
                if l == 0:
                    pool.wait_ge(s["mod_stored"], 32)
                else:
                    for b in range(2):
                        pool.wait_ge(s[f"c_stored{b}"], 16 * (T // 2))
                with pool.Fori(0, T - 2) as t:
                    prep(t)
                    rstd_of(l, t + 2)
                prep(T - 2)
                prep(T - 1)

                pool.wait_ge(s["bias_in"], 16 * 8 * (l + 1))
                bt = bias_t.rearrange("p h (j c) -> p (h j) c", c=GRID_W)
                pool.wait_ge(s["r8_ready"], T * (l + 1))
                pool.tensor_tensor(bt, bt, C("window").unsqueeze(1).to_broadcast([P, 64, GRID_W]), ALU.add).then_inc(s["bias_ready"], 1)

                def att(t, nk, prev, last):
                    if nk:
                        pool.wait_ge(s["d_stat"], g(t) + 1)
                        pool.tensor_tensor(dstat[:, 4:8], dstat[:, 0:4], eps8[:, 0:4], ALU.add).then_inc(s["g_att"], 1)
                        pool.wait_ge(s["g_att"], g(t) + 1)
                        pool.tensor_tensor(dstat[:, 4:8], dstat[:, 4:8], halfs[:, 0:4], ALU.pow).then_inc(s["d_rs"], 1)
                    if prev:
                        gp = g(t) - 1
                        w = 0 if prev == NTOK else 3
                        ch = Count(pool, s["g_x"], 4 * gp)
                        pool.wait_ge(s["xa_in"], 16 * gp + 16)
                        pool.wait_ge(s["res_mul"], 2 * gp + 2)
                        pool.tensor_tensor(xb, xb, xa, ALU.add).then_inc(s["x1_ready"], 1)
                        pool.wait_ge(s["x1_sq"], gp + 1)
                        ch.done(pool.tensor_tensor(h2s[:, 1:2], h2s[:, 0:1], eps8[:, 0:1], ALU.add)).sync()
                        ch.done(pool.tensor_tensor(h2s[:, 1:2], h2s[:, 1:2], halfs[:, 0:1], ALU.pow)).sync()
                        ch.done(pool.tensor_tensor(h2b, xb, h2s[:, 1:2].to_broadcast([P, D]), ALU.mult)).sync()
                        ch.done(pool.tensor_tensor(h2b, h2b, vec[:, w + 1, :], ALU.mult)).sync()
                        pool.tensor_tensor(h2b, h2b, vec[:, w + 2, :], ALU.add).then_inc(s["h2_ready"], 1)
                        assert ch.n == 4

                pool.wait_ge(s["vec_in"], 16 * 6 * (l + 1))
                over_tiles(pool, l, att)
                nt = T if l == 0 else TL
                gend = T * l + nt

                def s_sum(t, u, b):
                    pool.wait_ge(s["s_ob"], g(t) + 1)
                    pool.wait_ge(s[f"x1_in{b}"], 16 * (u + 1 + T // 2 * l))
                    pool.tensor_tensor(ob[b], ob[b], x1b[b], ALU.add).then_inc(s["s_x2"], 1)
                with pool.Fori(0, nt // 2) as i:
                    for b in range(2):
                        s_sum(2 * i + b, i, b)
                pool.wait_ge(s["r_slots"], l + 1)
                pairs, pairs_1, _ = pair_counts(pool, l)
                ge = lambda b: b + NBK[0] * l

                def e_gather(blk, b, first):
                    if not first:
                        pool.wait_ge(s["e_tr"], ge(blk) - 1)
                    pool.tensor_copy(idx1[b], table_u[:, span(blk, 1)]).then_inc(s["e_idx"], 1)
                    pool.wait_ge(s["e_idx"], ge(blk) + 1)
                    pool.sem_inc(s["idx_seen"], 1)
                    pool.indirect_dma_start(out=xg[b], out_offset=None, in_=h2_d[l],
                                            in_offset=bass.IndirectOffsetOnAxis(ap=idx1[b], axis=0)).then_inc(e_x_in[l][b], 16)
                for b in range(2):
                    e_gather(b, b, l == 0)
                with pool.Fori(1, pairs) as i:
                    for b in range(2):
                        e_gather(2 * i + b, b, False)
                spare_pairs(pool, l, pairs, [("e_idx", 2)])
                for b in range(2):
                    pool.wait_ge(s[f"e_stored{b}"], 16 * (pairs_1 + 1 + NBK[0] // 2 * l))
                    pool.sem_inc(s["idx_seen"], 1)

                def c_gather(t, b, first):
                    if not first:
                        if l < DEPTH - 1:
                            pool.wait_ge(s["c_x3"], g(t) - 1)
                        elif t >= 2:
                            pool.wait_ge(c_sum, t - 1)
                    pool.tensor_copy(idx2[b].unsqueeze(1), slots[:, span(t, 1), :]).then_inc(s["c_idx"], 1)
                    pool.wait_ge(s["c_idx"], g(t) + 1)
                    pool.sem_inc(s["idx_seen"], 1)
                    for j in range(TOPK):
                        pool.indirect_dma_start(out=y12[b][:, j, :], out_offset=None, in_=y_d[l],
                                                in_offset=bass.IndirectOffsetOnAxis(ap=idx2[b][:, j:j + 1], axis=0)).then_inc(s[f"c_y_in{b}"], 16)
                for b in range(2):
                    c_gather(b, b, l == 0)
                if l < DEPTH - 1:
                    c_gather(2, 0, False)
                    rstd_of(1, 0)
                    c_gather(3, 1, False)
                    c_gather(4, 0, False)
                    c_gather(5, 1, False)
                else:
                    for t in range(TL):
                        if t + 2 < TL:
                            c_gather(t + 2, t % 2, False)
                        pool.wait_ge(s["c_sq"], t + 1)
                        if t >= 2:
                            pool.wait_ge(s["c_x3"], T + t - 1)
                        sq, rs = h2s[:, t % 2:t % 2 + 1], h2s[:, 2 + t % 2:3 + t % 2]
                        pool.tensor_tensor(rs, sq, eps8[:, 0:1], ALU.add).then_inc(s["c_mean"], 1)
                        pool.wait_ge(s["c_mean"], t + 1)
                        pool.tensor_tensor(rs, rs, halfs[:, 0:1], ALU.pow).then_inc(s["c_rs"], 1)

        @block.vector
        def _(dve):
            dve.memset(cs[:, :, :], 0.0).then_inc(cs_ready, 1)
            dve.memset(relpad, 0.0).then_inc(relpad_set, 1)
            R_START = [0]
            dve.wait_ge(exp_c, 1)
            ch = Count(dve, v_init, 0)
            ch.done(dve.tensor_scalar(ctmp[:, :, :], ctmp[:, :, :], 1.0, None, ALU.add)).sync()
            ch.done(dve.reciprocal(ctmp[:, :, :], ctmp[:, :, :])).sync()
            dve.wait_ge(cs_ready, 1)
            for r in range(2):
                dve.tensor_tensor(cs[:, :, r], csrc[:, r, :], ctmp[:, r, :], ALU.mult).then_inc(cs_ready, 1)
            dve.wait_ge(consts_in, 16)
            for l in range(DEPTH):
                g = lambda t: t + T * l
                def normalise(l, t):
                    dve.wait_ge(s["rstd_ready"], t + T * l + 1)
                    dve.tensor_scalar(xt, xt, rstd[:, 0:1], None, ALU.mult).then_inc(s["xn_done"], 1)

                def mod_part(l, n, b, bank):
                    dve.wait_ge(s["mod_mm"], n + 1 + NMCH * l)
                    dve.tensor_copy(mod_bufs[l][1][b], bank).then_inc(s["mod_part"], 1)

                def mod_row(l, n, bank):
                    dve.wait_ge(s["mod_sel"], n + 1 + NMCH * l)
                    row = mod_bufs[l][2][:, span(n * MCH, MCH)]
                    dve.tensor_tensor(row, bank[0:2, :], row, ALU.add).then_inc(s["mod_row"], 1)

                def mod_gain(l, half):
                    w, chunks = ((1, 4), (4, NMCH))[half]
                    dve.wait_ge(s["mod_row"], chunks + NMCH * l)
                    a = mod_bufs[l][2][:, w * D:(w + 1) * D]
                    dve.scalar_tensor_tensor(a, a, 1.0, mod_bufs[l][3][:, half, :], ALU.add, ALU.mult).then_inc(s["mod_gain"], 1)

                if l == 0:
                    def mod_chunk(n, b):
                        mod_part(0, n, b, (B6, B7)[b][:, :])
                        mod_row(0, n, S0[:, b * 512:(b + 1) * 512])
                    dve.wait_ge(s["mod_rows_in"], 16 * 6)
                    with dve.Fori(0, 2) as i:
                        for b in range(2):
                            mod_chunk(2 * i + b, b)
                    mod_gain(0, 0)
                    normalise(0, 0)
                    for n in range(4, NMCH):
                        bank, rows = mod_banks(n)
                        mod_part(0, n, n % 2, bank)
                        mod_row(0, n, rows)
                        if n == 9:
                            normalise(0, 1)
                    mod_gain(0, 1)

                def rope(ch, x, t, rot, heads, outs):
                    q = rot // 4
                    ctab = cos[rot][:, span(t, 1), :]
                    stab = sin[rot][:, span(t, 1), :].rearrange("p o (a h c) -> p (o a) h c", a=2, h=2)
                    a3 = tmpA[:, 0:heads * rot].rearrange("p (h c) -> p h c", h=heads)
                    ch.done(dve.tensor_tensor(a3, x, ctab.to_broadcast([P, heads, rot]), ALU.mult))
                    x5 = x.rearrange("p h (a b c) -> p h a b c", a=2, b=2)
                    b5 = tmpB[:, 0:heads * rot].rearrange("p (h a b c) -> p h a b c", h=heads, a=2, b=2)
                    for half in range(2):
                        tab = stab[:, :, half, :].unsqueeze(1).to_broadcast([P, heads, 2, q])
                        ch.done(dve.tensor_tensor(b5[:, :, :, half, :], x5[:, :, :, 1 - half, :], tab, ALU.mult))
                    ch.sync()
                    b3 = tmpB[:, 0:heads * rot].rearrange("p (h c) -> p h c", h=heads)
                    for h0, h1, o in outs:
                        ai, bi = a3[:, h0:h1, :], b3[:, h0:h1, :]
                        if o.ndim == 4:
                            ai = ai.rearrange("p (a b) c -> p a b c", b=o.shape[2])
                            bi = bi.rearrange("p (a b) c -> p a b c", b=o.shape[2])
                        ch.done(dve.tensor_tensor(o, ai, bi, ALU.add))

                heads_of = lambda a, n: a.rearrange("p (h c) -> p h c", h=n)

                def evac_round(t, r, src, dst):
                    dve.wait_ge(s["round_tr"], ROUNDS * g(t) + r + 1)
                    dve.tensor_copy(dst, src).then_inc(s["round_evac"], 1)

                def to_qk(t, r, slot, n, rows=P):
                    evac_round(t, r, B7[0:rows, 0:n * P].rearrange("p (n c) -> p n c", n=n),
                               qk[0:rows, slot:slot + n, span(t * P, P)])

                N_PREP = 33

                def prep(t):
                    ch = Count(dve, s["v_prep"], N_PREP * g(t))
                    dve.wait_ge(s["u_evac"], NCH * g(t) + NCH)
                    ch.done(dve.tensor_tensor(tmpA[:, 0:384], U[:, AQ:AQ + 384], U[:, AQ:AQ + 384], ALU.mult))
                    ch.done(dve.tensor_tensor_reduce(tmpB[:, 0:192], U[:, CQ:CQ + 192], U[:, CQ:CQ + 192], 1.0 / 192, 0.0,
                                                     ALU.mult, ALU.add, s8[:, 6:7]))
                    ch.done(dve.tensor_tensor_reduce(tmpB[:, 192:320], U[:, CKV:CKV + 128], U[:, CKV:CKV + 128], 1.0 / 128, 0.0,
                                                     ALU.mult, ALU.add, s8[:, 7:8]))
                    ch.sync()
                    dve.tensor_reduce(s8[:, 0:6], heads_of(tmpA[:, 0:384], 6), AX.X, ALU.add).then_inc(s["stats"], 1)
                    dve.wait_ge(s["stats"], g(t) + 1)
                    for src, dst in ((DQ, ST_DQ), (DK, ST_DK)):
                        rope(ch, heads_of(U[:, src:src + 256], 8), t, 32, 8, [(0, 8, heads_of(st[:, dst:dst + 256], 8))])
                        ch.sync()
                    to_qk(t, 0, SL_NK, 4)
                    dve.wait_ge(s["r8_ready"], g(t) + 1)
                    ch.done(dve.scalar_tensor_tensor(lor[:, 0:192], U[:, CQ:CQ + 192], r8[:, 6:7], lgain[:, 0:192], ALU.mult, ALU.mult))
                    ch.done(dve.scalar_tensor_tensor(lor[:, 192:320], U[:, CKV:CKV + 128], r8[:, 7:8], lgain[:, 192:320], ALU.mult, ALU.mult))
                    ch.sync()
                    dve.sem_inc(s["lor_ready"], 1)
                    rope(ch, heads_of(U[:, KPE:KPE + 32], 1), t, 32, 1, [(0, 1, heads_of(kper, 1))])
                    ch.sync()
                    dve.wait_ge(s["round_tr"], ROUNDS * g(t) + 2)
                    ch.done(dve.tensor_copy(lorT[0:96, 0:2, :], B7[0:96, 0:256].rearrange("p (n c) -> p n c", n=2)))
                    ch.sync()
                    dve.tensor_copy(lorT[:, 2, :], B7[:, 256:384]).then_inc(s["round_evac"], 1)
                    a3 = heads_of(tmpA[:, 0:384], 6)
                    g3 = heads_of(st[:, ST_MK:ST_MK + 384], 6)
                    ch.done(dve.tensor_tensor(a3, heads_of(U[:, AQ:AQ + 384], 6), r8[:, 0:6].unsqueeze(2).to_broadcast([P, 6, 64]), ALU.mult))
                    ch.sync()
                    ch.done(dve.tensor_tensor(g3, a3, gains[:, :, :], ALU.mult))
                    ch.sync()
                    dve.sem_inc(s["u_used"], 1)
                    rope(ch, g3, t, 64, 6,
                         [(0, 4, st[:, ST_AQ:ST_AQ + 256].rearrange("p (b a c) -> p a b c", b=2, a=2)),
                          (4, 6, heads_of(st[:, ST_AK:ST_AK + 128], 2))])
                    ch.sync()
                    dve.sem_inc(s["st_ready"], 1)
                    dve.wait_ge(s["round_tr"], ROUNDS * g(t) + 3)
                    q3, k3 = heads_of(B7[:, 0:384], 4), heads_of(B7[:, 0:512], 4)
                    mq, mk = heads_of(st[:, ST_MQ:ST_MQ + 384], 4), heads_of(st[:, ST_MK:ST_MK + 384], 4)
                    ch.done(dve.tensor_copy(mq[:, :, 0:64], q3[:, :, 0:64]))
                    rope(ch, q3[:, :, 64:96], t, 32, 4, [(0, 4, mq[:, :, 64:96])])
                    ch.sync()
                    dve.sem_inc(s["round_evac"], 1)
                    dve.wait_ge(s["round_tr"], ROUNDS * g(t) + 4)
                    ch.done(dve.tensor_copy(mk[:, :, 0:64], k3[:, :, 0:64]))
                    ch.done(dve.tensor_copy(mk[:, :, 64:96], kper.unsqueeze(1).to_broadcast([P, 4, 32])))
                    ch.done(dve.tensor_copy(vals[:, span(t, 1), V_M:V_M + 256].rearrange("p o (h c) -> p (o h) c", h=4), k3[:, :, 64:128]))
                    ch.sync()
                    dve.sem_inc(s["round_evac"], 1)
                    dve.sem_inc(s["st_m_ready"], 1)
                    to_qk(t, 4, SL_AK, 4)
                    to_qk(t, 5, SL_AQ + 1, 3)
                    to_qk(t, 6, SL_MK, 4, 96)
                    to_qk(t, 7, SL_MQ, 4, 96)
                    assert ch.n == N_PREP, ch.n

                if l:
                    normalise(l, 1)
                if l == 0:
                    dve.wait_ge(s["mod_stored"], 32)
                else:
                    for b in range(2):
                        dve.wait_ge(s[f"c_stored{b}"], 16 * (T // 2))
                with dve.Fori(0, T - 2) as t:
                    prep(t)
                    normalise(l, t + 2)
                prep(T - 2)
                prep(T - 1)

                nt = T if l == 0 else TL
                gend = T * l + nt
                lam_init = 0.8 - 0.6 * math.exp(-0.3 * l)
                dve.wait_ge(s["lam_in"], 16 * 5 * (l + 1))
                ch = Count(dve, s["v_lam"], 7 * l)
                ch.done(dve.tensor_tensor_reduce(lamb[:, 0, :], lamb[:, 0, :], lamb[:, 1, :], 1.0, 0.0, ALU.mult, ALU.add, nlam[:, 2:3]))
                ch.done(dve.tensor_tensor_reduce(lamb[:, 2, :], lamb[:, 2, :], lamb[:, 3, :], 1.0, 0.0, ALU.mult, ALU.add, nlam[:, 3:4]))
                ch.done(dve.tensor_scalar(subg[:, :], subg[:, :], 1.0 - lam_init, None, ALU.mult))
                ch.sync()
                dve.sem_inc(s["lam_sum"], 1)
                dve.wait_ge(s["lam_exp"], l + 1)
                ch.done(dve.tensor_tensor(nlam[:, 2:3], nlam[:, 1:2], nlam[:, 0:1], ALU.subtract)).sync()
                ch.done(dve.tensor_scalar(nlam[:, 2:3], nlam[:, 2:3], -lam_init, None, ALU.add)).sync()
                N_O = 48

                def queries(kind, t):
                    cols = span(t * P, P)
                    ins = []
                    if kind == "diff":
                        for m in range(4):
                            r = slice(32 * m, 32 * m + 32)
                            dst = Qs[r, 0:8, :].rearrange("p (a m) c -> p a m c", a=2)[:, :, m, :]
                            ins.append(dve.tensor_scalar(dst, qk[r, SL_DQ:SL_DQ + 2, cols], 32 ** -0.5, None, ALU.mult))
                    if kind == "gqa":
                        for m in range(2):
                            r = slice(64 * m, 64 * m + 64)
                            ins.append(dve.tensor_scalar(Qs[r, 8 + 2 * m:10 + 2 * m, :], qk[r, SL_AQ:SL_AQ + 2, cols], 64 ** -0.5, None, ALU.mult))
                    if kind == "mla":
                        ins.append(dve.tensor_scalar(Qs[0:96, 12:16, :], qk[0:96, SL_MQ:SL_MQ + 4, cols], 96 ** -0.5, None, ALU.mult))
                    if kind == "na":
                        for m in range(2):
                            r = slice(64 * m, 64 * m + 64)
                            dst = Qs[r, 16:20, :].rearrange("p (a m) c -> p a m c", a=2)[:, :, m, :]
                            ins.append(dve.tensor_scalar(dst, qk[r, SL_NQ:SL_NQ + 2, cols], 64 ** -0.5, None, ALU.mult))
                    ins[-1].then_inc(s["qs_ready"], 1)

                def att(t, nk, prev, last):
                    n0, p0 = HEADS * g(t), NP * g(t)
                    ch = Count(dve, s["v_o"], N_O * g(t)) if nk else Count(dve, s["v_lam"], 7 * l + 6)
                    for k in range(HEADS):
                        if nk:
                            Sk = (S0, S1)[k % 2]
                            dve.wait_ge(s["scored"], n0 + k + 1)
                            if nk == NTOK and k >= 16:
                                h = k - 16
                                if h == 0 and not prev:
                                    dve.wait_ge(s["bias_ready"], l + 1)
                                bt = bias_t[:, h:h + 1, span((7 - 2 * t) * GRID_W, SEQ)]
                                ch.done(dve.tensor_tensor(Sk[:, 0:SEQ].unsqueeze(1), Sk[:, 0:SEQ].unsqueeze(1), bt, ALU.add)).sync()
                            dve.tensor_reduce(nmax[:, k:k + 1], Sk[:, 0:nk], AX.X, ALU.max, negate=True).then_inc(s["neg_max"], 1)
                        if (nk and k) or (prev and k == 0):
                            m = (k - 1) % HEADS
                            dve.wait_ge(s["exp_done"], n0 + k + 2)
                            ch.done(dve.reciprocal(rinv[:, m:m + 1], rsum[:, m:m + 1])).sync()
                            if m < 8 and m % 2:
                                ra = ratio[:, m // 2:m // 2 + 1]
                                ch.done(dve.scalar_tensor_tensor(ra, rinv[:, m:m + 1], nlam[:, 2:3], rsum[:, m - 1:m], ALU.mult, ALU.mult)).sync()
                                dve.scalar_tensor_tensor(Pb[m % 3][:, 0:nk], Pb[m % 3][:, 0:nk], ra, Pb[(m - 1) % 3][:, 0:nk],
                                                         ALU.mult, ALU.add).then_inc(s["comb_done"], 1)
                        at_T = product_at(k, 2, nk, prev)
                        if at_T:
                            j, _, n = at_T
                            h = 4 if n == NTOK else 1
                            dve.wait_ge(s["p_tr"], p0 + j + 3)
                            dve.wait_ge(s["pv_done"], p0 + j + 1)
                            dve.tensor_copy(PTs[j % 2][:, 0:h, :].rearrange("p a b -> p (a b)"), PT[:, 0:h * P]).then_inc(s["pt_v"], 1)
                        if k == 5 and prev:
                            dve.wait_ge(s["ot_tr"], g(t))
                            dve.tensor_copy(OT[:, 0:4, :].rearrange("p a b -> p (a b)"), PT[:, 0:512]).then_inc(s["ot_v"], 1)
                        at_V = product_at(k, 3, nk, prev)
                        if at_V:
                            j, m, n = at_V
                            dve.wait_ge(s["pv_done"], p0 + j + 3)
                            if 0 <= j < 4:
                                o = O[:, 512 + 64 * j:576 + 64 * j]
                                dve.tensor_scalar(o, B6[:, 0:64], rinv[:, m - 1:m], None, ALU.mult).then_inc(s["o_evac"], 1)
                                dve.wait_ge(s["o_evac"], p0 + j + 3)
                                ins = dve.tensor_tensor_reduce(dtmp[:, 64:128], o, o, 1.0 / 64, 0.0, ALU.mult, ALU.add, dstat[:, j:j + 1])
                                if j == 3:
                                    ins.then_inc(s["d_stat"], 1)
                                else:
                                    ch.done(ins)
                            else:
                                base = {2: 0, 3: 768, 4: 256}[m // 4]
                                dve.tensor_scalar(O[:, base + 64 * (m % 4):base + 64 * (m % 4) + 64], B6[:, 0:64], rinv[:, m:m + 1], None,
                                                  ALU.mult).then_inc(s["o_evac"], 1)
                        if k == 2 and prev:
                            dve.wait_ge(s["o_evac"], p0 + 2)
                            dve.sem_inc(s["o_all"], 1)
                        if k in (10, 15) and prev:
                            gp, c = g(t) - 1, int(k == 15)
                            if c == 0:
                                dve.wait_ge(s["x1_stored"], 16 * gp)
                                dve.wait_ge(s["h2_ready"], gp)
                            dve.wait_ge(s["op_mm"], 2 * gp + c + 1)
                            dve.tensor_tensor(xb[:, c * 512:(c + 1) * 512], B7[:, :], vec[:, 0 if prev == NTOK else 3, c * 512:(c + 1) * 512],
                                              ALU.mult).then_inc(s["res_mul"], 1)
                        if k == 14 and nk:
                            dve.wait_ge(s["d_rs"], g(t) + 1)
                            o4 = O[:, 512:768].rearrange("p (h c) -> p h c", h=4)
                            ch.done(dve.tensor_tensor(o4, o4, dstat[:, 4:8].unsqueeze(2).to_broadcast([P, 4, 64]), ALU.mult)).sync()
                            ch.done(dve.tensor_tensor(o4, o4, subg[:, :].unsqueeze(1).to_broadcast([P, 4, 64]), ALU.mult))
                        if k == HEADS - 1 and not prev:
                            dve.wait_ge(s["vec_in"], 16 * 6 * (l + 1))
                        if k == 2 and nk:
                            queries("na", t)
                        if nk and not last and k in (9, 13, 17):
                            queries({9: "diff", 13: "gqa", 17: "mla"}[k], t + 1)
                    if nk:
                        ch.sync()
                        assert ch.n <= N_O, ch.n
                        if ch.n < N_O:
                            dve.sem_inc(s["v_o"], N_O - ch.n)
                    else:
                        assert ch.n == 1

                dve.wait_ge(s["round_evac"], ROUNDS * T * (l + 1))
                ch.done(dve.memset(Qs, 0.0)).sync()
                for kind in ("diff", "gqa", "mla"):
                    queries(kind, 0)
                over_tiles(dve, l, att)

                def x_half(m, b):
                    return (hT2, XT)[m == "e_"][b][:, 0:4, :].rearrange("p a b -> p (a b)")

                def first_T(m, gi, b):
                    dve.wait_ge(s[m + "tr"], gi + 1)
                    dve.tensor_copy(x_half(m, b), PT[:, 0:512]).then_inc(s[m + "t_v"], 1)

                def ffn(m, gi, b, more, part=None, row=None):
                    ch = Count(dve, s["v_" + m[0]], 3 * gi)
                    G = (S0, S1)[b]
                    dve.wait_ge(s[m + "ex"], gi + 1)
                    ch.done(dve.tensor_scalar(gex[b], gex[b], 1.0, None, ALU.add)).sync()
                    ch.done(dve.reciprocal(gex[b], gex[b])).sync()
                    ch.done(dve.tensor_tensor(gex[b], G[:, 0:DE], gex[b], ALU.mult)).sync()
                    dve.wait_ge(s[m + "u"], gi + 1)
                    dve.tensor_tensor(hid[b], G[:, 512:512 + DE], gex[b], ALU.mult).then_inc(s[m + "hid"], 1)
                    dve.wait_ge(s[m + "ht"], gi + 1)
                    dve.tensor_copy(hidT[b].rearrange("p a b -> p (a b)"), B7[:, 0:256]).then_inc(s[m + "htv"], 1)
                    if part:
                        part()
                    if more:
                        dve.wait_ge(s[m + "tr"], gi + 2)
                        dve.tensor_copy(x_half(m, 1 - b), PT[:, 0:512]).then_inc(s[m + "t_v"], 1)
                    if row:
                        row()
                    dve.wait_ge(s[m + "d"], gi + 1)

                def s_block(t, u, b, more, first, stream):
                    dve.wait_ge(s["s_rt"], g(t) + 1)
                    dve.tensor_copy(lg[:, span(t, 1), :], B6[:, 0:NE].unsqueeze(1)).then_inc(s["s_lg"], 1)
                    if l == 0:
                        ffn("s_", g(t), b, more, lambda: mod_part(1, t, b, B6[:, :]), lambda: mod_row(1, t, B6[:, :]))
                    else:
                        ffn("s_", g(t), b, more)
                    if not first:
                        dve.wait_ge(s[f"s_stored{b}"], 16 * (u + T // 2 * l))
                    dve.tensor_tensor(ob[b], (S0, S1)[b][:, :], g2[:, stream, :], ALU.mult).then_inc(s["s_ob"], 1)

                first_T("s_", g(0), 0)
                if l == 0:
                    dve.wait_ge(s["mod_rows_in"], 16 * 12)
                for b in range(2):
                    s_block(b, 0, b, True, l == 0, 0)
                if l == 0:
                    for b in range(2):
                        s_block(2 + b, 1, b, True, False, 0)
                    for b in range(2):
                        s_block(4 + b, 2, b, b == 0, False, 1)
                else:
                    for b in range(2):
                        s_block(2 + b, 1, b, b == 0, False, 0)

                ch = Count(dve, s["v_r"], R_START[0])
                row = lambda a: a.rearrange("p a b -> p (a b)")
                sc_, sel_ = score[:, 0:nt, :], selb[:, 0:nt, :]
                step = lambda ins: ch.done(ins).sync()
                dve.wait_ge(s["r_exp"], l + 1)
                step(dve.tensor_scalar(sc_, sc_, 1.0, None, ALU.add))
                step(dve.reciprocal(sc_, sc_))
                step(dve.tensor_tensor(sel_, sc_, rb.unsqueeze(1).to_broadcast([P, nt, NE]), ALU.add))
                q = row(sel_).rearrange("p (a b) -> p a b", b=4)
                ng = nt * NG
                pr = lambda n: pair[:, n, 0:ng]
                ch.done(dve.tensor_tensor(pr(0), q[:, :, 0], q[:, :, 1], ALU.max))
                ch.done(dve.tensor_tensor(pr(1), q[:, :, 2], q[:, :, 3], ALU.max))
                ch.done(dve.tensor_tensor(pr(2), q[:, :, 0], q[:, :, 1], ALU.min))
                ch.done(dve.tensor_tensor(pr(3), q[:, :, 2], q[:, :, 3], ALU.min)).sync()
                step(dve.tensor_tensor(pr(3), pr(2), pr(3), ALU.max))
                step(dve.tensor_tensor(pr(4), pr(0), pr(1), ALU.min))
                step(dve.tensor_tensor(pr(3), pr(3), pr(4), ALU.max))
                step(dve.tensor_tensor(pr(0), pr(0), pr(1), ALU.max))
                ch.done(dve.memset(gs8[:, 0:nt, 4:8], -BIG))
                step(dve.tensor_tensor(gs8[:, 0:nt, 0:4], pr(0).rearrange("p (a b) -> p a b", b=4), pr(3).rearrange("p (a b) -> p a b", b=4), ALU.add))

                def best(src):
                    for t in range(nt):
                        ch.done(dve.max(mx8[:, t, :], src[:, t, :]))
                    ch.sync()
                    for t in range(nt):
                        ch.done(dve.max_index(ix8[:, t, :], mx8[:, t, :], src[:, t, :]))
                    ch.sync()
                best(gs8)
                step(dve.tensor_copy(gidx[:, 0:nt].unsqueeze(2), ix8[:, 0:nt, 0:1]))
                grp = C("group_of").unsqueeze(1).to_broadcast([P, nt, NE])
                step(dve.tensor_tensor(tmp16[:, 0:nt, :], grp, gidx[:, 0:nt].unsqueeze(2).to_broadcast([P, nt, NE]), ALU.is_equal))
                step(dve.tensor_scalar(tmp16[:, 0:nt, :], tmp16[:, 0:nt, :], 1.0, BIG, ALU.subtract, ALU.mult))
                step(dve.tensor_tensor(sel_, sel_, tmp16[:, 0:nt, :], ALU.add))
                best(selb)
                step(dve.tensor_copy(eidx[:, 0:nt, :], ix8[:, 0:nt, 0:TOPK]))
                exi = C("expert").unsqueeze(1).to_broadcast([P, nt, NE])
                ohs = (oh0, oh1)
                for j in range(TOPK):
                    ch.done(dve.tensor_tensor(ohs[j][:, 0:nt, :], exi, eidx[:, 0:nt, j:j + 1].to_broadcast([P, nt, NE]), ALU.is_equal))
                ch.sync()
                dve.tensor_tensor(both[:, 0:nt, :], oh0[:, 0:nt, :], oh1[:, 0:nt, :], ALU.add).then_inc(s["r_mat"], 1)
                dve.wait_ge(s["r_cum"], l + 1)
                ch.done(dve.memset(offs[:, 0, :], 0.0))
                step(dve.tensor_copy(row(tots[:, 0:nt, :]), B7[:, 0:nt * NE]))
                for t in range(1, nt):
                    step(dve.tensor_tensor(offs[:, t, :], offs[:, t - 1, :], tots[:, t - 1, :], ALU.add))
                step(dve.tensor_tensor(count_e, offs[:, nt - 1, :], tots[:, nt - 1, :], ALU.add))
                step(dve.tensor_tensor(cmp6[:, :, 0:nt], count_e.unsqueeze(2).to_broadcast([P, NE, nt]),
                                       C("tile_start")[:, 0:nt].unsqueeze(1).to_broadcast([P, NE, nt]), ALU.is_gt))
                step(dve.tensor_reduce(nblk, cmp6[:, :, 0:nt], AX.X, ALU.add))
                step(dve.tensor_tensor_scan(bend, ones[:, 0:NE], nblk, 0.0, ALU.mult, ALU.add))
                nb = NBK[l]
                step(dve.tensor_tensor(cmpb[:, 0:nb, :], bend.unsqueeze(1).to_broadcast([P, nb, NE]),
                                       C("block")[:, 0:nb].unsqueeze(2).to_broadcast([P, nb, NE]), ALU.is_le))
                step(dve.tensor_reduce(bexp[:, 0:nb], cmpb[:, 0:nb, :], AX.X, ALU.add))
                step(dve.tensor_scalar(bexp[:, 0:nb], bexp[:, 0:nb], float(NE - 1), None, ALU.min))
                step(dve.tensor_copy(bexp_i[:, 0:nb], bexp[:, 0:nb]))
                even = cmpb[:, 0:nb // 2, 0]
                step(dve.tensor_tensor(even, C("block")[:, 0:nb:2], bend[:, NE - 1:NE].to_broadcast([P, nb // 2]), ALU.is_lt))
                step(dve.tensor_reduce(npair_f[:, 0:1], even, AX.X, ALU.add))
                for n in (1, 2):
                    ch.done(dve.tensor_scalar(npair_f[:, n:n + 1], npair_f[:, 0:1], float(n), None, ALU.subtract))
                ch.sync()
                step(dve.tensor_copy(npair_i, npair_f))
                dve.sem_inc(s["r_ready"], 1)
                step(dve.tensor_tensor(bbase, bend, nblk, ALU.subtract))
                step(dve.tensor_scalar(bbase, bbase, float(P), None, ALU.mult))
                step(dve.tensor_tensor(row(posn[:, 0:nt, :]), B6[:, 0:nt * NE], row(offs[:, 0:nt, :]), ALU.add))
                step(dve.tensor_tensor(posn[:, 0:nt, :], posn[:, 0:nt, :], bbase.unsqueeze(1).to_broadcast([P, nt, NE]), ALU.add))
                for j in range(TOPK):
                    step(dve.tensor_tensor(tmp16[:, 0:nt, :], posn[:, 0:nt, :], ohs[j][:, 0:nt, :], ALU.mult))
                    step(dve.tensor_reduce(slotf[:, 0:nt, j], tmp16[:, 0:nt, :], AX.X, ALU.add))
                nb, ns = NBK[l], TOPK * nt
                sf, bo = row(slotf[:, 0:nt, :]), row(block_of[:, 0:nt, :])
                ge_b, hot_b, hot_p = from_block[:, 0:ns, 0:nb + 1], in_block[:, 0:ns, 0:nb], in_place[:, 0:ns, :]
                step(dve.tensor_scalar(bo, sf, 1.0 / P, None, ALU.mult))
                step(dve.tensor_tensor(ge_b, bo.unsqueeze(2).to_broadcast([P, ns, nb + 1]),
                                       C("block")[:, 0:nb + 1].unsqueeze(1).to_broadcast([P, ns, nb + 1]), ALU.is_ge))
                ch.done(dve.tensor_reduce(bo, ge_b[:, :, 1:nb + 1], AX.X, ALU.add))
                step(dve.tensor_tensor(hot_b, ge_b[:, :, 0:nb], ge_b[:, :, 1:nb + 1], ALU.subtract))
                step(dve.tensor_scalar(bo, bo, float(P), None, ALU.mult))
                step(dve.tensor_tensor(bo, sf, bo, ALU.subtract))
                ch.done(dve.tensor_tensor(hot_p, bo.unsqueeze(2).to_broadcast([P, ns, P]),
                                          C("place").unsqueeze(1).to_broadcast([P, ns, P]), ALU.is_equal))
                for j in range(TOPK):
                    hj = hot_b.rearrange("p (t j) b -> p t j b", j=TOPK)[:, :, j, :]
                    ch.done(dve.tensor_tensor(hj, hj, C("token")[:, 0:nt].unsqueeze(2).to_broadcast([P, nt, nb]), ALU.mult))
                ch.sync()
                dve.sem_inc(s["r_hot"], 1)
                ch.done(dve.tensor_copy(slots[:, 0:nt, :], slotf[:, 0:nt, :]))
                dve.wait_ge(s["r_tab"], l + 1)
                step(dve.tensor_copy(table_u[:, 0:nb], B6[:, 0:nb]))
                dve.sem_inc(s["r_slots"], 1)
                for j in range(TOPK):
                    step(dve.tensor_tensor(tmp16[:, 0:nt, :], sc_, ohs[j][:, 0:nt, :], ALU.mult))
                    step(dve.tensor_reduce(wts[:, 0:nt, j], tmp16[:, 0:nt, :], AX.X, ALU.add))
                step(dve.tensor_reduce(wsum[:, 0:nt], wts[:, 0:nt, :], AX.X, ALU.add))
                step(dve.reciprocal(wsum[:, 0:nt], wsum[:, 0:nt]))
                step(dve.tensor_tensor(wts[:, 0:nt, :], wts[:, 0:nt, :], wsum[:, 0:nt].unsqueeze(2).to_broadcast([P, nt, TOPK]), ALU.mult))
                R_START[0] += ch.n
                if l == 0:
                    for n in range(nt, NMCH):
                        c0 = 512 * (n % 2)
                        mod_part(1, n, n % 2, S1[:, c0:c0 + 512])
                        mod_row(1, n, S0[:, c0:c0 + 512])
                    mod_gain(1, 0)
                    mod_gain(1, 1)
                dve.wait_ge(s["s_x2"], gend)
                pairs, pairs_1, pairs_2 = pair_counts(dve, l)
                ge = lambda b: b + NBK[0] * l
                first_T("e_", ge(0), 0)

                def e_block(blk, u, b, more, first):
                    ffn("e_", ge(blk), b, more)
                    if not first:
                        dve.wait_ge(s[f"e_stored{b}"], 16 * (u + NBK[0] // 2 * l))
                    dve.tensor_copy(yb[b][:, 0:512], (S0, S1)[b][:, 0:512]).then_inc(s["e_y_v"], 1)

                for b in range(2):
                    e_block(b, 0, b, True, l == 0)
                with dve.Fori(1, pairs_1) as i:
                    for b in range(2):
                        e_block(2 * i + b, i, b, True, False)
                for b in range(2):
                    e_block(2 * pairs_2 + 2 + b, pairs_2 + 1, b, b == 0, False)
                dve.wait_ge(s["e_y_v"], 2 * pairs_1 + 2 + NBK[0] * l)
                spare_pairs(dve, l, pairs, [("e_t_v", 2), ("v_e", 6), ("e_hid", 2), ("e_htv", 2), ("e_y_v", 2)])
                def c_tile(t, u, b, stream, first):
                    ch = Count(dve, s["v_c"], 3 * g(t))
                    dve.wait_ge(s[f"c_y_in{b}"], 16 * TOPK * (u + 1 + T // 2 * l))
                    w = lambda j: wts[:, span(t, 1), j]
                    y1, y2 = y12[b][:, 0, :], y12[b][:, 1, :]
                    ch.done(dve.tensor_scalar(y1, y1, w(0), None, ALU.mult)).sync()
                    ch.done(dve.scalar_tensor_tensor(y1, y2, w(1), y1, ALU.mult, ALU.add)).sync()
                    ch.done(dve.tensor_tensor(y1, y1, g2[:, stream, :], ALU.mult)).sync()
                    assert ch.n == 3
                    dve.wait_ge(s[f"c_x_in{b}"], 16 * (u + 1 + T // 2 * l))
                    if not first:
                        dve.wait_ge(s[f"c_stored{b}"], 16 * (u + T // 2 * l))
                    if l < DEPTH - 1:
                        dve.tensor_tensor(xt if t == 0 else x3b[b], y1, x2b[b], ALU.add).then_inc(s["c_x3"], 1)
                    else:
                        dve.tensor_tensor(x3b[b], y1, x2b[b], ALU.add).then_inc(c_sum, 1)

                def c_final(t, b):
                    dve.wait_ge(s["c_rs"], t + 1)
                    dve.scalar_tensor_tensor(x3b[b], x3b[b], h2s[:, 2 + b:3 + b], fgain, ALU.mult, ALU.mult).then_inc(s["c_x3"], 1)
                if l < DEPTH - 1:
                    for b in range(2):
                        c_tile(b, 0, b, 0, True)
                    dve.wait_ge(s["c_stored0"], 16)
                    normalise(1, 0)
                    for t in range(2, nt):
                        c_tile(t, t // 2, t % 2, int(t >= TL), False)
                else:
                    dve.wait_ge(fgain_in, 16)
                    for t in range(nt):
                        c_tile(t, t // 2, t % 2, 0, False)
                        if t:
                            c_final(t - 1, (t - 1) % 2)
                    c_final(nt - 1, (nt - 1) % 2)


_INS = ["tokens", "c", "c_ctx", "w_mod", "b_mod", "norm_mix", "norm_ffn", "w_in", "w_out",
        "gqa_q_norm", "gqa_k_norm", "na_rel_bias", "diff_lq1", "diff_lk1", "diff_lq2", "diff_lk2", "diff_subln",
        "mla_q_norm", "mla_w_q_up", "mla_kv_norm", "mla_w_kv_up", "router_w", "router_b",
        "moe_w_gate", "moe_w_up", "moe_w_down", "shared_w_gate", "shared_w_up", "shared_w_down", "final_norm"]


def kernel(**inputs):
    import concourse.bacc as bacc
    from concourse.bass_utils import run_bass_kernel_spmd

    nc = bacc.Bacc("TRN2", target_bir_lowering=False, num_devices=1)
    arrays, A = {}, {}
    inputs["tokens"] = np.concatenate([inputs["x"][0], inputs["ctx"][0]])
    for name in _INS:
        a = np.ascontiguousarray(inputs[name])
        arrays[f"in_{name}"] = a
        A[name] = nc.dram_tensor(f"in_{name}", a.shape, mybir.dt.from_np(a.dtype), kind="ExternalInput").ap()
    out = nc.dram_tensor("out", (1, SEQ, D), F32, kind="ExternalOutput").ap()
    program(nc, A, out)
    return run_bass_kernel_spmd(nc, [arrays], core_ids=[0]).results[0]["out"]
```
